# Optimizing a Trainium2 kernel written in Bass

```python
import math
import jax
import jax.numpy as jnp
from jax import lax
import numpy as np
import jax, jax.numpy as jnp

D_MODEL = 1024
BATCH = 1
SEQ = 256
DEPTH = 2

GRID_W = 64
CTX_LEN = 256
N_MIXERS = 3
N_MOD = 9
NORM_EPS = 1e-6
D_FF = 2816
FFT_GROUPS = 8
FFT_GROUP_W = D_MODEL // FFT_GROUPS
RET_HEADS = D_MODEL // 256
RET_DK = D_MODEL // RET_HEADS
RET_DV = 2 * RET_DK
RET_HK = RET_HEADS * RET_DK
RET_HV = RET_HEADS * RET_DV
RET_CHUNK = 128
ROPE_BASE = 10000.0
ROPE_FREQS = RET_DK // 4
S5_GROUP = 16
S5_GROUPS = D_MODEL // S5_GROUP
S5_STATE = 64
S5_DT_MIN = 0.001
S5_DT_MAX = 0.1
S5_C_STD = 0.5
N_FNET = (DEPTH + 2) // N_MIXERS
N_RET = (DEPTH + 1) // N_MIXERS
N_S5 = DEPTH // N_MIXERS


def _rmsnorm(h, g):
    h32 = h.astype(jnp.float32)
    y = h32 * lax.rsqrt(jnp.mean(h32 * h32, axis=-1, keepdims=True) + NORM_EPS)
    return (y * g.astype(jnp.float32)).astype(h.dtype)

def _modnorm(h, g, shift, scale):
    return _rmsnorm(h, g) * (1.0 + scale) + shift

def _ffn_half(h, g, shift, scale, gate, w_in, w_out):
    a, b = jnp.split(_modnorm(h, g, shift, scale) @ w_in, 2, axis=-1)
    return h + 0.5 * gate * ((jax.nn.silu(a) * b) @ w_out)

def _fourier_mixer(u, w_out):
    b, n, d = u.shape
    ug = u.astype(jnp.float32).reshape(b, n, FFT_GROUPS, FFT_GROUP_W)
    f = jnp.real(jnp.fft.fft2(ug, axes=(1, 3), norm='ortho'))
    return f.reshape(b, n, d).astype(u.dtype) @ w_out

def _heads(t, dh):
    b, n, _ = t.shape
    return jnp.swapaxes(t.reshape(b, n, -1, dh).astype(jnp.float32), 1, 2)

def _rotate(t, cos, sin):
    t1, t2 = jnp.split(t, 2, axis=-1)
    return jnp.concatenate([t1 * cos - t2 * sin, t2 * cos + t1 * sin], axis=-1)

def _rope_2d(t, rope):
    cos_r, sin_r, cos_c, sin_c = rope
    t_row, t_col = jnp.split(t, 2, axis=-1)
    return jnp.concatenate([_rotate(t_row, cos_r, sin_r), _rotate(t_col, cos_c, sin_c)], axis=-1)

def _ret_project(u, w_in, rope):
    q, k, v, g = jnp.split(u @ w_in, [RET_HK, 2 * RET_HK, 2 * RET_HK + RET_HV], axis=-1)
    q, k = _heads(q, RET_DK), _heads(k, RET_DK)
    if rope is not None:
        q, k = _rope_2d(q, rope), _rope_2d(k, rope)
    return q, k * RET_DK ** -0.5, _heads(v, RET_DV), g

def _ret_project_kv(u, w_in):
    k, v = jnp.split(u @ w_in[:, RET_HK:2 * RET_HK + RET_HV], [RET_HK], axis=-1)
    return _heads(k, RET_DK) * RET_DK ** -0.5, _heads(v, RET_DV)

def _ret_scan(q, k, v, log_gamma, s0, strict, reverse):
    if reverse:
        q, k, v = jnp.flip(q, 2), jnp.flip(k, 2), jnp.flip(v, 2)
    b, h, n, _ = q.shape
    dv = v.shape[-1]
    nc = n // RET_CHUNK

    def chunks(t):
        return jnp.moveaxis(t.reshape(b, h, nc, RET_CHUNK, t.shape[-1]), 2, 0)

    idx = jnp.arange(RET_CHUNK, dtype=jnp.float32)
    diff = idx[:, None] - idx[None, :]
    keep = diff > 0 if strict else diff >= 0
    intra = jnp.where(keep, jnp.exp(jnp.maximum(diff, 0.0)[None] * log_gamma[:, None, None]), 0.0)
    q_dec = jnp.exp((idx + 1.0)[None, :] * log_gamma[:, None])[None, :, :, None]
    k_dec = jnp.exp((RET_CHUNK - 1.0 - idx)[None, :] * log_gamma[:, None])[None, :, :, None]
    c_dec = jnp.exp(RET_CHUNK * log_gamma)[None, :, None, None]

    def step(s, qkv):
        qc, kc, vc = qkv
        scores = jnp.einsum('bhld,bhmd->bhlm', qc, kc) * intra
        o = jnp.einsum('bhlm,bhme->bhle', scores, vc) + jnp.einsum('bhld,bhde->bhle', qc * q_dec, s)
        s = c_dec * s + jnp.einsum('bhld,bhle->bhde', kc * k_dec, vc)
        return s, o

    s_fin, o = lax.scan(step, s0, (chunks(q), chunks(k), chunks(v)))
    o = jnp.moveaxis(o, 0, 2).reshape(b, h, n, dv)
    if reverse:
        o = jnp.flip(o, 2)
    return o, s_fin

def _ret_final_state(k, v, log_gamma, reverse):
    n = k.shape[2]
    pos = jnp.arange(n, dtype=jnp.float32)
    expo = pos if reverse else (n - 1.0) - pos
    w = jnp.exp(expo[None, :] * log_gamma[:, None])
    return jnp.einsum('bhnd,bhne,hn->bhde', k, v, w)

def _ret_out(o, g, w_out):
    mu = jnp.mean(o, axis=-1, keepdims=True)
    var = jnp.mean(jnp.square(o - mu), axis=-1, keepdims=True)
    o = (o - mu) * lax.rsqrt(var + NORM_EPS)
    b, h, n, dv = o.shape
    o = jnp.swapaxes(o, 1, 2).reshape(b, n, h * dv).astype(g.dtype)
    return (jax.nn.silu(g) * o) @ w_out

def _retention_mixer(u, uc, w_in, w_out, decay_logit, rope, need_ctx_out):
    log_gamma = jax.nn.log_sigmoid(decay_logit.astype(jnp.float32))
    q, k, v, g = _ret_project(u, w_in, rope)
    yc = None
    if need_ctx_out:
        qc, kc, vc, gc = _ret_project(uc, w_in, None)
        zero = jnp.zeros(kc.shape[:2] + (RET_DK, RET_DV), jnp.float32)
        oc_f, s_f = _ret_scan(qc, kc, vc, log_gamma[0], zero, False, False)
        oc_b, s_b = _ret_scan(qc, kc, vc, log_gamma[1], zero, True, True)
        yc = _ret_out(oc_f + oc_b, gc, w_out)
    else:
        kc, vc = _ret_project_kv(uc, w_in)
        s_f = _ret_final_state(kc, vc, log_gamma[0], False)
        s_b = _ret_final_state(kc, vc, log_gamma[1], True)
    o_f, _ = _ret_scan(q, k, v, log_gamma[0], s_f, False, False)
    o_b, _ = _ret_scan(q, k, v, log_gamma[1], s_b, True, True)
    return _ret_out(o_f + o_b, g, w_out), yc

def _lin_combine(left, right):
    a_l, b_l = left
    a_r, b_r = right
    return a_r * a_l, a_r * b_l + b_r

def _s5_discretise(lam_re, lam_im, log_dt, b_re, b_im):
    lam = lax.complex(lam_re.astype(jnp.float32), lam_im.astype(jnp.float32))
    dt = jnp.exp(log_dt.astype(jnp.float32))[:, None]
    a_bar = jnp.exp(lam * dt)
    b_bar = ((a_bar - 1.0) / lam)[..., None] * lax.complex(b_re.astype(jnp.float32),
                                                          b_im.astype(jnp.float32))
    return a_bar, b_bar

def _s5_drive(u, b_bar):
    b, n, _ = u.shape
    ug = u.astype(jnp.float32).reshape(b, n, S5_GROUPS, S5_GROUP)
    return lax.complex(jnp.einsum('bngc,gpc->nbgp', ug, jnp.real(b_bar)),
                       jnp.einsum('bngc,gpc->nbgp', ug, jnp.imag(b_bar)))

def _s5_scan(a_bar, bu, reverse):
    a = jnp.broadcast_to(a_bar, (bu.shape[0], 1) + a_bar.shape)
    _, h = lax.associative_scan(_lin_combine, (a, bu), reverse=reverse, axis=0)
    return h

def _s5_read(h, c_re, c_im):
    n, b = h.shape[:2]
    y = (jnp.einsum('gcp,nbgp->bngc', c_re, jnp.real(h))
         - jnp.einsum('gcp,nbgp->bngc', c_im, jnp.imag(h)))
    return y.reshape(b, n, D_MODEL)

def _s5_glu(y, w_glu, dtype):
    a, b = jnp.split(jax.nn.gelu(y).astype(dtype) @ w_glu, 2, axis=-1)
    return a * jax.nn.sigmoid(b)

def _s5_mixer(u, uc, lam_re, lam_im, log_dt, b_re, b_im, c_re, c_im, d_skip, w_glu, need_ctx_out):
    d32 = d_skip.astype(jnp.float32)
    y = u.astype(jnp.float32) * d32
    yc = uc.astype(jnp.float32) * d32 if need_ctx_out else None
    for dirn in range(2):
        reverse = dirn == 1
        a_bar, b_bar = _s5_discretise(lam_re[dirn], lam_im[dirn], log_dt[dirn], b_re[dirn], b_im[dirn])
        hc = _s5_scan(a_bar, _s5_drive(uc, b_bar), reverse)
        s_init = hc[0] if reverse else hc[-1]
        bu = _s5_drive(u, b_bar)
        bu = bu.at[-1 if reverse else 0].add(a_bar * s_init)
        hl = _s5_scan(a_bar, bu, reverse)
        cr, ci = c_re[dirn].astype(jnp.float32), c_im[dirn].astype(jnp.float32)
        y = y + _s5_read(hl, cr, ci)
        if need_ctx_out:
            yc = yc + _s5_read(hc, cr, ci)
    out = _s5_glu(y, w_glu, u.dtype)
    out_c = _s5_glu(yc, w_glu, uc.dtype) if need_ctx_out else None
    return out, out_c

def first_inputs(seed: int = 0) -> dict:
    key = jax.random.key(seed)
    ks = jax.random.split(key, 23)
    f32 = jnp.float32
    d = D_MODEL

    def nrm(k, shape, scale):
        return scale * jax.random.normal(k, shape, f32)

    g, p, cg = S5_GROUPS, S5_STATE, S5_GROUP
    base_logit = jnp.log(2.0 ** (5.0 + jnp.arange(RET_HEADS, dtype=f32)) - 1.0)
    return {
        'x': nrm(ks[0], (BATCH, SEQ, d), 1.0),
        'c': nrm(ks[1], (BATCH, d), 1.0),
        'ctx': nrm(ks[2], (BATCH, CTX_LEN, d), 1.0),
        'c_ctx': nrm(ks[3], (d,), 1.0),
        'w_mod': nrm(ks[4], (DEPTH, d, N_MOD * d), 0.5 * d ** -0.5),
        'b_mod': nrm(ks[5], (DEPTH, N_MOD * d), 0.02),
        'norm_g': 1.0 + nrm(ks[6], (DEPTH, 3, d), 0.02),
        'ffn_w_in': nrm(ks[7], (DEPTH, 2, d, 2 * D_FF), d ** -0.5),
        'ffn_w_out': nrm(ks[8], (DEPTH, 2, D_FF, d), D_FF ** -0.5),
        'fnet_w_out': nrm(ks[9], (N_FNET, d, d), d ** -0.5),
        'ret_w_in': nrm(ks[10], (N_RET, d, 2 * RET_HK + 2 * RET_HV), d ** -0.5),
        'ret_w_out': nrm(ks[11], (N_RET, RET_HV, d), RET_HV ** -0.5),
        'ret_decay_logit': base_logit + nrm(ks[12], (N_RET, 2, RET_HEADS), 0.1),
        's5_lam_re': -0.5 + nrm(ks[13], (N_S5, 2, g, p), 0.01),
        's5_lam_im': jnp.pi * jnp.arange(p, dtype=f32) + nrm(ks[14], (N_S5, 2, g, p), 0.01),
        's5_log_dt': jax.random.uniform(ks[15], (N_S5, 2, g), f32,
                                        math.log(S5_DT_MIN), math.log(S5_DT_MAX)),
        's5_b_re': nrm(ks[16], (N_S5, 2, g, p, cg), (2 * cg) ** -0.5),
        's5_b_im': nrm(ks[17], (N_S5, 2, g, p, cg), (2 * cg) ** -0.5),
        's5_c_re': nrm(ks[18], (N_S5, 2, g, cg, p), S5_C_STD),
        's5_c_im': nrm(ks[19], (N_S5, 2, g, cg, p), S5_C_STD),
        's5_d': nrm(ks[20], (N_S5, d), 1.0),
        's5_w_glu': nrm(ks[21], (N_S5, d, 2 * d), d ** -0.5),
        'final_norm_g': 1.0 + nrm(ks[22], (d,), 0.02),
    }

def first_block(x, c, ctx, c_ctx, w_mod, b_mod, norm_g, ffn_w_in, ffn_w_out, fnet_w_out,
              ret_w_in, ret_w_out, ret_decay_logit, s5_lam_re, s5_lam_im, s5_log_dt,
              s5_b_re, s5_b_im, s5_c_re, s5_c_im, s5_d, s5_w_glu, final_norm_g):
    bsz, n_lat, _ = x.shape
    rows = n_lat // GRID_W
    r_idx, c_idx = jnp.meshgrid(jnp.arange(rows, dtype=jnp.float32),
                                jnp.arange(GRID_W, dtype=jnp.float32), indexing='ij')
    inv_freq = jnp.exp(-math.log(ROPE_BASE) * jnp.arange(ROPE_FREQS, dtype=jnp.float32) / ROPE_FREQS)
    ang_r = r_idx.reshape(-1)[:, None] * inv_freq
    ang_c = c_idx.reshape(-1)[:, None] * inv_freq
    rope = (jnp.cos(ang_r), jnp.sin(ang_r), jnp.cos(ang_c), jnp.sin(ang_c))

    silu_c = jax.nn.silu(c)
    silu_cc = jax.nn.silu(c_ctx)
    h, hc = x, ctx
    for i in range(DEPTH):
        kind = i % N_MIXERS
        j = i // N_MIXERS
        last = i == DEPTH - 1
        ctx_used = (not last) or kind != 0
        m = (silu_c @ w_mod[i] + b_mod[i]).reshape(bsz, N_MOD, 1, D_MODEL)
        mc = (silu_cc @ w_mod[i] + b_mod[i]).reshape(N_MOD, D_MODEL)

        h = _ffn_half(h, norm_g[i, 0], m[:, 0], m[:, 1], m[:, 2], ffn_w_in[i, 0], ffn_w_out[i, 0])
        u = _modnorm(h, norm_g[i, 1], m[:, 3], m[:, 4])
        if ctx_used:
            hc = _ffn_half(hc, norm_g[i, 0], mc[0], mc[1], mc[2], ffn_w_in[i, 0], ffn_w_out[i, 0])
            uc = _modnorm(hc, norm_g[i, 1], mc[3], mc[4])

        if kind == 0:
            y = _fourier_mixer(u, fnet_w_out[j])
            yc = _fourier_mixer(uc, fnet_w_out[j]) if not last else None
        elif kind == 1:
            y, yc = _retention_mixer(u, uc, ret_w_in[j], ret_w_out[j], ret_decay_logit[j], rope, not last)
        else:
            y, yc = _s5_mixer(u, uc, s5_lam_re[j], s5_lam_im[j], s5_log_dt[j], s5_b_re[j], s5_b_im[j],
                              s5_c_re[j], s5_c_im[j], s5_d[j], s5_w_glu[j], not last)

        h = h + m[:, 5] * y
        h = _ffn_half(h, norm_g[i, 2], m[:, 6], m[:, 7], m[:, 8], ffn_w_in[i, 1], ffn_w_out[i, 1])
        if not last:
            hc = hc + mc[5] * yc
            hc = _ffn_half(hc, norm_g[i, 2], mc[6], mc[7], mc[8], ffn_w_in[i, 1], ffn_w_out[i, 1])
    return _rmsnorm(h, final_norm_g)


D_MIX = D_MODEL
SSD_INNER = D_MIX // 2
SSD_HEAD_DIM = 64
SSD_HEADS = SSD_INNER // SSD_HEAD_DIM
SSD_GROUPS = 2
SSD_STATE = 128
SSD_CONV = 4
SSD_CHUNK = 128
SSD_XBC = SSD_INNER + 2 * SSD_GROUPS * SSD_STATE
POOL_WIDTH = D_MIX // 4
POOL_GROUPS = 4
POOL_GROUP_DIM = POOL_WIDTH // POOL_GROUPS
ATTN_WIDTH = D_MIX - SSD_INNER - POOL_WIDTH
ATTN_HEAD_DIM = 64
ATTN_HEADS = ATTN_WIDTH // ATTN_HEAD_DIM
ROPE_DIM = ATTN_HEAD_DIM // 4
ROPE_THETA = 500000.0
MOBA_BLOCK = 256
MOBA_TOPK = 3
MOBA_QCHUNK = 64
RMS_EPS = 1e-6

OFF_Z = 0
OFF_XBC = OFF_Z + SSD_INNER
OFF_DT = OFF_XBC + SSD_XBC
OFF_POOL = OFF_DT + SSD_HEADS
OFF_Q = OFF_POOL + POOL_WIDTH
OFF_K = OFF_Q + ATTN_WIDTH
OFF_V = OFF_K + ATTN_WIDTH
IN_COLS = OFF_V + ATTN_WIDTH


def _rmsnorm_2(x, g):
    x32 = x.astype(jnp.float32)
    y = x32 * lax.rsqrt(jnp.mean(x32 * x32, axis=-1, keepdims=True) + RMS_EPS)
    return y.astype(x.dtype) * g

def _swiglu(h, wg, wu, wd):
    return (jax.nn.silu(h @ wg) * (h @ wu)) @ wd

def _partial_rope(t, pos):
    half = ROPE_DIM // 2
    inv_freq = ROPE_THETA ** (-jnp.arange(0, ROPE_DIM, 2, dtype=jnp.float32) / ROPE_DIM)
    ang = pos[:, None] * inv_freq[None, :]
    cos = jnp.cos(ang)[None, :, None, :]
    sin = jnp.sin(ang)[None, :, None, :]
    t32 = t[..., :ROPE_DIM].astype(jnp.float32)
    x1, x2 = t32[..., :half], t32[..., half:]
    rot = jnp.concatenate([x1 * cos - x2 * sin, x2 * cos + x1 * sin], axis=-1).astype(t.dtype)
    return jnp.concatenate([rot, t[..., ROPE_DIM:]], axis=-1)

def _ssd_chunked(xdt, dA, Bm, Cm):
    b, S, H, P = xdt.shape
    G = SSD_GROUPS
    HG = H // G
    N = Bm.shape[-1]
    L = SSD_CHUNK
    nc = S // L
    x = xdt.reshape(b, nc, L, G, HG, P)
    a = dA.reshape(b, nc, L, G, HG).transpose(0, 3, 4, 1, 2)
    Bc = Bm.reshape(b, nc, L, G, N)
    Cc = Cm.reshape(b, nc, L, G, N)
    a_cs = jnp.cumsum(a, axis=-1)
    causal = jnp.tril(jnp.ones((L, L), dtype=bool))
    seg = jnp.exp(jnp.where(causal, a_cs[..., :, None] - a_cs[..., None, :], -jnp.inf))
    cb = jnp.einsum('bclgn,bcsgn->bgcls', Cc, Bc)
    y_diag = jnp.einsum('bgcls,bghcls,bcsghp->bclghp', cb, seg, x)
    decay_in = jnp.exp(a_cs[..., -1:] - a_cs)
    states = jnp.einsum('bclgn,bghcl,bclghp->bcghpn', Bc, decay_in, x)
    chunk_decay = jnp.exp(a_cs[..., -1])

    def step(h, inp):
        st, dec = inp
        return h * dec[..., None, None] + st, h

    h0 = jnp.zeros(states.shape[:1] + states.shape[2:], states.dtype)
    _, prev = lax.scan(step, h0, (jnp.moveaxis(states, 1, 0), jnp.moveaxis(chunk_decay, -1, 0)))
    prev = jnp.moveaxis(prev, 0, 1)
    y_off = jnp.einsum('bclgn,bcghpn,bghcl->bclghp', Cc, prev, jnp.exp(a_cs))
    return (y_diag + y_off).reshape(b, S, H, P)

def _ssd_mixer(z, xbc, dt_raw, conv_w, conv_b, dt_bias, a_log, d_skip, norm_g):
    b, S, C = xbc.shape
    xbc = lax.conv_general_dilated(
        xbc, conv_w[:, None, :], window_strides=(1,), padding=[(SSD_CONV - 1, 0)],
        dimension_numbers=('NWC', 'WIO', 'NWC'), feature_group_count=C)
    xbc = jax.nn.silu(xbc + conv_b)
    gn = SSD_GROUPS * SSD_STATE
    xs = xbc[..., :SSD_INNER].reshape(b, S, SSD_HEADS, SSD_HEAD_DIM)
    Bm = xbc[..., SSD_INNER:SSD_INNER + gn].reshape(b, S, SSD_GROUPS, SSD_STATE)
    Cm = xbc[..., SSD_INNER + gn:].reshape(b, S, SSD_GROUPS, SSD_STATE)
    dt = jax.nn.softplus((dt_raw + dt_bias).astype(jnp.float32))
    A = -jnp.exp(a_log.astype(jnp.float32))
    y = _ssd_chunked(xs * dt[..., None], dt * A, Bm, Cm)
    y = y + d_skip[:, None] * xs
    y = y.reshape(b, S, SSD_INNER).astype(z.dtype)
    return _rmsnorm_2(y * jax.nn.silu(z), norm_g)

def _pool_mixer(u, pool_w, pool_scale):
    S = u.shape[1]
    c = jnp.cumsum(u.astype(jnp.float32), axis=1)
    t = jnp.arange(1, S + 1, dtype=jnp.float32)
    outs = []
    for g in range(POOL_GROUPS):
        w = 2 ** (g + 1)
        sl = slice(g * POOL_GROUP_DIM, (g + 1) * POOL_GROUP_DIM)
        cg = c[..., sl]
        shifted = jnp.pad(cg, ((0, 0), (w, 0), (0, 0)))[:, :S]
        mean = (cg - shifted) / jnp.minimum(t, float(w))[None, :, None]
        outs.append(jnp.einsum('bsc,cd->bsd', (mean - u[..., sl]).astype(u.dtype), pool_w[g]))
    return jnp.concatenate(outs, axis=-1) * pool_scale

def _moba_attention(q, k, v):
    b, S, H, Dh = q.shape
    q = q.transpose(0, 2, 1, 3)
    k = k.transpose(0, 2, 1, 3)
    v = v.transpose(0, 2, 1, 3)
    nb = -(-S // MOBA_BLOCK)
    sp = nb * MOBA_BLOCK
    topk = min(MOBA_TOPK, nb)
    pad = ((0, 0), (0, 0), (0, sp - S), (0, 0))
    k_pad = jnp.pad(k, pad)
    v_pad = jnp.pad(v, pad)
    kb = k_pad.reshape(b, H, nb, MOBA_BLOCK, Dh)
    vb = v_pad.reshape(b, H, nb, MOBA_BLOCK, Dh)
    k_mean = jnp.mean(kb.astype(jnp.float32), axis=3)
    gate = jnp.einsum('bhsd,bhnd->bhsn', q.astype(jnp.float32), k_mean)
    q_blk = jnp.arange(S) // MOBA_BLOCK
    past = jnp.arange(nb)[None, :] < q_blk[:, None]
    gate = jnp.where(past, gate, -jnp.inf)
    _, sel = lax.top_k(gate, topk)
    sel_valid = sel < q_blk[None, None, :, None]
    nq = S // MOBA_QCHUNK

    def chunks(t):
        return jnp.moveaxis(t.reshape((b, H, nq, MOBA_QCHUNK) + t.shape[3:]), 2, 0)

    bidx = jnp.arange(b)[:, None, None, None]
    hidx = jnp.arange(H)[None, :, None, None]
    scale = Dh ** -0.5

    def attend(args):
        qi, si, vi, ci = args
        start = ci * MOBA_QCHUNK
        q_pos = start + jnp.arange(MOBA_QCHUNK)
        kg = kb[bidx, hidx, si]
        vg = vb[bidx, hidx, si]
        s_sel = jnp.einsum('bhqd,bhqkjd->bhqkj', qi, kg).astype(jnp.float32) * scale
        s_sel = jnp.where(vi[..., None], s_sel, -jnp.inf).reshape(b, H, MOBA_QCHUNK, topk * MOBA_BLOCK)
        own = (start // MOBA_BLOCK) * MOBA_BLOCK
        ko = lax.dynamic_slice_in_dim(k_pad, own, MOBA_BLOCK, axis=2)
        vo = lax.dynamic_slice_in_dim(v_pad, own, MOBA_BLOCK, axis=2)
        s_own = jnp.einsum('bhqd,bhjd->bhqj', qi, ko).astype(jnp.float32) * scale
        k_pos = own + jnp.arange(MOBA_BLOCK)
        s_own = jnp.where(k_pos[None, :] <= q_pos[:, None], s_own, -jnp.inf)
        p = jax.nn.softmax(jnp.concatenate([s_sel, s_own], axis=-1), axis=-1).astype(v.dtype)
        p_sel = p[..., :topk * MOBA_BLOCK].reshape(b, H, MOBA_QCHUNK, topk, MOBA_BLOCK)
        return (jnp.einsum('bhqkj,bhqkjd->bhqd', p_sel, vg)
                + jnp.einsum('bhqj,bhjd->bhqd', p[..., topk * MOBA_BLOCK:], vo))

    out = lax.map(attend, (chunks(q), chunks(sel), chunks(sel_valid), jnp.arange(nq)))
    out = jnp.moveaxis(out, 0, 2).reshape(b, H, S, Dh)
    return out.transpose(0, 2, 1, 3).reshape(b, S, H * Dh)

def _hybrid_mixer(h, w_in, conv_w, conv_b, dt_bias, a_log, d_skip, ssd_norm, pool_w, pool_scale, w_out):
    b, S, _ = h.shape
    proj = h @ w_in
    z = proj[..., OFF_Z:OFF_XBC]
    xbc = proj[..., OFF_XBC:OFF_DT]
    dt_raw = proj[..., OFF_DT:OFF_POOL]
    u = proj[..., OFF_POOL:OFF_Q]
    pos = jnp.arange(S, dtype=jnp.float32)
    q = _partial_rope(proj[..., OFF_Q:OFF_K].reshape(b, S, ATTN_HEADS, ATTN_HEAD_DIM), pos)
    k = _partial_rope(proj[..., OFF_K:OFF_V].reshape(b, S, ATTN_HEADS, ATTN_HEAD_DIM), pos)
    v = proj[..., OFF_V:IN_COLS].reshape(b, S, ATTN_HEADS, ATTN_HEAD_DIM)
    y_ssd = _ssd_mixer(z, xbc, dt_raw, conv_w, conv_b, dt_bias, a_log, d_skip, ssd_norm)
    y_pool = _pool_mixer(u, pool_w, pool_scale).astype(h.dtype)
    y_attn = _moba_attention(q, k, v)
    return jnp.concatenate([y_ssd, y_pool, y_attn], axis=-1) @ w_out

def second_inputs(seed: int = 0) -> dict:
    key = jax.random.key(seed)
    ks = jax.random.split(key, 24)
    f32 = jnp.float32

    def nrm(k, shape, fan_in):
        return jax.random.normal(k, shape, f32) * fan_in ** -0.5

    def gain(k, shape):
        return 1.0 + 0.05 * jax.random.normal(k, shape, f32)

    u_dt = jax.random.uniform(ks[9], (DEPTH, SSD_HEADS), f32)
    dt0 = jnp.exp(u_dt * (math.log(0.1) - math.log(0.001)) + math.log(0.001))
    dt_bias = dt0 + jnp.log(-jnp.expm1(-dt0))
    a_log = jnp.log(jax.random.uniform(ks[10], (DEPTH, SSD_HEADS), f32, 1.0, 16.0))
    return {
        "x": jax.random.normal(ks[0], (BATCH, SEQ, D_MODEL), f32),
        "ff1_norm_pre": gain(ks[1], (DEPTH, D_MODEL)),
        "ff1_w_gate": nrm(ks[2], (DEPTH, D_MODEL, D_FF), D_MODEL),
        "ff1_w_up": nrm(ks[3], (DEPTH, D_MODEL, D_FF), D_MODEL),
        "ff1_w_down": nrm(ks[4], (DEPTH, D_FF, D_MODEL), D_FF),
        "ff1_norm_post": gain(ks[5], (DEPTH, D_MODEL)),
        "mix_norm_pre": gain(ks[6], (DEPTH, D_MODEL)),
        "w_in": nrm(ks[7], (DEPTH, D_MODEL, IN_COLS), D_MODEL),
        "conv_w": nrm(ks[8], (DEPTH, SSD_CONV, SSD_XBC), SSD_CONV),
        "conv_b": 0.01 * jax.random.normal(ks[11], (DEPTH, SSD_XBC), f32),
        "dt_bias": dt_bias,
        "a_log": a_log,
        "d_skip": gain(ks[12], (DEPTH, SSD_HEADS)),
        "ssd_norm": gain(ks[13], (DEPTH, SSD_INNER)),
        "pool_w": nrm(ks[14], (DEPTH, POOL_GROUPS, POOL_GROUP_DIM, POOL_GROUP_DIM), POOL_GROUP_DIM),
        "pool_scale": gain(ks[15], (DEPTH, POOL_WIDTH)),
        "w_out": nrm(ks[16], (DEPTH, D_MIX, D_MODEL), D_MIX),
        "mix_norm_post": gain(ks[17], (DEPTH, D_MODEL)),
        "ff2_norm_pre": gain(ks[18], (DEPTH, D_MODEL)),
        "ff2_w_gate": nrm(ks[19], (DEPTH, D_MODEL, D_FF), D_MODEL),
        "ff2_w_up": nrm(ks[20], (DEPTH, D_MODEL, D_FF), D_MODEL),
        "ff2_w_down": nrm(ks[21], (DEPTH, D_FF, D_MODEL), D_FF),
        "ff2_norm_post": gain(ks[22], (DEPTH, D_MODEL)),
    }

def second_block(x, ff1_norm_pre, ff1_w_gate, ff1_w_up, ff1_w_down, ff1_norm_post,
              mix_norm_pre, w_in, conv_w, conv_b, dt_bias, a_log, d_skip, ssd_norm,
              pool_w, pool_scale, w_out, mix_norm_post,
              ff2_norm_pre, ff2_w_gate, ff2_w_up, ff2_w_down, ff2_norm_post):
    h = x
    for l in range(DEPTH):
        f = _swiglu(_rmsnorm_2(h, ff1_norm_pre[l]), ff1_w_gate[l], ff1_w_up[l], ff1_w_down[l])
        h = h + 0.5 * _rmsnorm_2(f, ff1_norm_post[l])
        m = _hybrid_mixer(_rmsnorm_2(h, mix_norm_pre[l]), w_in[l], conv_w[l], conv_b[l], dt_bias[l],
                          a_log[l], d_skip[l], ssd_norm[l], pool_w[l], pool_scale[l], w_out[l])
        h = h + _rmsnorm_2(m, mix_norm_post[l])
        f = _swiglu(_rmsnorm_2(h, ff2_norm_pre[l]), ff2_w_gate[l], ff2_w_up[l], ff2_w_down[l])
        h = h + 0.5 * _rmsnorm_2(f, ff2_norm_post[l])
    return h


def setup_inputs(seed=0):
    out = dict(first_inputs(seed))
    for name, value in second_inputs(seed + 1).items():
        if name != "x":
            out[name + "_2"] = value
    return out


def reference(
    x, c, ctx, c_ctx, w_mod, b_mod, norm_g, ffn_w_in, ffn_w_out, fnet_w_out, ret_w_in,
    ret_w_out, ret_decay_logit, s5_lam_re, s5_lam_im, s5_log_dt, s5_b_re, s5_b_im, s5_c_re,
    s5_c_im, s5_d, s5_w_glu, final_norm_g, ff1_norm_pre_2, ff1_w_gate_2, ff1_w_up_2,
    ff1_w_down_2, ff1_norm_post_2, mix_norm_pre_2, w_in_2, conv_w_2, conv_b_2, dt_bias_2,
    a_log_2, d_skip_2, ssd_norm_2, pool_w_2, pool_scale_2, w_out_2, mix_norm_post_2,
    ff2_norm_pre_2, ff2_w_gate_2, ff2_w_up_2, ff2_w_down_2, ff2_norm_post_2,
):
    x = first_block(
        x, c, ctx, c_ctx, w_mod, b_mod, norm_g, ffn_w_in, ffn_w_out, fnet_w_out, ret_w_in,
        ret_w_out, ret_decay_logit, s5_lam_re, s5_lam_im, s5_log_dt, s5_b_re, s5_b_im, s5_c_re,
        s5_c_im, s5_d, s5_w_glu, final_norm_g,
    )
    return second_block(
        x, ff1_norm_pre_2, ff1_w_gate_2, ff1_w_up_2, ff1_w_down_2, ff1_norm_post_2,
        mix_norm_pre_2, w_in_2, conv_w_2, conv_b_2, dt_bias_2, a_log_2, d_skip_2, ssd_norm_2,
        pool_w_2, pool_scale_2, w_out_2, mix_norm_post_2, ff2_norm_pre_2, ff2_w_gate_2,
        ff2_w_up_2, ff2_w_down_2, ff2_norm_post_2,
    )


_drawn_inputs = setup_inputs


def setup_inputs(seed=0):
    import zlib

    import numpy as np

    out = dict(_drawn_inputs(seed))
    spreads = {}
    factors = {'norm_g': 3.113, 'conv_b_2': 4.713, 'd_skip_2': 2.803}
    for name, (base, spread) in spreads.items():
        noise = np.random.default_rng([zlib.crc32(name.encode()), seed]).standard_normal(out[name].shape)
        drawn = base * np.exp(spread * noise) if base else spread * noise
        out[name] = jnp.asarray(drawn.astype(out[name].dtype))
    for name, factor in factors.items():
        out[name] = (out[name] * factor).astype(out[name].dtype)
    return out
```

```python
import math
import numpy as np
import concourse.bass as bass
from concourse import mybir
from contextlib import ExitStack

P = 128
D = 1024
DT = D // P
SEQ = 256
NTOK = 2 * SEQ
DFF = 2816
FT = DFF // P
RING = 4
UCOLS = 256
KT_MAX = 4
EPS = 1e-6
RET_HEADS, RET_DK, RET_DV = 4, 256, 512
SSD_HEADS, SSD_INNER, SSD_GROUPS = 8, 512, 2
POOL_GROUPS = 4
ATTN_HEADS, ATTN_DH = 4, 64
LAYERS2 = 2
LOG1P_TERMS = [1.0 / (2 * k + 1) for k in range(10, 0, -1)]

VEC_FIELDS = [("b_mod", 144), ("norm_g", 48), ("final_g", 8), ("decay", 8)]
LAYER_FIELDS = [("pre1", 8), ("post1", 8), ("mix_pre", 8), ("mix_post", 8), ("pre2", 8), ("post2", 8),
                ("conv_w", 32), ("conv_b", 8), ("ssd_norm", 4), ("pool_scale", 2), ("d_skip", 4),
                ("dt_bias", 8), ("a_log", 8)]


def offsets(fields):
    at, out = 0, {}
    for name, n in fields:
        out[name] = at
        at += n
    return out, at


VEC_AT, VEC_N = offsets(VEC_FIELDS)
LAYER_AT, LAYER_N = offsets(LAYER_FIELDS)


class Gemm:

    def __init__(self, name, n, ks, src, tokens, mode="feature", act="u", evac=None, k_outer=False, **more):
        self.name, self.n, self.ks, self.src, self.tokens = name, n, ks, src, tokens
        self.mode, self.act, self.evac, self.k_outer = mode, act, evac, k_outer
        self.units = 2 * len(ks)
        self.more = more

    def order(self, it):
        starts = [sum(self.ks[:i]) for i in range(len(self.ks))]
        if self.k_outer and isinstance(it, int) and it == 0:
            return [(p, s, k) for s, k in zip(starts, self.ks) for p in range(2)]
        return [(p, s, k) for p in range(2) for s, k in zip(starts, self.ks)]

    def closes(self, it, pair):
        order = self.order(it)
        return 1 + max(u for u, (p, _, _) in enumerate(order) if p == pair)

    def counts(self):
        out = {"unit": self.n * self.units, "pair": self.n,
               "unit_div": self.n * self.units // RING}
        if self.evac == "swiglu":
            out["g"] = self.n
        return out


class Stage:
    def __init__(self, kind, counts, **more):
        self.kind, self.c, self.more = kind, counts, more

    def counts(self):
        return self.c


class Tally:

    def __init__(self):
        self.n = {}

    def __getitem__(self, k):
        return self.n.get(k, 0)

    def add(self, stage):
        for k, v in stage.counts().items():
            self.n[k] = self[k] + v

    def enter(self, layer, stages):
        self.start, self.per = dict(self.n), {}
        for s in stages:
            for k, v in s.counts().items():
                self.per[k] = self.per.get(k, 0) + v
        for k, v in self.per.items():
            self.n[k] = layer * v + self.start.get(k, 0)

    def leave(self, layers):
        self.n = dict(self.start)
        for k, v in self.per.items():
            self.n[k] = self[k] + layers * v


def loop(eng, a, b, body):
    if b - a == 1:
        body(a)
    elif b > a:
        with eng.Fori(a, b) as i:
            body(i)


def host_tables():
    f = np.float32
    w, n = np.arange(P), np.arange(SEQ)
    ang_w, ang_n = 2 * np.pi * np.outer(w, w) / P, 2 * np.pi * np.outer(n, n) / SEQ
    s = 1.0 / math.sqrt(SEQ * P)
    dft = np.zeros((P, 5, SEQ), f)
    dft[:, 0, :P], dft[:, 0, P:] = np.cos(ang_w) * s, np.sin(ang_w) * s
    for b in range(2):
        dft[:, 1 + b] = np.cos(ang_n)[b * P:(b + 1) * P]
        dft[:, 3 + b] = -np.sin(ang_n)[b * P:(b + 1) * P]

    ident = np.eye(P, dtype=f)
    sel = np.zeros((P, 2), f)
    sel[0:2, 0] = sel[2:4, 1] = 1.0

    grid_w, freqs = 64, RET_DK // 4
    inv = np.exp(-math.log(10000.0) * np.arange(freqs) / freqs)
    pos = np.stack([n // grid_w, n % grid_w])
    ang = inv[np.arange(P) % freqs][:, None, None] * pos[None]
    sign = np.where(np.arange(P) < freqs, -1.0, 1.0)[:, None, None]
    ret = np.zeros((P, 5 * SEQ * 1 + 2 * SEQ + P), f)
    ret[:, 0:512] = np.cos(ang).reshape(P, -1)
    ret[:, 512:1024] = (np.sin(ang) * sign).reshape(P, -1)
    delta = n[None, None, :] - (w[:, None, None] + P * np.arange(2)[None, :, None])
    ret[:, 1024:1536] = delta.reshape(P, -1)
    swap = np.zeros((P, P), f)
    swap[np.arange(P) ^ freqs, np.arange(P)] = 1.0
    ret[:, 1536:1664] = swap
    ret = ret[:, :1664]

    key = w[:, None] + P * np.arange(2)[None, :]
    tri = (key[:, :, None] <= n[None, None, :]).astype(f)
    band = np.zeros((P, 2, POOL_GROUPS, SEQ), f)
    for g in range(POOL_GROUPS):
        win = 2 ** (g + 1)
        inside = (key[:, :, None] <= n) & (key[:, :, None] > n - win)
        band[:, :, g] = inside / np.minimum(n + 1, win) - (key[:, :, None] == n)
    rd, theta = ATTN_DH // 4, 500000.0
    invf = theta ** (-np.arange(0, rd, 2) / rd)
    d = np.arange(P) % ATTN_DH
    a2 = np.where(d[:, None] < rd, invf[d % (rd // 2)][:, None] * n[None], 0.0)
    sg = np.where(d < rd // 2, -1.0, 1.0)[:, None]
    sw = np.zeros((P, P), f)
    partner = np.where(d < rd, np.arange(P) ^ (rd // 2), np.arange(P))
    sw[partner, np.arange(P)] = 1.0
    mask = np.where(n[None, None, :] <= key[:, :, None], 0.0, -1e30)
    two = np.concatenate([tri.reshape(P, -1), band.reshape(P, -1), np.cos(a2), np.sin(a2) * sg,
                          mask.reshape(P, -1), sw, ident], axis=1).astype(f)
    return dft.reshape(P, -1), sel, ret, two


TWO_FIELDS = [("tri", 512), ("band", 2048), ("cos", 256), ("sin", 256), ("mask", 512), ("swap", 128),
              ("ident", 128)]
TWO_AT, TWO_N = offsets(TWO_FIELDS)


def build(nc, T):
    f32, f32r = mybir.dt.float32, mybir.dt.float32r
    ALU, ACT = mybir.AluOpType, mybir.ActivationFunctionType
    AX = mybir.AxisListType.X

    def rows(ap):
        return ap.rearrange("(k p) n -> p k n", p=P)

    def two_halves(w, second):
        return lambda it, pair, k0, kt: rows(w)[:, k0:k0 + kt, bass.ds(it * UCOLS + pair * second, UCOLS)]

    def in_turn(w, first=0):
        return lambda it, pair, k0, kt: rows(w)[:, k0:k0 + kt, bass.ds(it * 2 * UCOLS + pair * UCOLS + first, UCOLS)]

    def stats(tokens, source, half=False):
        return Stage("stats", {"sq": DT, "stat": 1}, tokens=tokens, source=source, half=half)

    def block1():
        out = []
        for i in range(2):
            for piece in range(3):
                tokens = NTOK if i == 0 or piece < 2 else SEQ
                out.append(stats(tokens, "load" if i == piece == 0 else "gemm"))
                out.append(Gemm("mod", 6, [4, 4], in_turn(T["w_mod"][i], piece * 3 * D), tokens, mode="mod",
                                evac="rows"))
                out.append(Stage("coef", {"modcol": 1, "coef": 1}, layer=i, piece=piece))
                out.append(Stage("apply", {"xr": DT, "uhi": DT, "ulo": DT}, tokens=tokens, mod=True))
                if piece != 1:
                    j = piece // 2
                    out.append(Gemm("up", 11, [4, 4], two_halves(T["ffn_w_in"][i, j], DFF), tokens,
                                    evac="swiglu", k_outer=True, waits="ulo", wide=True))
                    out.append(Gemm("down", 2, [4, 4, 4, 4, 3, 3], in_turn(T["ffn_w_out"][i, j]), tokens, act="g",
                                    evac="resid", waits="g", wide=True))
                elif i == 0:
                    out.append(Stage("fourier", {"fl": 16}, tokens=tokens))
                    out.append(Gemm("fnet", 2, [4, 4], in_turn(T["fnet_w_out"][0]), tokens, evac="resid",
                                    k_outer=False, waits="fl"))
                else:
                    w = T["ret_w_in"][0]
                    out.append(Gemm("q", 2, [4, 4], in_turn(w), SEQ, evac="to_q", k_outer=True, waits="ulo"))
                    out.append(Gemm("k", 2, [4, 4], in_turn(w, D), NTOK, evac="to_k"))
                    out.append(Gemm("v", 4, [4, 4], in_turn(w, 2 * D), NTOK, mode="tokens", evac="to_v"))
                    out.append(Gemm("gate", 4, [4, 4], in_turn(w, 4 * D), SEQ, evac="to_gate"))
                    out.append(Stage("retention", {"mix_lo": RET_HEADS}))
                    out.append(Gemm("ret_out", 2, [4, 4, 4, 4], in_turn(T["ret_w_out"][0]), SEQ, evac="resid",
                                    waits="mix_lo", view="ret"))
        out.append(stats(SEQ, "gemm"))
        out.append(Stage("final", {"post": DT}))
        return out

    def block2(l):
        w = lambda name: T[name][l]
        wi = w("w_in_2")
        fixed = lambda cols: (lambda it, pair, k0, kt: rows(wi)[:, k0:k0 + kt, cols[pair]:cols[pair] + UCOLS])

        def ffn(n, pre, post):
            gate, up = w(f"ff{n}_w_gate_2"), w(f"ff{n}_w_up_2")
            pick = lambda it, pair, k0, kt: rows((gate, up)[pair])[:, k0:k0 + kt, bass.ds(it * UCOLS, UCOLS)]
            return [stats(SEQ, "post"), Stage("apply", {"xr": DT, "uhi": DT, "ulo": DT}, tokens=SEQ, gain=pre),
                    Gemm("up", 11, [4, 4], pick, SEQ, evac="swiglu", k_outer=True, waits="ulo",
                         wide=False),
                    Gemm("down", 2, [4, 4, 4, 4, 3, 3], in_turn(w(f"ff{n}_w_down_2")), SEQ, act="g", evac="store",
                         waits="g", wide=False),
                    stats(SEQ, "store", half=True), Stage("post", {"post": DT, "px": DT}, gain=post)]
        return ffn(1, "pre1", "post1") + [
            stats(SEQ, "post"), Stage("apply", {"xr": DT, "uhi": DT, "ulo": DT}, tokens=SEQ, gain="mix_pre"),
            Gemm("z", 1, [4, 4], in_turn(wi, 0), SEQ, evac="to_z", k_outer=True, waits="ulo"),
            Gemm("pool_v", 1, [4, 4], fixed((1544, 2312)), SEQ, mode="tokens", evac="to_pool_v"),
            Gemm("q_k", 1, [4, 4], fixed((1800, 2056)), SEQ, evac="to_q_k"),
            Gemm("xbc", 2, [4, 4], in_turn(wi, 512), SEQ, evac="to_xbc"),
            Stage("mixer", {"mix_lo": 3}),
            Gemm("mix_out", 2, [4, 4], in_turn(w("w_out_2")), SEQ, evac="store", waits="mix_lo"),
            stats(SEQ, "store"), Stage("post", {"post": DT, "px": DT}, gain="mix_post")
        ] + ffn(2, "pre2", "post2")

    def follower(stages, j):
        return next((s for s in stages[j + 1:] if isinstance(s, Gemm)), None)

    ctx = ExitStack()
    with ctx:
        def overlay(specs):
            with ExitStack() as s:
                return [s.enter_context(nc.sbuf_tensor(n, shape, dt)) for n, shape, dt in specs]

        def sb(name, shape, dt=f32):
            return ctx.enter_context(nc.sbuf_tensor(name, shape, dt))

        def sem(name):
            return ctx.enter_context(nc.semaphore(name))

        h = sb("h", [P, DT, NTOK])
        f_out = h[:, :, SEQ:NTOK]
        u_hi, u_lo = sb("u_hi", [P, DT, NTOK], f32r), sb("u_lo", [P, DT, NTOK], f32r)
        raw = sb("raw", [P, RING, KT_MAX * UCOLS])
        w_hi = sb("w_hi", [P, RING, KT_MAX * UCOLS], f32r)
        w_lo = sb("w_lo", [P, RING, KT_MAX * UCOLS], f32r)
        ones = sb("ones", [P, P])
        acc = sb("acc", [P, NTOK])
        rstd = sb("rstd", [P, NTOK])
        tmp1, tmp2 = sb("tmp1", [P, 2, NTOK]), sb("tmp2", [P, 2, NTOK])
        vec = sb("vec", [P, VEC_N])
        lvec = sb("lvec", [P, LAYER_N])
        mod = sb("mod", [P, 24, 2])
        coef = sb("coef", [P, DT, 2])
        cond_hi = sb("cond_hi", [P, DT, P], f32r)
        cond = sb("cond", [P, DT, 2])
        sel = sb("sel", [P, 2])
        eps = sb("eps", [P, 2])

        g_hi, g_lo = overlay([("g_hi", [P, FT, NTOK], f32r), ("g_lo", [P, FT, NTOK], f32r)])
        mod_rows, = overlay([("mod_rows", [P, 3 * D], f32)])
        dft, dft_hi, dft_lo, ab_hi, ab_lo = overlay([
            ("dft", [P, 5, SEQ], f32), ("dft_hi", [P, 5, SEQ], f32r), ("dft_lo", [P, 5, SEQ], f32r),
            ("ab_hi", [P, 2, NTOK], f32r), ("ab_lo", [P, 2, NTOK], f32r)])
        rq, rk, rv, rg, rtab, decay, weighted, lgam = overlay([
            ("rq", [P, DT, SEQ], f32), ("rk", [P, DT, NTOK], f32), ("rv", [P, 4, 2 * D], f32),
            ("rg", [P, 16, SEQ], f32), ("rtab", [P, 1664], f32), ("decay_w", [P, 4, SEQ], f32),
            ("weighted", [P, 4, SEQ], f32), ("lgam", [P, 64], f32)])
        ro = tmp1[:, :, :].rearrange("p a (b n) -> p (a b) n", n=SEQ)
        rt = tmp2[:, :, :].rearrange("p a (b n) -> p (a b) n", n=SEQ)
        rcos = rtab[:, 0:512].rearrange("p (r n) -> p r n", r=2)
        rsin = rtab[:, 512:1024].rearrange("p (r n) -> p r n", r=2)
        rdelta = rtab[:, 1024:1536].rearrange("p (b n) -> p b n", b=2)
        rswap = rtab[:, 1536:1664]

        tab_spec = [("tables", [P, TWO_N], f32), ("poolw", [P, 2, P], f32), ("dtw", [P, 64], f32)]
        tables, poolw, dtw, g2_hi, g2_lo = overlay(tab_spec + [
            ("g2_hi", [P, FT, SEQ], f32r), ("g2_lo", [P, FT, SEQ], f32r)])
        (_, _, _, zs, xpad, cx, pool_u, att_v, qk, xtok, cb, seg, mixf, probs, probs_t, dtw_hi, dtw_lo,
         small) = overlay([(n + "_", s, d) for n, s, d in tab_spec] + [
             ("zs", [P, 4, SEQ], f32), ("xpad", [P, 8, SEQ + 3], f32), ("cx", [P, 8, SEQ], f32),
             ("pool_u", [P, 2, SEQ], f32), ("att_v", [P, 2, SEQ], f32), ("qk", [P, 4, SEQ], f32),
             ("xtok", [P, 2, SSD_INNER], f32), ("cb", [P, 4, SEQ], f32), ("seg", [P, 2, 2, SEQ], f32),
             ("mixf", [P, 8, SEQ], f32), ("probs", [P, 2, SEQ], f32), ("probs_t", [P, 2, SEQ], f32),
             ("dtw_hi", [P, 64], f32r), ("dtw_lo", [P, 64], f32r), ("small", [P, 320], f32)])
        tab = {n: tables[:, TWO_AT[n]:TWO_AT[n] + c] for n, c in TWO_FIELDS}
        tri = tab["tri"].rearrange("p (b n) -> p b n", b=2)
        band = tab["band"].rearrange("p (b g n) -> p b g n", b=2, g=POOL_GROUPS)
        mask = tab["mask"].rearrange("p (b n) -> p b n", b=2)
        small_fields, _ = offsets([(n, 16) for n in """dt_in neg_abs e_dt s_den s_dt s2 series log1p dt da neg_a
                                                       acs mx neg_mx sums inv""".split()])

        def sm(name):
            return small[:, small_fields[name]:small_fields[name] + 16].rearrange("p (b n) -> p b n", b=2)

        ps = ctx.enter_context(nc.psum_tensor("ps", [P, 8, 512], f32))
        STAT = 4

        def vecs(name, a=0, n=1):
            return vec[:, VEC_AT[name] + a:VEC_AT[name] + a + n]

        def lv(name, a=0, n=1):
            return lvec[:, LAYER_AT[name] + a:LAYER_AT[name] + a + n]

        hi_ready = sem("hi_ready")
        lo_ready = sem("lo_ready")
        unit_used = sem("unit_used")
        banks01_read = sem("banks01_read")
        banks23_read = sem("banks23_read")
        x_landed = sem("x_landed")
        vec_landed = sem("vec_landed")
        cond_landed = sem("cond_landed")
        sel_landed = sem("sel_landed")
        dft_landed = sem("dft_landed")
        ret_landed = sem("ret_landed")
        tables_landed = sem("tables_landed")
        lvec_landed = sem("lvec_landed")
        poolw_landed = sem("poolw_landed")
        dtw_landed = sem("dtw_landed")
        out_landed = sem("out_landed")
        setup_ready = sem("setup_ready")
        cond_silu_ready = sem("cond_silu_ready")
        cond_ready = sem("cond_ready")
        cond_lo_ready = sem("cond_lo_ready")
        squares_ready = sem("squares_ready")
        sums_ready = sem("sums_ready")
        stat_ready = sem("stat_ready")
        root_ready = sem("root_ready")
        rstd_ready = sem("rstd_ready")
        scaled_ready = sem("scaled_ready")
        u_hi_ready = sem("u_hi_ready")
        u_lo_ready = sem("u_lo_ready")
        g_hi_ready = sem("g_hi_ready")
        g_lo_ready = sem("g_lo_ready")
        modcol_ready = sem("modcol_ready")
        coef_ready = sem("coef_ready")
        post_ready = sem("post_ready")
        post_scaled_ready = sem("post_scaled_ready")
        dft_hi_ready = sem("dft_hi_ready")
        dft_lo_ready = sem("dft_lo_ready")
        ab_ready = sem("ab_ready")
        ab_hi_ready = sem("ab_hi_ready")
        ab_lo_ready = sem("ab_lo_ready")
        f_ready = sem("f_ready")
        f_hi_ready = sem("f_hi_ready")
        f_lo_ready = sem("f_lo_ready")
        dve_order = sem("dve_order")
        mix_hi_ready = sem("mix_hi_ready")
        mix_lo_ready = sem("mix_lo_ready")
        swapped = sem("swapped")
        scores_ready = sem("scores_ready")
        head_out_ready = sem("head_out_ready")
        head_stat_ready = sem("head_stat_ready")
        decay_exp_ready = sem("decay_exp_ready")
        decays_ready = sem("decays_ready")
        head_out_copied = sem("head_out_copied")
        head_squares_ready = sem("head_squares_ready")
        head_root_ready = sem("head_root_ready")
        decay_abs_ready = sem("decay_abs_ready")
        log_gamma_ready = sem("log_gamma_ready")
        roped = sem("roped")
        exponents_ready = sem("exponents_ready")
        weighted_ready = sem("weighted_ready")
        head_sums_ready = sem("head_sums_ready")
        centred_ready = sem("centred_ready")
        gated_ready = sem("gated_ready")
        dt_ready = sem("dt_ready")
        qk_swapped = sem("qk_swapped")
        pool_mean_ready = sem("pool_mean_ready")
        cb_ready = sem("cb_ready")
        pool_out_ready = sem("pool_out_ready")
        xtok_ready = sem("xtok_ready")
        acs_ready = sem("acs_ready")
        head_acs_ready = sem("head_acs_ready")
        head_y_ready = sem("head_y_ready")
        att_scores_ready = sem("att_scores_ready")
        probs_turned = sem("probs_turned")
        att_out_ready = sem("att_out_ready")
        ssd_stat_ready = sem("ssd_stat_ready")
        dtw_hi_ready = sem("dtw_hi_ready")
        conv_ready = sem("conv_ready")
        pool_mean_copied = sem("pool_mean_copied")
        dt_exp_ready = sem("dt_exp_ready")
        xtok_copied = sem("xtok_copied")
        segment_exp_ready = sem("segment_exp_ready")
        probs_exp_ready = sem("probs_exp_ready")
        probs_t_copied = sem("probs_t_copied")
        att_copied = sem("att_copied")
        ssd_squares_ready = sem("ssd_squares_ready")
        ssd_root_ready = sem("ssd_root_ready")
        dtw_lo_ready = sem("dtw_lo_ready")
        conv_sum_ready = sem("conv_sum_ready")
        dt_taken = sem("dt_taken")
        da_ready = sem("da_ready")
        qk_roped = sem("qk_roped")
        cb_taken = sem("cb_taken")
        pool_out_taken = sem("pool_out_taken")
        acs_taken = sem("acs_taken")
        segment_taken = sem("segment_taken")
        att_masked = sem("att_masked")
        max_ready = sem("max_ready")
        segment_ready = sem("segment_ready")
        probs_ready = sem("probs_ready")
        y_gated = sem("y_gated")
        ssd_sums_ready = sem("ssd_sums_ready")
        y_normed = sem("y_normed")
        poolw_zeroed = sem("poolw_zeroed")
        raw_landed = [sem(f"raw_landed{i}") for i in range(RING)]
        read = (banks01_read, banks23_read)

        def begun(value):
            return not isinstance(value, int) or value > 0

        class Order:

            def __init__(self, eng, sem):
                self.eng, self.sem, self.n = eng, sem, 0

            def enter(self, layer, per):
                self.first, self.per, self.n = self.n, per, layer * per + self.n
                self.k = 0

            def leave(self, layers):
                assert self.k == self.per, ("instructions of a layer in order", self.k)
                self.n = self.first + layers * self.per

            def link(self, ins):
                self.n = self.n + 1
                self.k = self.k + 1 if hasattr(self, "k") else 0
                ins.then_inc(self.sem, 1)
                self.eng.wait_ge(self.sem, self.n)

        def unit_rows(g, it, u):
            return g.order(it)[u]

        def operand(g, k):
            if g.more.get("view") == "ret":
                v = [t[:, :, :].rearrange("p a (b n) -> p (a b) n", n=SEQ) for t in (u_hi, u_lo)]
                return [x[:, k, 0:g.tokens] for x in v]
            pair = (u_hi, u_lo) if g.act == "u" else (g_hi, g_lo) if g.more["wide"] else (g2_hi, g2_lo)
            return [t[:, k, 0:g.tokens] for t in pair]

        def sp_gemm(sp, g, t):
            def turn(it):
                for u, (pair, k0, kt) in enumerate(unit_rows(g, it, u_) for u_ in range(g.units)):
                    q, slot = it * g.units + u + t["unit"], u % RING
                    if begun(q - (RING - 1)):
                        sp.wait_ge(lo_ready, q - (RING - 1))
                    dst = raw[:, slot, 0:kt * UCOLS].rearrange("p (k n) -> p k n", k=kt)
                    sp.dma_start(dst, g.src(it, pair, k0, kt)).then_inc(raw_landed[slot], 16)
            turn(0)
            loop(sp, 1, g.n, turn)

        def split_hi(act, g, t, it, u):
            q, slot = it * g.units + u + t["unit"], u % RING
            cols = unit_rows(g, it, u)[2] * UCOLS
            landed = (it * (g.units // RING) + u // RING) * 16 + (t["unit_div"]) * 16 + 16
            act.wait_ge(raw_landed[slot], landed)
            if begun(q - (RING - 1)):
                act.wait_ge(unit_used, q - (RING - 1))
            act.activation(w_hi[:, slot, 0:cols], raw[:, slot, 0:cols], ACT.Copy).then_inc(hi_ready, 1)

        def split_lo(dve, g, t, it, u):
            q, slot = it * g.units + u + t["unit"], u % RING
            cols = unit_rows(g, it, u)[2] * UCOLS
            dve.wait_ge(hi_ready, q + 1)
            dve.tensor_tensor(w_lo[:, slot, 0:cols], raw[:, slot, 0:cols], w_hi[:, slot, 0:cols].bitcast(f32),
                              ALU.subtract).then_inc(lo_ready, 1)

        def stream(eng, g, t, nxt, split, evacuate):
            t_next = {"unit": t["unit"] + g.n * g.units, "unit_div": t["unit_div"] + g.n * (g.units // RING)}

            def turn(it):
                last = isinstance(it, int) and it == g.n - 1
                for u in range(g.units):
                    v = u + RING
                    if v < g.units:
                        split(eng, g, t, it, v)
                    elif not last:
                        split(eng, g, t, it + 1, v - g.units)
                    elif nxt is not None:
                        split(eng, nxt, t_next, 0, v - g.units)
                    for pair in range(2):
                        if g.closes(it, pair) == u + 1:
                            evacuate(eng, g, t, it, pair)
            turn(0)
            if g.n > 1:
                loop(eng, 1, g.n - 1, turn)
                turn(g.n - 1)

        def complete(eng, g, t, it, pair):
            if begun(it * g.units + t["unit"] + g.closes(it, pair)):
                eng.wait_ge(unit_used, it * g.units + t["unit"] + g.closes(it, pair))

        def blocks(g, pair):
            return ps[:, 2 * pair:2 * pair + 2, 0:g.tokens]

        def act_evacuate(act, g, t, it, pair):
            done = read[pair]
            tile2 = bass.ds(it * 4 + 2 * pair, 2)
            if g.evac == "swiglu":
                if pair == 0:
                    complete(act, g, t, it, 0)
                    if begun(it + t["pair"]):
                        act.wait_ge(banks23_read, it + t["pair"])
                    act.activation(tmp1[:, :, 0:g.tokens], blocks(g, 0), ACT.Silu).then_inc(done, 1)
                else:
                    act.wait_ge(banks23_read, it + t["pair"] + 1)
                    hi = g_hi if g.more["wide"] else g2_hi
                    act.activation(hi[:, bass.ds(it * 2, 2), 0:g.tokens], tmp2[:, :, 0:g.tokens],
                                   ACT.Copy).then_inc(g_hi_ready, 1)
                return
            if g.evac in ("resid", "store", "rows"):
                return
            complete(act, g, t, it, pair)
            func = ACT.Silu if g.evac in ("to_gate", "to_z") else ACT.Copy
            if g.evac == "to_v":
                src = ps[:, 2 * pair:2 * pair + 2, :].rearrange("p b (c n) -> p (b c) n", c=2)
                dst = rv[:, :, bass.ds(it * 2 * UCOLS + pair * UCOLS, UCOLS)]
            elif g.evac == "to_pool_v":
                src = ps[:, 2 * pair, :].rearrange("p (c n) -> p c n", c=2)
                dst = (pool_u, att_v)[pair][:, :, :]
            elif g.evac == "to_q_k":
                src, dst = blocks(g, pair), qk[:, 2 * pair:2 * pair + 2, :]
            elif g.evac == "to_xbc":
                src, dst = blocks(g, pair), xpad[:, tile2, 3:3 + SEQ]
            else:
                to = {"to_q": rq, "to_k": rk, "to_gate": rg, "to_z": zs}[g.evac]
                src, dst = blocks(g, pair), to[:, tile2, 0:g.tokens]
            act.activation(dst, src, func).then_inc(done, 1)

        def dve_evacuate(dve, g, t, it, pair):
            done = read[pair]
            if g.evac == "swiglu":
                if pair == 1:
                    complete(dve, g, t, it, 1)
                    dve.wait_ge(banks01_read, it + t["pair"] + 1)
                    if begun(it + t["g"]):
                        dve.wait_ge(g_lo_ready, it + t["g"])
                    dve.tensor_tensor(tmp2[:, :, 0:g.tokens], blocks(g, 1), tmp1[:, :, 0:g.tokens],
                                      ALU.mult).then_inc(done, 1)
                    dve.wait_ge(g_hi_ready, it + t["g"] + 1)
                    hi, lo = (g_hi, g_lo) if g.more["wide"] else (g2_hi, g2_lo)
                    two = bass.ds(it * 2, 2)
                    dve.tensor_tensor(lo[:, two, 0:g.tokens], tmp2[:, :, 0:g.tokens],
                                      hi[:, two, 0:g.tokens].bitcast(f32), ALU.subtract
                                      ).then_inc(g_lo_ready, 1)
                return
            if g.evac == "rows":
                complete(dve, g, t, it, pair)
                at = bass.ds(it * 2 * UCOLS + pair * UCOLS, UCOLS)
                dve.tensor_copy(mod_rows[0:4, at], ps[0:4, 2 * pair, 0:UCOLS]).then_inc(done, 1)
            elif g.evac == "store":
                complete(dve, g, t, it, pair)
                dve.tensor_copy(f_out[:, bass.ds(it * 4 + 2 * pair, 2), :], blocks(g, pair)).then_inc(done, 1)
            elif g.evac == "resid":
                complete(dve, g, t, it, pair)
                for b in range(2):
                    for s in range(g.tokens // SEQ):
                        tile, tok = it * 4 + 2 * pair + b, slice(s * SEQ, (s + 1) * SEQ)
                        ins = dve.scalar_tensor_tensor(h[:, tile, tok], ps[:, 2 * pair + b, tok],
                                                       mod[:, 16 + tile, s:s + 1], h[:, tile, tok],
                                                       ALU.mult, ALU.add)
                ins.then_inc(done, 1)

        def pe_gemm(pe, g, t):
            def turn(it):
                for u in range(g.units):
                    pair, k0, kt = unit_rows(g, it, u)
                    slot = u % RING
                    if k0 == 0:
                        if begun(it + t["pair"]):
                            pe.wait_ge(read[pair], it + t["pair"])
                    pe.wait_ge(lo_ready, it * g.units + u + t["unit"] + 1)
                    final = k0 + kt == sum(g.ks)
                    if g.mode == "mod":
                        for k in range(kt):
                            for w in (w_hi, w_lo):
                                ins = pe.matmul(ps[:, 2 * pair, 0:UCOLS], cond_hi[:, k0 + k, :],
                                                w[:, slot, k * UCOLS:(k + 1) * UCOLS],
                                                start=k0 + k == 0 and w is w_hi,
                                                stop=final and k == kt - 1 and w is w_lo)
                    elif g.mode == "tokens":
                        for tb in range(g.tokens // P):
                            out = ps[:, 2 * pair + tb // 2, (tb % 2) * UCOLS:(tb % 2 + 1) * UCOLS]
                            for k in range(kt):
                                if tb == 0 and it_is_first(it):
                                    arrived(pe, g, t, k0 + k)
                                hi, lo = [x[:, tb * P:(tb + 1) * P] for x in operand(g, k0 + k)]
                                cols = slice(k * UCOLS, (k + 1) * UCOLS)
                                for n, (a, w) in enumerate(((hi, w_hi), (hi, w_lo), (lo, w_hi))):
                                    ins = pe.matmul(out, a, w[:, slot, cols],
                                                    start=k0 + k == 0 and n == 0 and tb % 2 == 0,
                                                    stop=final and k == kt - 1 and n == 2, skip_group_check=True)
                    else:
                        for b in range(2):
                            out = ps[:, 2 * pair + b, 0:g.tokens]
                            for k in range(kt):
                                if b == 0 and it_is_first(it):
                                    arrived(pe, g, t, k0 + k)
                                hi, lo = operand(g, k0 + k)
                                cols = slice(k * UCOLS + b * P, k * UCOLS + b * P + P)
                                for n, (w, a) in enumerate(((w_hi, hi), (w_hi, lo), (w_lo, hi))):
                                    ins = pe.matmul(out, w[:, slot, cols], a, start=k0 + k == 0 and n == 0,
                                                    stop=final and k == kt - 1 and n == 2)
                    ins.then_inc(unit_used, 1)
            turn(0)
            loop(pe, 1, g.n, turn)

        def it_is_first(it):
            return isinstance(it, int) and it == 0

        def arrived(pe, g, t, k):
            what = g.more.get("waits")
            if what == "ulo":
                if begun(t["ulo"] - DT + k + 1):
                    pe.wait_ge(u_lo_ready, t["ulo"] - DT + k + 1)
            elif what == "g" and k in (0, 19, 20):
                if begun(t["g"] - (FT // 2) + k // 2 + 1 if k else t["g"] - 2):
                    pe.wait_ge(g_lo_ready, t["g"] - (FT // 2) + k // 2 + 1 if k else t["g"] - 2)
            elif what == "fl" and k == 0:
                pe.wait_ge(f_lo_ready, 16)
            elif what == "mix_lo" and k == 0:
                if begun(t["mix_lo"]):
                    pe.wait_ge(mix_lo_ready, t["mix_lo"])

        def source_tile(g, src, tile):
            n = g.more["tokens"]
            return (f_out[:, tile, 0:n] if src == "store" else h[:, tile, 0:n])

        def act_stats(act, g, t):
            src, n = g.more["source"], g.more["tokens"]
            for k in range(DT):
                if src == "load":
                    if k == 0:
                        act.wait_ge(x_landed, 16)
                elif src == "post":
                    if begun(t["post"] - DT + k + 1):
                        act.wait_ge(post_ready, t["post"] - DT + k + 1)
                else:
                    if begun(t["pair"] - 1 + k // 4):
                        act.wait_ge(read[(k // 2) % 2], t["pair"] - 1 + k // 4)
                if begun(t["sq"] + k - 1):
                    act.wait_ge(sums_ready, t["sq"] + k - 1)
                act.activation(tmp1[:, k % 2, 0:n], source_tile(g, src, k), ACT.Square
                               ).then_inc(squares_ready, 1)
            act.wait_ge(stat_ready, t["stat"] + 1)
            dm = 1.0 / D
            four = 4.0 if g.more.get("half") else 1.0
            act.activation(rstd[:, 0:n], ps[:, STAT, 0:n], ACT.Sqrt, scale=dm * four,
                           bias=eps[:, 1:2] if four == 4.0 else eps[:, 0:1]).then_inc(root_ready, 1)

        def dve_stats(dve, g, t):
            n = g.more["tokens"]
            for k in range(DT):
                dve.wait_ge(squares_ready, t["sq"] + k + 1)
                if k == 0:
                    dve.tensor_copy(acc[:, 0:n], tmp1[:, 0, 0:n]).then_inc(sums_ready, 1)
                else:
                    if begun(t["sq"] + k):
                        dve.wait_ge(sums_ready, t["sq"] + k)
                    dve.tensor_tensor(acc[:, 0:n], acc[:, 0:n], tmp1[:, k % 2, 0:n], ALU.add
                                      ).then_inc(sums_ready, 1)
            dve.wait_ge(root_ready, t["stat"] + 1)
            dve.reciprocal(rstd[:, 0:n], rstd[:, 0:n]).then_inc(rstd_ready, 1)

        def pe_stats(pe, g, t):
            n = g.more["tokens"]
            pe.wait_ge(sums_ready, t["sq"] + DT)
            pe.matmul(ps[:, STAT, 0:n], ones[:, :], acc[:, 0:n], start=True, stop=True
                      ).then_inc(stat_ready, 1)

        def act_apply(act, g, t):
            n = g.more["tokens"]
            if g.more.get("mod"):
                if begun(t["coef"]):
                    act.wait_ge(coef_ready, t["coef"])
            for k in range(DT):
                act.wait_ge(scaled_ready, t["xr"] + k + 1)
                if begun(t["ulo"] + k - 1):
                    act.wait_ge(u_lo_ready, t["ulo"] + k - 1)
                for out in (tmp1[:, k % 2, :], u_hi[:, k, :]):
                    if g.more.get("mod"):
                        for s in range(n // SEQ):
                            tok = slice(s * SEQ, (s + 1) * SEQ)
                            ins = act.activation(out[:, tok], tmp2[:, k % 2, tok], ACT.Identity,
                                                 scale=coef[:, k, s:s + 1], bias=mod[:, k, s:s + 1])
                    else:
                        ins = act.activation(out[:, 0:n], tmp2[:, k % 2, 0:n], ACT.Copy,
                                             scale=lv(g.more["gain"], k))
                ins.then_inc(u_hi_ready, 1)

        def dve_apply(dve, g, t):
            n = g.more["tokens"]
            if begun(t["stat"]):
                dve.wait_ge(rstd_ready, t["stat"])

            def scaled(k):
                if begun(t["uhi"] + k - 1):
                    dve.wait_ge(u_hi_ready, t["uhi"] + k - 1)
                dve.tensor_tensor(tmp2[:, k % 2, 0:n], h[:, k, 0:n], rstd[:, 0:n], ALU.mult
                                  ).then_inc(scaled_ready, 1)
            scaled(0)
            for k in range(DT):
                if k + 1 < DT:
                    scaled(k + 1)
                dve.wait_ge(u_hi_ready, t["uhi"] + k + 1)
                dve.tensor_tensor(u_lo[:, k, 0:n], tmp1[:, k % 2, 0:n], u_hi[:, k, 0:n].bitcast(f32),
                                  ALU.subtract).then_inc(u_lo_ready, 1)

        def dve_post(dve, g, t, first=False):
            if begun(t["stat"]):
                dve.wait_ge(rstd_ready, t["stat"])
            for k in range(DT + 1):
                if k < DT:
                    if begun(t["post"] + k - 1):
                        dve.wait_ge(post_ready, t["post"] + k - 1)
                    dve.tensor_tensor(tmp2[:, k % 2, 0:SEQ], f_out[:, k, :], rstd[:, 0:SEQ], ALU.mult
                                      ).then_inc(post_scaled_ready, 1)
                if k > 0:
                    if begun(t["px"] + k):
                        dve.wait_ge(post_scaled_ready, t["px"] + k)
                    dve.scalar_tensor_tensor(h[:, k - 1, 0:SEQ], tmp2[:, (k - 1) % 2, 0:SEQ],
                                             lv(g.more["gain"], k - 1), h[:, k - 1, 0:SEQ], ALU.mult, ALU.add
                                             ).then_inc(post_ready, 1)

        def pe_coef(pe, g, t):
            if begun(t["pair"]):
                pe.wait_ge(banks01_read, t["pair"])
            if begun(t["pair"]):
                pe.wait_ge(banks23_read, t["pair"])
            for j in range(24):
                ins = pe.matmul(ps[:, 7, 2 * j:2 * j + 2], mod_rows[0:4, j * P:(j + 1) * P], sel[0:4, :],
                                start=True, stop=True)
            ins.then_inc(modcol_ready, 1)

        def dve_coef(dve, g, t, order):
            i, piece = g.more["layer"], g.more["piece"]
            dve.wait_ge(modcol_ready, t["modcol"] + 1)
            bias = vecs("b_mod", i * 72 + piece * 24, 24).unsqueeze(2).to_broadcast([P, 24, 2])
            order.link(dve.tensor_tensor(mod[:, :, :], ps[:, 7, 0:48].rearrange("p (j s) -> p j s", s=2), bias,
                                         ALU.add))
            if piece != 1:
                dve.tensor_scalar(mod[:, 16:24, :], mod[:, 16:24, :], 0.5, None, ALU.mult)
            gain = vecs("norm_g", (i * 3 + piece) * 8, 8).unsqueeze(2).to_broadcast([P, DT, 2])
            dve.scalar_tensor_tensor(coef[:, :, :], mod[:, 8:16, :], 1.0, gain, ALU.add, ALU.mult
                                     ).then_inc(coef_ready, 1)

        def log1p(dve, order, e, den, s, s2, r, out):
            order.link(dve.tensor_scalar(den, e, 2.0, None, ALU.add))
            order.link(dve.reciprocal(den, den))
            order.link(dve.tensor_tensor(s, e, den, ALU.mult))
            order.link(dve.tensor_tensor(s2, s, s, ALU.mult))
            order.link(dve.tensor_scalar(r, s2, LOG1P_TERMS[0], None, ALU.mult))
            for c in LOG1P_TERMS[1:]:
                order.link(dve.scalar_tensor_tensor(r, r, c, s2, ALU.add, ALU.mult))
            order.link(dve.scalar_tensor_tensor(out, r, 1.0, s, ALU.add, ALU.mult))
            order.link(dve.tensor_scalar(out, out, 2.0, None, ALU.mult))

        def pe_fourier(pe, t):
            def step1(j):
                g, s = j // 2, j % 2
                if begun(t["ulo"]):
                    pe.wait_ge(u_lo_ready, t["ulo"])
                pe.wait_ge(dft_lo_ready, 1)
                if begun(j - 1):
                    pe.wait_ge(ab_lo_ready, j - 1)
                for tb in range(2):
                    tok = slice(s * SEQ + tb * P, s * SEQ + (tb + 1) * P)
                    for n, (a, w) in enumerate(((u_hi, dft_hi), (u_hi, dft_lo), (u_lo, dft_hi))):
                        ins = pe.matmul(ps[:, 5 + j % 2, tb * SEQ:(tb + 1) * SEQ], a[:, g, tok], w[:, 0, :],
                                        start=n == 0, stop=n == 2)
                ins.then_inc(ab_ready, 1)

            def step2(j):
                pe.wait_ge(ab_lo_ready, j + 1)
                if begun(j - 1):
                    pe.wait_ge(f_lo_ready, j - 1)
                n = 0
                for tb in range(2):
                    for part in range(2):
                        cols = slice(tb * SEQ + part * P, tb * SEQ + (part + 1) * P)
                        for a, w in ((ab_hi, dft_hi), (ab_hi, dft_lo), (ab_lo, dft_hi)):
                            ins = pe.matmul(ps[:, j % 2, 0:SEQ], a[:, j % 2, cols], w[:, 1 + 2 * part + tb, :],
                                            start=n == 0, stop=n == 11)
                            n += 1
                ins.then_inc(f_ready, 1)
            step1(0)
            for j in range(16):
                if j + 1 < 16:
                    step1(j + 1)
                step2(j)

        def act_fourier(act, t):
            act.wait_ge(dft_landed, 16)
            act.activation(dft_hi[:, :, :], dft[:, :, :], ACT.Copy).then_inc(dft_hi_ready, 1)

            def take_ab(j):
                act.wait_ge(ab_ready, j + 1)
                if begun(j - 1):
                    act.wait_ge(f_ready, j - 1)
                act.activation(ab_hi[:, j % 2, :], ps[:, 5 + j % 2, :], ACT.Copy).then_inc(ab_hi_ready, 1)
            take_ab(0)
            for j in range(16):
                if j + 1 < 16:
                    take_ab(j + 1)
                g, tok = j // 2, slice((j % 2) * SEQ, (j % 2 + 1) * SEQ)
                act.wait_ge(f_ready, j + 1)
                act.activation(u_hi[:, g, tok], ps[:, j % 2, 0:SEQ], ACT.Copy).then_inc(f_hi_ready, 1)

        def dve_fourier(dve, t):
            dve.wait_ge(dft_hi_ready, 1)
            dve.tensor_tensor(dft_lo[:, :, :], dft[:, :, :], dft_hi[:, :, :].bitcast(f32), ALU.subtract
                              ).then_inc(dft_lo_ready, 1)

            def take_ab(j):
                dve.wait_ge(ab_hi_ready, j + 1)
                dve.tensor_tensor(ab_lo[:, j % 2, :], ps[:, 5 + j % 2, :], ab_hi[:, j % 2, :].bitcast(f32),
                                  ALU.subtract).then_inc(ab_lo_ready, 1)
            take_ab(0)
            for j in range(16):
                if j + 1 < 16:
                    take_ab(j + 1)
                g, tok = j // 2, slice((j % 2) * SEQ, (j % 2 + 1) * SEQ)
                dve.wait_ge(f_hi_ready, j + 1)
                dve.tensor_tensor(u_lo[:, g, tok], ps[:, j % 2, 0:SEQ], u_hi[:, g, tok].bitcast(f32),
                                  ALU.subtract).then_inc(f_lo_ready, 1)

        LG = {n: lgam[:, 8 * i:8 * i + 8] for i, n in
              enumerate("neg_abs e den s s2 r log1p lg".split())}

        def rope_tile(j):
            return rq[:, j, 0:SEQ] if j < DT else rk[:, j - DT, 0:SEQ]

        def ret_view(tensor):
            return tensor[:, :, :].rearrange("p a (b n) -> p (a b) n", n=SEQ)

        def pe_retention(pe, t):
            if begun(t["pair"]):
                pe.wait_ge(banks01_read, t["pair"])
            if begun(t["pair"]):
                pe.wait_ge(banks23_read, t["pair"])
            pe.wait_ge(ret_landed, 16)
            for j in range(2 * DT):
                if begun(j - 1):
                    pe.wait_ge(roped, j - 1)
                pe.matmul(ps[:, 5 + j % 2, 0:SEQ], rswap, rope_tile(j), start=True, stop=True
                          ).then_inc(swapped, 1)

            def scores(hd):
                pe.wait_ge(roped, 2 * DT)
                if begun(hd):
                    pe.wait_ge(weighted_ready, hd)
                for kb in range(4):
                    for i in range(2):
                        ins = pe.matmul(ps[:, 5 + kb // 2, (kb % 2) * SEQ:(kb % 2 + 1) * SEQ],
                                        rk[:, 2 * hd + i, kb * P:(kb + 1) * P], rq[:, 2 * hd + i, :],
                                        start=i == 0, stop=i == 1)
                ins.then_inc(scores_ready, 1)

            scores(0)
            for hd in range(RET_HEADS):
                pe.wait_ge(weighted_ready, hd + 1)
                if begun(hd):
                    pe.wait_ge(head_out_copied, hd)
                for dv in range(4):
                    for kb in range(4):
                        at = hd * RET_DV + dv * P
                        ins = pe.matmul(ps[:, dv // 2, (dv % 2) * SEQ:(dv % 2 + 1) * SEQ], rv[:, kb, at:at + P],
                                        weighted[:, kb, :], start=kb == 0, stop=kb == 3)
                ins.then_inc(head_out_ready, 1)
                if hd + 1 < RET_HEADS:
                    scores(hd + 1)
                for i in range(2):
                    pe.wait_ge(head_sums_ready, 2 * hd + i + 1)
                    pe.matmul(ps[:, STAT, 0:SEQ], ones[:, :], acc[:, 0:SEQ], start=True, stop=True
                              ).then_inc(head_stat_ready, 1)

        def act_retention(act, t):
            act.wait_ge(vec_landed, 16)
            act.wait_ge(decay_abs_ready, 1)
            act.activation(LG["e"], LG["neg_abs"], ACT.Exp).then_inc(decay_exp_ready, 1)
            act.wait_ge(log_gamma_ready, 1)
            act.wait_ge(ret_landed, 16)
            for hd in range(RET_HEADS):
                act.wait_ge(exponents_ready, hd + 1)
                act.activation(decay[:, 0:2, :], decay[:, 0:2, :], ACT.Exp)
                act.activation(decay[:, 2:4, :], rdelta, ACT.Exp, scale=lgam[:, 56 + hd:57 + hd],
                               bias=lgam[:, 40 + hd:41 + hd])
                act.activation(rt[:, 2:4, :], rdelta, ACT.Exp, scale=lgam[:, 36 + hd:37 + hd],
                               bias=lgam[:, 44 + hd:45 + hd]).then_inc(decays_ready, 1)
                act.wait_ge(head_out_ready, hd + 1)
                if begun(hd):
                    act.wait_ge(mix_lo_ready, hd)
                act.activation(ro, ps[:, 0:2, :].rearrange("p a (b n) -> p (a b) n", b=2), ACT.Copy
                               ).then_inc(head_out_copied, 1)
                act.wait_ge(centred_ready, hd + 1)
                act.activation(rt, ro, ACT.Square).then_inc(head_squares_ready, 1)
                if begun(2 * hd + 2):
                    act.wait_ge(head_stat_ready, 2 * hd + 2)
                act.activation(rstd[:, 0:SEQ], ps[:, STAT, 0:SEQ], ACT.Sqrt, scale=1.0 / RET_DV, bias=eps[:, 0:1]
                               ).then_inc(head_root_ready, 1)
                act.wait_ge(gated_ready, hd + 1)
                act.activation(ret_view(u_hi)[:, 4 * hd:4 * hd + 4, :], ro, ACT.Copy
                               ).then_inc(mix_hi_ready, 1)

        def dve_retention(dve, t, order):
            x = vecs("decay", 0, 8)
            dve.scalar_tensor_tensor(LG["neg_abs"], x, -1.0, x, ALU.mult, ALU.min
                                     ).then_inc(decay_abs_ready, 1)
            dve.wait_ge(decay_exp_ready, 1)
            log1p(dve, order, LG["e"], LG["den"], LG["s"], LG["s2"], LG["r"], LG["log1p"])
            order.link(dve.scalar_tensor_tensor(LG["lg"], x, 0.0, LG["log1p"], ALU.min, ALU.subtract))
            order.link(dve.tensor_scalar(lgam[:, 32:40], LG["lg"], -1.0, None, ALU.mult))
            dve.tensor_scalar(lgam[:, 40:48], LG["lg"], float(SEQ), None, ALU.mult
                              ).then_inc(log_gamma_ready, 1)
            dve.wait_ge(ret_landed, 16)
            for j in range(2 * DT):
                dve.wait_ge(swapped, j + 1)
                part = tmp2[:, j % 2, 0:SEQ]
                if begun(j - 1):
                    dve.wait_ge(roped, j - 1)
                dve.tensor_tensor(part, ps[:, 5 + j % 2, 0:SEQ], rsin[:, j % 2, :], ALU.mult)
                order.link(dve.tensor_tensor(rope_tile(j), rope_tile(j), rcos[:, j % 2, :], ALU.mult))
                dve.tensor_tensor(rope_tile(j), rope_tile(j), part, ALU.add).then_inc(roped, 1)
            for hd in range(RET_HEADS):
                dve.tensor_scalar(decay[:, 0:2, :], rdelta, 0.0, lgam[:, 56 + hd:57 + hd], ALU.max, ALU.mult)
                order.link(dve.tensor_scalar(rt[:, 0:2, :], rdelta, 0.0, lgam[:, 36 + hd:37 + hd], ALU.min,
                                             ALU.mult))
                dve.tensor_tensor(decay[:, 0:2, :], decay[:, 0:2, :], rt[:, 0:2, :], ALU.add
                                  ).then_inc(exponents_ready, 1)
                dve.wait_ge(decays_ready, hd + 1)
                order.link(dve.tensor_tensor(decay[:, 2:4, :], decay[:, 2:4, :], rt[:, 2:4, :], ALU.add))
                dve.wait_ge(scores_ready, hd + 1)
                dve.scalar_tensor_tensor(weighted[:, :, :], ps[:, 5:7, :].rearrange("p a (b n) -> p (a b) n", b=2),
                                         RET_DK ** -0.5, decay[:, :, :], ALU.mult, ALU.mult
                                         ).then_inc(weighted_ready, 1)
                dve.wait_ge(head_out_copied, hd + 1)
                dve.tensor_reduce(acc[:, 0:SEQ], ro.rearrange("p t n -> p n t"), AX, ALU.add
                                  ).then_inc(head_sums_ready, 1)
                dve.wait_ge(head_stat_ready, 2 * hd + 1)
                mean = ps[:, STAT, 0:SEQ].unsqueeze(1).to_broadcast([P, 4, SEQ])
                dve.scalar_tensor_tensor(ro, mean, -1.0 / RET_DV, ro, ALU.mult, ALU.add
                                         ).then_inc(centred_ready, 1)
                dve.wait_ge(head_squares_ready, hd + 1)
                dve.tensor_reduce(acc[:, 0:SEQ], rt.rearrange("p t n -> p n t"), AX, ALU.add
                                  ).then_inc(head_sums_ready, 1)
                dve.wait_ge(head_root_ready, hd + 1)
                order.link(dve.reciprocal(rstd[:, 0:SEQ], rstd[:, 0:SEQ]))
                inv = rstd[:, 0:SEQ].unsqueeze(1).to_broadcast([P, 4, SEQ])
                order.link(dve.tensor_tensor(ro, ro, inv, ALU.mult))
                dve.tensor_tensor(ro, ro, rg[:, 4 * hd:4 * hd + 4, :], ALU.mult
                                  ).then_inc(gated_ready, 1)
                dve.wait_ge(mix_hi_ready, hd + 1)
                four = slice(4 * hd, 4 * hd + 4)
                dve.tensor_tensor(ret_view(u_lo)[:, four, :], ro, ret_view(u_hi)[:, four, :].bitcast(f32),
                                  ALU.subtract).then_inc(mix_lo_ready, 1)

        HD2 = SSD_INNER // SSD_HEADS

        def head_y(hd):
            return ps[(hd % 2) * HD2:(hd % 2 + 1) * HD2, hd // 4, ((hd // 2) % 2) * SEQ:((hd // 2) % 2 + 1) * SEQ]

        def pe_mixer(pe, t, l):
            if begun(t["pair"]):
                pe.wait_ge(banks01_read, t["pair"])
            if begun(t["pair"]):
                pe.wait_ge(banks23_read, t["pair"])
            pe.wait_ge(tables_landed, 16)
            pe.wait_ge(dtw_lo_ready, l + 1)
            for tb in range(2):
                for k in range(DT):
                    tok = slice(tb * P, (tb + 1) * P)
                    for n, (a, w) in enumerate(((u_hi, dtw_hi), (u_hi, dtw_lo), (u_lo, dtw_hi))):
                        ins = pe.matmul(ps[:, 5, tb * 8:tb * 8 + 8], a[:, k, tok], w[:, k * 8:k * 8 + 8],
                                        start=k == 0 and n == 0, stop=k == DT - 1 and n == 2)
            ins.then_inc(dt_ready, 1)
            for i in range(4):
                ins = pe.matmul(ps[:, 6 + i // 2, (i % 2) * SEQ:(i % 2 + 1) * SEQ], tab["swap"], qk[:, i, :],
                                start=True, stop=True)
            ins.then_inc(qk_swapped, 1)
            for g in range(POOL_GROUPS):
                out = ps[(g % 2) * 64:(g % 2 + 1) * 64, 0, (g // 2) * SEQ:(g // 2 + 1) * SEQ]
                for tb in range(2):
                    ins = pe.matmul(out, pool_u[:, tb, g * 64:(g + 1) * 64], band[:, tb, g, :], start=tb == 0,
                                    stop=tb == 1)
            ins.then_inc(pool_mean_ready, 1)
            pe.wait_ge(conv_ready, l + 1)
            for g in range(SSD_GROUPS):
                for sbk in range(2):
                    ins = pe.matmul(ps[:, 2 + g, sbk * SEQ:(sbk + 1) * SEQ], cx[:, 4 + g, sbk * P:(sbk + 1) * P],
                                    cx[:, 6 + g, :], start=True, stop=True)
            ins.then_inc(cb_ready, 1)
            pe.wait_ge(pool_mean_copied, l + 1)
            pe.wait_ge(poolw_landed, 64 * (l + 1))
            for j in range(2):
                ins = pe.matmul(ps[:, 1, j * SEQ:(j + 1) * SEQ], poolw[:, j, :], mixf[:, 6 + j, :], start=True,
                                stop=True)
            ins.then_inc(pool_out_ready, 1)
            pe.wait_ge(dt_taken, l + 1)
            for tb in range(2):
                for j in range(4):
                    ins = pe.matmul(ps[:, 4 + tb, j * P:(j + 1) * P], cx[:, j, tb * P:(tb + 1) * P], tab["ident"],
                                    start=True, stop=True)
            ins.then_inc(xtok_ready, 1)
            pe.wait_ge(da_ready, l + 1)
            pe.wait_ge(qk_roped, l + 1)
            for tb in range(2):
                for sbk in range(tb + 1):
                    ins = pe.matmul(ps[:, 6, tb * 8:tb * 8 + 8], tri[:, sbk, tb * P:(tb + 1) * P],
                                    sm("da")[:, sbk, :], start=sbk == 0, stop=sbk == tb)
            ins.then_inc(acs_ready, 1)

            def ssd_sums(hd):
                if hd == 0:
                    pe.wait_ge(acs_taken, l + 1)
                if hd >= 2:
                    if begun(l * SSD_HEADS + hd - 1):
                        pe.wait_ge(segment_taken, l * SSD_HEADS + hd - 1)
                for sbk in range(2):
                    ins = pe.matmul(ps[:, 6 + hd % 2, 0:SEQ], sm("da")[:, sbk, hd:hd + 1].to_broadcast([P, P]),
                                    tri[:, sbk, :], start=sbk == 0, stop=sbk == 1)
                ins.then_inc(head_acs_ready, 1)

            def ssd_out(hd):
                pe.wait_ge(segment_ready, l * SSD_HEADS + hd + 1)
                if hd == 0:
                    pe.wait_ge(xtok_copied, l + 1)
                    pe.wait_ge(pool_out_taken, l + 1)
                for sbk in range(2):
                    ins = pe.matmul(head_y(hd), xtok[:, sbk, hd * HD2:(hd + 1) * HD2], seg[:, hd % 2, sbk, :],
                                    start=sbk == 0, stop=sbk == 1)
                ins.then_inc(head_y_ready, 1)

            def att_scores(a):
                r = slice((a % 2) * ATTN_DH, (a % 2 + 1) * ATTN_DH)
                if a == 0:
                    pe.wait_ge(cb_taken, l + 1)
                if a >= 2:
                    if begun(l * ATTN_HEADS + a - 1):
                        pe.wait_ge(att_masked, l * ATTN_HEADS + a - 1)
                for nb in range(2):
                    ins = pe.matmul(ps[:, 2 + a % 2, nb * SEQ:(nb + 1) * SEQ], qk[r, a // 2, nb * P:(nb + 1) * P],
                                    qk[r, 2 + a // 2, :], start=True, stop=True)
                ins.then_inc(att_scores_ready, 1)

            def att_out(a):
                pe.wait_ge(probs_ready, l * ATTN_HEADS + a + 1)
                if a == 0:
                    pe.wait_ge(xtok_copied, l + 1)
                for nb in range(2):
                    for mb in range(2):
                        at = mb * SEQ + nb * P
                        ins = pe.matmul(ps[:, 4, at:at + P], probs[:, nb, mb * P:(mb + 1) * P], tab["ident"],
                                        start=True, stop=True)
                ins.then_inc(probs_turned, 1)
                pe.wait_ge(probs_t_copied, l * ATTN_HEADS + a + 1)
                for mb in range(2):
                    out = ps[(a % 2) * 64:(a % 2 + 1) * 64, 5, (a // 2) * SEQ:(a // 2 + 1) * SEQ]
                    ins = pe.matmul(out, att_v[:, mb, a * 64:(a + 1) * 64], probs_t[:, mb, :], start=mb == 0,
                                    stop=mb == 1)
                ins.then_inc(att_out_ready, 1)

            for x in range(4):
                ssd_sums(2 * x)
                ssd_sums(2 * x + 1)
                att_scores(x)
                ssd_out(2 * x)
                ssd_out(2 * x + 1)
                att_out(x)
            pe.wait_ge(ssd_sums_ready, l + 1)
            pe.matmul(ps[:, 6, 0:SEQ], ones[:, :], acc[:, 0:SEQ], start=True, stop=True
                      ).then_inc(ssd_stat_ready, 1)

        def act_mixer(act, t, l):
            act.wait_ge(dtw_landed, 16 * (l + 1))
            act.activation(dtw_hi[:, :], dtw[:, :], ACT.Copy).then_inc(dtw_hi_ready, 1)
            for j in range(8):
                act.wait_ge(conv_sum_ready, 8 * l + j + 1)
                ins = act.activation(cx[:, j, :], cx[:, j, :], ACT.Silu, bias=lv("conv_b", j))
            ins.then_inc(conv_ready, 1)
            act.wait_ge(pool_mean_ready, l + 1)
            act.activation(mixf[:, 6:8, :], ps[:, 0, :].rearrange("p (b n) -> p b n", b=2), ACT.Copy
                           ).then_inc(pool_mean_copied, 1)
            act.wait_ge(dt_taken, l + 1)
            act.activation(sm("e_dt"), sm("neg_abs"), ACT.Exp)
            act.activation(sm("neg_a")[:, 0, :], lv("a_log", 0, 8), ACT.Exp).then_inc(dt_exp_ready, 1)
            act.wait_ge(xtok_ready, l + 1)
            act.activation(xtok[:, :, :], ps[:, 4:6, :], ACT.Copy).then_inc(xtok_copied, 1)
            act.wait_ge(pool_out_taken, l + 1)
            act.activation(u_hi[:, 4:6, 0:SEQ], mixf[:, 4:6, :], ACT.Copy).then_inc(mix_hi_ready, 1)
            for x in range(4):
                for hd in (2 * x, 2 * x + 1):
                    act.wait_ge(segment_taken, l * SSD_HEADS + hd + 1)
                    act.activation(seg[:, hd % 2, :, :], seg[:, hd % 2, :, :], ACT.Exp
                                   ).then_inc(segment_exp_ready, 1)
                act.wait_ge(max_ready, l * ATTN_HEADS + x + 1)
                for nb in range(2):
                    ins = act.activation(probs[:, nb, :], probs[:, nb, :], ACT.Exp, bias=sm("neg_mx")[:, 0, nb:nb + 1],
                                         accum_out=sm("sums")[:, 0, nb:nb + 1])
                ins.then_inc(probs_exp_ready, 1)
                act.wait_ge(probs_turned, l * ATTN_HEADS + x + 1)
                act.activation(probs_t[:, :, :], ps[:, 4, :].rearrange("p (b n) -> p b n", b=2), ACT.Copy
                               ).then_inc(probs_t_copied, 1)
            act.wait_ge(att_out_ready, (l + 1) * ATTN_HEADS)
            act.activation(mixf[:, 6:8, :], ps[:, 5, :].rearrange("p (b n) -> p b n", b=2), ACT.Copy
                           ).then_inc(att_copied, 1)
            act.activation(u_hi[:, 6:8, 0:SEQ], ps[:, 5, :].rearrange("p (b n) -> p b n", b=2), ACT.Copy
                           ).then_inc(mix_hi_ready, 1)
            squares = xtok[:, :, :].rearrange("p a (b n) -> p (a b) n", b=2)
            act.wait_ge(y_gated, l + 1)
            act.activation(squares, mixf[:, 0:4, :], ACT.Square).then_inc(ssd_squares_ready, 1)
            act.wait_ge(ssd_stat_ready, l + 1)
            act.activation(rstd[:, 0:SEQ], ps[:, 6, 0:SEQ], ACT.Sqrt, scale=1.0 / SSD_INNER, bias=eps[:, 0:1]
                           ).then_inc(ssd_root_ready, 1)
            act.wait_ge(y_normed, l + 1)
            act.activation(u_hi[:, 0:4, 0:SEQ], mixf[:, 0:4, :], ACT.Copy).then_inc(mix_hi_ready, 1)

        def dve_mixer(dve, t, l, order):
            dve.wait_ge(dtw_hi_ready, l + 1)
            dve.tensor_tensor(dtw_lo[:, :], dtw[:, :], dtw_hi[:, :].bitcast(f32), ALU.subtract
                              ).then_inc(dtw_lo_ready, 1)
            if begun(t["pair"]):
                dve.wait_ge(banks01_read, t["pair"])
            if begun(t["pair"]):
                dve.wait_ge(banks23_read, t["pair"])
            order.link(dve.memset(xpad[:, :, 0:3], 0.0))
            for i in range(4):
                for j in range(8):
                    w = lv("conv_w", 4 * j + i)
                    if i == 0:
                        ins = dve.tensor_scalar(cx[:, j, :], xpad[:, j, 0:SEQ], w, None, ALU.mult)
                    else:
                        ins = dve.scalar_tensor_tensor(cx[:, j, :], xpad[:, j, i:i + SEQ], w, cx[:, j, :], ALU.mult,
                                                       ALU.add)
                    if i == 3:
                        ins.then_inc(conv_sum_ready, 1)
                    elif j == 7:
                        order.link(ins)
            dve.wait_ge(dt_ready, l + 1)
            heads = lambda name: lv(name, 0, 8).unsqueeze(1).to_broadcast([P, 2, 8])
            order.link(dve.tensor_tensor(sm("dt_in"), ps[:, 5, 0:16].rearrange("p (b n) -> p b n", b=2),
                                         heads("dt_bias"), ALU.add))
            dve.scalar_tensor_tensor(sm("neg_abs"), sm("dt_in"), -1.0, sm("dt_in"), ALU.mult, ALU.min
                                     ).then_inc(dt_taken, 1)
            dve.wait_ge(dt_exp_ready, l + 1)
            log1p(dve, order, sm("e_dt"), sm("s_den"), sm("s_dt"), sm("s2"), sm("series"), sm("log1p"))
            order.link(dve.scalar_tensor_tensor(sm("dt"), sm("dt_in"), 0.0, sm("log1p"), ALU.max, ALU.add))
            dve.scalar_tensor_tensor(sm("da"), sm("dt"), -1.0, sm("neg_a")[:, 0:1, :].to_broadcast([P, 2, 8]),
                                     ALU.mult, ALU.mult).then_inc(da_ready, 1)
            dve.wait_ge(tables_landed, 16)
            dve.wait_ge(qk_swapped, l + 1)
            both = lambda name: tab[name].unsqueeze(1).to_broadcast([P, 2, SEQ])
            for i in range(2):
                part = tmp2[:, i, :].rearrange("p (b n) -> p b n", b=2)
                dve.tensor_tensor(part, ps[:, 6 + i, :].rearrange("p (b n) -> p b n", b=2), both("sin"), ALU.mult)
                order.link(dve.tensor_tensor(qk[:, 2 * i:2 * i + 2, :], qk[:, 2 * i:2 * i + 2, :], both("cos"),
                                             ALU.mult))
                ins = dve.tensor_tensor(qk[:, 2 * i:2 * i + 2, :], qk[:, 2 * i:2 * i + 2, :], part, ALU.add)
            ins.then_inc(qk_roped, 1)
            dve.wait_ge(cb_ready, l + 1)
            for g in range(SSD_GROUPS):
                ins = dve.tensor_tensor(cb[:, 2 * g:2 * g + 2, :], ps[:, 2 + g, :].rearrange("p (b n) -> p b n", b=2),
                                        tri, ALU.mult)
            ins.then_inc(cb_taken, 1)
            dve.wait_ge(pool_out_ready, l + 1)
            for j in range(2):
                ins = dve.tensor_scalar(mixf[:, 4 + j, :], ps[:, 1, j * SEQ:(j + 1) * SEQ], lv("pool_scale", j), None,
                                        ALU.mult)
            ins.then_inc(pool_out_taken, 1)

            def split(a, b, n):
                dve.wait_ge(mix_hi_ready, RET_HEADS + 3 * l + n)
                dve.tensor_tensor(u_lo[:, a:b, 0:SEQ], mixf[:, a:b, :], u_hi[:, a:b, 0:SEQ].bitcast(f32),
                                  ALU.subtract).then_inc(mix_lo_ready, 1)
            split(4, 6, 1)
            dve.wait_ge(acs_ready, l + 1)
            dve.tensor_copy(sm("acs"), ps[:, 6, 0:16].rearrange("p (b n) -> p b n", b=2)
                            ).then_inc(acs_taken, 1)
            dve.wait_ge(acs_taken, l + 1)
            for x in range(4):
                for hd in (2 * x, 2 * x + 1):
                    dve.wait_ge(head_acs_ready, l * SSD_HEADS + hd + 1)
                    if hd >= 2:
                        if begun(l * SSD_HEADS + hd - 1):
                            dve.wait_ge(head_y_ready, l * SSD_HEADS + hd - 1)
                    for sbk in range(2):
                        ins = dve.tensor_scalar(seg[:, hd % 2, sbk, :], ps[:, 6 + hd % 2, 0:SEQ],
                                                sm("acs")[:, sbk, hd:hd + 1], 0.0, ALU.subtract, ALU.min)
                    ins.then_inc(segment_taken, 1)
                dve.wait_ge(att_scores_ready, l * ATTN_HEADS + x + 1)
                dve.scalar_tensor_tensor(probs[:, :, :], ps[:, 2 + x % 2, :].rearrange("p (b n) -> p b n", b=2),
                                         ATTN_DH ** -0.5, mask, ALU.mult, ALU.add
                                         ).then_inc(att_masked, 1)
                dve.wait_ge(att_masked, l * ATTN_HEADS + x + 1)
                dve.tensor_reduce(sm("neg_mx")[:, 0, 0:2], probs[:, :, :], AX, ALU.max, negate=True
                                  ).then_inc(max_ready, 1)
                for hd in (2 * x, 2 * x + 1):
                    dve.wait_ge(segment_exp_ready, l * SSD_HEADS + hd + 1)
                    for sbk in range(2):
                        ins = dve.scalar_tensor_tensor(seg[:, hd % 2, sbk, :], seg[:, hd % 2, sbk, :],
                                                       sm("dt")[:, sbk, hd:hd + 1], cb[:, 2 * (hd // 4) + sbk, :],
                                                       ALU.mult, ALU.mult)
                    ins.then_inc(segment_ready, 1)
                dve.wait_ge(probs_exp_ready, l * ATTN_HEADS + x + 1)
                order.link(dve.reciprocal(sm("inv")[:, 0, 0:2], sm("sums")[:, 0, 0:2]))
                for nb in range(2):
                    ins = dve.tensor_scalar(probs[:, nb, :], probs[:, nb, :], sm("inv")[:, 0, nb:nb + 1], None,
                                            ALU.mult)
                ins.then_inc(probs_ready, 1)
                dve.wait_ge(probs_turned, l * ATTN_HEADS + x + 1)
            dve.wait_ge(att_copied, l + 1)
            split(6, 8, 2)
            dve.wait_ge(head_y_ready, (l + 1) * SSD_HEADS)
            for j in range(4):
                ins = dve.scalar_tensor_tensor(mixf[:, j, :], cx[:, j, :], lv("d_skip", j),
                                               ps[:, j // 2, (j % 2) * SEQ:(j % 2 + 1) * SEQ], ALU.mult, ALU.add)
            order.link(ins)
            dve.tensor_tensor(mixf[:, 0:4, :], mixf[:, 0:4, :], zs[:, :, :], ALU.mult
                              ).then_inc(y_gated, 1)
            dve.wait_ge(ssd_squares_ready, l + 1)
            dve.tensor_reduce(acc[:, 0:SEQ], xtok[:, :, :].rearrange("p a (b n) -> p n (a b)", b=2), AX, ALU.add
                              ).then_inc(ssd_sums_ready, 1)
            dve.wait_ge(ssd_root_ready, l + 1)
            order.link(dve.reciprocal(rstd[:, 0:SEQ], rstd[:, 0:SEQ]))
            order.link(dve.tensor_tensor(mixf[:, 0:4, :], mixf[:, 0:4, :],
                                         rstd[:, 0:SEQ].unsqueeze(1).to_broadcast([P, 4, SEQ]), ALU.mult))
            for j in range(4):
                ins = dve.tensor_scalar(mixf[:, j, :], mixf[:, j, :], lv("ssd_norm", j), None, ALU.mult)
            ins.then_inc(y_normed, 1)
            split(0, 4, 3)

        first, ORDER_DVE = block1(), 31
        block = ctx.enter_context(nc.Block())

        @block.sync
        def _(sp):
            t = Tally()
            sp.dma_start(h[:, :, :], rows(T["xT"])).then_inc(x_landed, 16)
            for g in first:
                if isinstance(g, Gemm):
                    sp_gemm(sp, g, t)
                t.add(g)
            with sp.Fori(0, LAYERS2) as l:
                stages = block2(l)
                t.enter(l, stages)
                for g in stages:
                    if isinstance(g, Gemm):
                        sp_gemm(sp, g, t)
                    t.add(g)
            t.leave(LAYERS2)
            if begun(t["post"]):
                sp.wait_ge(post_ready, t["post"])
            sp.dma_start(rows(T["outT"]), h[:, :, 0:SEQ]).then_inc(out_landed, 16)
            sp.wait_ge(out_landed, 16)

        @block.gpsimd
        def _(pool):
            pool.memset(ones[:, :], 1.0)
            pool.memset(eps[:, 0:1], EPS)
            pool.memset(eps[:, 1:2], 4.0 * EPS)
            pool.memset(cond_hi[:, :, :].bitcast(f32), 0.0).then_inc(setup_ready, 1)

        @block.scalar
        def _(act):
            act.dma_start(cond[:, :, :], T["cond"]).then_inc(cond_landed, 16)
            act.dma_start(vec[:, :], T["vec"]).then_inc(vec_landed, 16)
            act.dma_start(sel[:, :], T["sel"]).then_inc(sel_landed, 16)
            act.wait_ge(cond_landed, 16)
            act.wait_ge(setup_ready, 1)
            act.activation(cond[:, :, :], cond[:, :, :], ACT.Silu).then_inc(cond_silu_ready, 1)
            act.wait_ge(cond_silu_ready, 1)
            act.activation(cond_hi[:, :, 0:4:2], cond[:, :, :], ACT.Copy).then_inc(cond_ready, 1)
            t = Tally()
            gemm0 = follower(first, -1)
            for u in range(RING):
                split_hi(act, gemm0, {"unit": 0, "unit_div": 0}, 0, u)
            for j, g in enumerate(first):
                if isinstance(g, Gemm):
                    stream(act, g, t, follower(first, j), split_hi, act_evacuate)
                elif g.kind == "stats":
                    act_stats(act, g, t)
                elif g.kind == "coef" and g.more["piece"] == 1:
                    act.wait_ge(modcol_ready, t["modcol"] + 1)
                    if g.more["layer"] == 0:
                        act.dma_start(dft[:, :, :], T["dft"]).then_inc(dft_landed, 16)
                    else:
                        act.dma_start(rtab[:, :], T["ret_tables"]).then_inc(ret_landed, 16)
                elif g.kind == "apply":
                    act_apply(act, g, t)
                elif g.kind == "fourier":
                    act_fourier(act, t)
                elif g.kind == "retention":
                    act_retention(act, t)
                elif g.kind == "final":
                    act.dma_start(tables[:, :], T["tables2"]).then_inc(tables_landed, 16)
                t.add(g)
            with act.Fori(0, LAYERS2) as l:
                stages = block2(l)
                t.enter(l, stages)
                if begun(t["post"]):
                    act.wait_ge(post_ready, t["post"])
                act.wait_ge(poolw_zeroed, 1)
                act.dma_start(lvec[:, :], T["layer_vec"][l]).then_inc(lvec_landed, 16)
                for g in range(POOL_GROUPS):
                    r = slice((g % 2) * 64, (g % 2 + 1) * 64)
                    act.dma_start(poolw[r, g // 2, r], T["pool_w_2"][l, g]).then_inc(poolw_landed, 16)
                act.dma_start(dtw[:, :].rearrange("p (k n) -> p k n", n=8),
                              rows(T["w_in_2"][l])[:, :, 1536:1544]).then_inc(dtw_landed, 16)
                for u in range(RING):
                    split_hi(act, follower(stages, -1), t, 0, u)
                act.wait_ge(lvec_landed, 16 * (l + 1))
                for j, g in enumerate(stages):
                    if isinstance(g, Gemm):
                        stream(act, g, t, follower(stages, j), split_hi, act_evacuate)
                    elif g.kind == "stats":
                        act_stats(act, g, t)
                    elif g.kind == "apply":
                        act_apply(act, g, t)
                    elif g.kind == "mixer":
                        act_mixer(act, t, l)
                    t.add(g)

        @block.vector
        def _(dve):
            order = Order(dve, dve_order)
            t = Tally()
            dve.wait_ge(vec_landed, 16)
            dve.wait_ge(cond_ready, 1)
            dve.tensor_tensor(cond_hi[:, :, 1:4:2], cond[:, :, :], cond_hi[:, :, 0:4:2].bitcast(f32), ALU.subtract
                              ).then_inc(cond_lo_ready, 1)
            for u in range(RING):
                split_lo(dve, follower(first, -1), {"unit": 0, "unit_div": 0}, 0, u)
            for j, g in enumerate(first):
                if isinstance(g, Gemm):
                    stream(dve, g, t, follower(first, j), split_lo, dve_evacuate)
                elif g.kind == "stats":
                    dve_stats(dve, g, t)
                elif g.kind == "coef":
                    dve_coef(dve, g, t, order)
                elif g.kind == "apply":
                    dve_apply(dve, g, t)
                elif g.kind == "fourier":
                    dve_fourier(dve, t)
                elif g.kind == "retention":
                    dve_retention(dve, t, order)
                elif g.kind == "final":
                    if begun(t["stat"]):
                        dve.wait_ge(rstd_ready, t["stat"])
                    for k in range(DT):
                        if begun(k - 1):
                            dve.wait_ge(post_ready, k - 1)
                        order.link(dve.tensor_tensor(tmp2[:, k % 2, 0:SEQ], h[:, k, 0:SEQ], rstd[:, 0:SEQ], ALU.mult))
                        dve.tensor_scalar(h[:, k, 0:SEQ], tmp2[:, k % 2, 0:SEQ], vecs("final_g", k), None, ALU.mult
                                          ).then_inc(post_ready, 1)
                    dve.memset(poolw[:, :, :], 0.0).then_inc(poolw_zeroed, 1)
                t.add(g)
            with dve.Fori(0, LAYERS2) as l:
                stages = block2(l)
                t.enter(l, stages)
                order.enter(l, ORDER_DVE)
                for u in range(RING):
                    split_lo(dve, follower(stages, -1), t, 0, u)
                dve.wait_ge(lvec_landed, 16 * (l + 1))
                for j, g in enumerate(stages):
                    if isinstance(g, Gemm):
                        stream(dve, g, t, follower(stages, j), split_lo, dve_evacuate)
                    elif g.kind == "stats":
                        dve_stats(dve, g, t)
                    elif g.kind == "apply":
                        dve_apply(dve, g, t)
                    elif g.kind == "post":
                        dve_post(dve, g, t)
                    elif g.kind == "mixer":
                        dve_mixer(dve, t, l, order)
                    t.add(g)
                order.leave(LAYERS2)

        @block.tensor
        def _(pe):
            t = Tally()
            pe.wait_ge(setup_ready, 1)
            pe.wait_ge(sel_landed, 16)
            pe.wait_ge(cond_lo_ready, 1)
            for g in first:
                if isinstance(g, Gemm):
                    pe_gemm(pe, g, t)
                elif g.kind == "stats":
                    pe_stats(pe, g, t)
                elif g.kind == "coef":
                    pe_coef(pe, g, t)
                elif g.kind == "fourier":
                    pe_fourier(pe, t)
                elif g.kind == "retention":
                    pe_retention(pe, t)
                t.add(g)
            with pe.Fori(0, LAYERS2) as l:
                stages = block2(l)
                t.enter(l, stages)
                for g in stages:
                    if isinstance(g, Gemm):
                        pe_gemm(pe, g, t)
                    elif g.kind == "stats":
                        pe_stats(pe, g, t)
                    elif g.kind == "mixer":
                        pe_mixer(pe, t, l)
                    t.add(g)


def kernel(**inputs):
    import numpy as _np
    import concourse.bacc as _bacc
    from concourse import mybir as _mybir
    from concourse.bass_utils import run_bass_kernel_spmd as _run

    a = {k: _np.asarray(v) for k, v in inputs.items()}

    def tiles(v):
        return v.reshape(-1, P).T

    vec = [tiles(a["b_mod"]), tiles(a["norm_g"]), tiles(a["final_norm_g"]),
           _np.broadcast_to(a["ret_decay_logit"].reshape(1, 8), (P, 8))]
    layers = []
    for l in range(LAYERS2):
        conv = a["conv_w_2"][l].reshape(4, 8, P).transpose(2, 1, 0).reshape(P, 32)
        layers.append(_np.concatenate(
            [tiles(a[n][l]) for n in ("ff1_norm_pre_2", "ff1_norm_post_2", "mix_norm_pre_2", "mix_norm_post_2",
                                      "ff2_norm_pre_2", "ff2_norm_post_2")]
            + [conv, tiles(a["conv_b_2"][l]), tiles(a["ssd_norm_2"][l]), tiles(a["pool_scale_2"][l]),
               tiles(_np.repeat(a["d_skip_2"][l], SSD_INNER // SSD_HEADS)),
               _np.broadcast_to(a["dt_bias_2"][l][None], (P, 8)),
               _np.broadcast_to(a["a_log_2"][l][None], (P, 8))], axis=1))
    dft, sel, ret_tables, tables2 = host_tables()
    arrays = {
        "xT": _np.concatenate([a["x"][0].T, a["ctx"][0].T], axis=1),
        "cond": _np.stack([a["c"][0].reshape(DT, P).T, a["c_ctx"].reshape(DT, P).T], axis=2),
        "vec": _np.concatenate(vec, axis=1), "layer_vec": _np.stack(layers),
        "dft": dft.reshape(P, 5, SEQ), "sel": sel, "ret_tables": ret_tables, "tables2": tables2,
    }
    for name in ("w_mod", "ffn_w_in", "ffn_w_out", "fnet_w_out", "ret_w_in", "ret_w_out", "ff1_w_gate_2",
                 "ff1_w_up_2", "ff1_w_down_2", "ff2_w_gate_2", "ff2_w_up_2", "ff2_w_down_2", "w_in_2", "pool_w_2",
                 "w_out_2"):
        arrays[name] = a[name]
    arrays = {k: _np.ascontiguousarray(v) for k, v in arrays.items()}
    nc = _bacc.Bacc("TRN2", target_bir_lowering=False, num_devices=1)
    f = _mybir.dt.float32
    T = {k: nc.dram_tensor("in_" + k, v.shape, f, kind="ExternalInput").ap() for k, v in arrays.items()}
    T["outT"] = nc.dram_tensor("outT", (D, SEQ), f, kind="ExternalOutput").ap()
    build(nc, T)
    r = _run(nc, [{"in_" + k: v for k, v in arrays.items()}], core_ids=[0])
    return _np.ascontiguousarray(r.results[0]["outT"].T).reshape(1, SEQ, D)
```

```python
import math
import numpy as np
import concourse.bass as bass
from concourse import mybir
from contextlib import ExitStack

P = 128
D = 1024
DT = D // P
SEQ = 256
NTOK = 2 * SEQ
DFF = 2816
FT = DFF // P
RING = 4
UCOLS = 256
KT_MAX = 4
EPS = 1e-6
RET_HEADS, RET_DK, RET_DV = 4, 256, 512
SSD_HEADS, SSD_INNER, SSD_GROUPS = 8, 512, 2
POOL_GROUPS = 4
ATTN_HEADS, ATTN_DH = 4, 64
LAYERS2 = 2
LOG1P_TERMS = [1.0 / (2 * k + 1) for k in range(10, 0, -1)]

VEC_FIELDS = [("b_mod", 144), ("norm_g", 48), ("final_g", 8), ("decay", 8)]
LAYER_FIELDS = [("pre1", 8), ("post1", 8), ("mix_pre", 8), ("mix_post", 8), ("pre2", 8), ("post2", 8),
                ("conv_w", 32), ("conv_b", 8), ("ssd_norm", 4), ("pool_scale", 2), ("d_skip", 4),
                ("dt_bias", 8), ("a_log", 8)]


def offsets(fields):
    at, out = 0, {}
    for name, n in fields:
        out[name] = at
        at += n
    return out, at


VEC_AT, VEC_N = offsets(VEC_FIELDS)
LAYER_AT, LAYER_N = offsets(LAYER_FIELDS)


class Gemm:

    def __init__(self, name, n, ks, src, tokens, mode="feature", act="u", evac=None, k_outer=False, riders=0,
                 rider_src=None, first=0, **more):
        self.name, self.n, self.ks, self.src, self.tokens = name, n, ks, src, tokens
        self.mode, self.act, self.evac, self.k_outer = mode, act, evac, k_outer
        self.riders, self.rider_src, self.first = riders, rider_src, first
        self.more, self.kind = more, "gemm"
        self.units = 2 * len(ks) + 2 * riders
        self.squares = evac in ("resid", "store")
        self.last_half_first = more.get("last_half_first", False)
        self.norm_after = more.get("norm_after", False)

    def order(self, it):
        starts = [sum(self.ks[:i]) for i in range(len(self.ks))]
        if self.last_half_first:
            starts.reverse()
        ride = [("rider", r, s, 4) for r in range(self.riders) for s in (0, 4)]
        if self.k_outer and isinstance(it, int) and it == 0:
            return [("main", p, s, k) for s, k in zip(starts, self.ks) for p in range(2)] + ride
        main = [("main", p, s, k) for p in range(2) for s, k in zip(starts, self.ks)]
        if not main or not ride:
            return main + ride
        assert len(main) == len(ride)
        return [unit for both in zip(main, ride) for unit in both]

    def closes(self, it, kind, pair):
        return 1 + max(u for u, (what, p, _, _) in enumerate(self.order(it)) if (what, p) == (kind, pair))

    def counts(self):
        out = {"unit": self.n * self.units, "unit_div": self.n * self.units // RING,
               "rider": self.n * self.riders}
        if self.ks:
            out["pair"] = self.n
        if self.evac == "swiglu":
            out["g"] = self.n
        if self.squares:
            out["sq"], out["sum"] = 4, 2
        if self.norm_after:
            out["stat"], out["normed"] = 1, self.n
        return out


class Stage:
    def __init__(self, kind, counts, **more):
        self.kind, self.c, self.more, self.name = kind, counts, more, kind

    def counts(self):
        return self.c


class Tally:

    def __init__(self):
        self.n = {}

    def __getitem__(self, k):
        return self.n.get(k, 0)

    def add(self, stage):
        for k, v in stage.counts().items():
            self.n[k] = self[k] + v

    def enter(self, layer, stages):
        self.start, self.per = dict(self.n), {}
        for s in stages:
            for k, v in s.counts().items():
                self.per[k] = self.per.get(k, 0) + v
        for k, v in self.per.items():
            self.n[k] = layer * v + self.start.get(k, 0)

    def leave(self, layers):
        self.n = dict(self.start)
        for k, v in self.per.items():
            self.n[k] = self[k] + layers * v


def loop(eng, a, b, body):
    if b - a == 1:
        body(a)
    elif b > a:
        with eng.Fori(a, b) as i:
            body(i)


def host_tables():
    f = np.float32
    w, n = np.arange(P), np.arange(SEQ)
    ang_w, ang_n = 2 * np.pi * np.outer(w, w) / P, 2 * np.pi * np.outer(n, n) / SEQ
    s = 1.0 / math.sqrt(SEQ * P)
    dft = np.zeros((P, 5, SEQ), f)
    dft[:, 0, :P], dft[:, 0, P:] = np.cos(ang_w) * s, np.sin(ang_w) * s
    for b in range(2):
        dft[:, 1 + b] = np.cos(ang_n)[b * P:(b + 1) * P]
        dft[:, 3 + b] = -np.sin(ang_n)[b * P:(b + 1) * P]

    ident = np.eye(P, dtype=f)
    grid_w, freqs = 64, RET_DK // 4
    inv = np.exp(-math.log(10000.0) * np.arange(freqs) / freqs)
    pos = np.stack([n // grid_w, n % grid_w])
    ang = inv[np.arange(P) % freqs][:, None, None] * pos[None]
    sign = np.where(np.arange(P) < freqs, -1.0, 1.0)[:, None, None]
    ret = np.zeros((P, 5 * SEQ * 1 + 2 * SEQ + P), f)
    ret[:, 0:512] = np.cos(ang).reshape(P, -1)
    ret[:, 512:1024] = (np.sin(ang) * sign).reshape(P, -1)
    delta = n[None, None, :] - (w[:, None, None] + P * np.arange(2)[None, :, None])
    ret[:, 1024:1536] = delta.reshape(P, -1)
    swap = np.zeros((P, P), f)
    swap[np.arange(P) ^ freqs, np.arange(P)] = 1.0
    ret[:, 1536:1664] = swap
    ret = ret[:, :1664]

    key = w[:, None] + P * np.arange(2)[None, :]
    tri = (key[:, :, None] <= n[None, None, :]).astype(f)
    band = np.zeros((P, 2, POOL_GROUPS, SEQ), f)
    for g in range(POOL_GROUPS):
        win = 2 ** (g + 1)
        inside = (key[:, :, None] <= n) & (key[:, :, None] > n - win)
        band[:, :, g] = inside / np.minimum(n + 1, win) - (key[:, :, None] == n)
    rd, theta = ATTN_DH // 4, 500000.0
    invf = theta ** (-np.arange(0, rd, 2) / rd)
    d = np.arange(P) % ATTN_DH
    a2 = np.where(d[:, None] < rd, invf[d % (rd // 2)][:, None] * n[None], 0.0)
    sg = np.where(d < rd // 2, -1.0, 1.0)[:, None]
    sw = np.zeros((P, P), f)
    partner = np.where(d < rd, np.arange(P) ^ (rd // 2), np.arange(P))
    sw[partner, np.arange(P)] = 1.0
    mask = np.where(n[None, None, :] <= key[:, :, None], 0.0, -1e30)
    two = np.concatenate([tri.reshape(P, -1), band.reshape(P, -1), np.cos(a2), np.sin(a2) * sg,
                          mask.reshape(P, -1), sw, ident], axis=1).astype(f)
    return dft.reshape(P, -1), ret, two


TWO_FIELDS = [("tri", 512), ("band", 2048), ("cos", 256), ("sin", 256), ("mask", 512), ("swap", 128),
              ("ident", 128)]
TWO_AT, TWO_N = offsets(TWO_FIELDS)


def build(nc, T):
    f32, f32r = mybir.dt.float32, mybir.dt.float32r
    ALU, ACT = mybir.AluOpType, mybir.ActivationFunctionType
    AX = mybir.AxisListType.X

    def rows(ap):
        return ap.rearrange("(k p) n -> p k n", p=P)

    def two_halves(w, second, first=0):
        return lambda it, pair, k0, kt: rows(w)[:, k0:k0 + kt,
                                                bass.ds((it + first) * UCOLS + pair * second, UCOLS)]

    def in_turn(w, first=0):
        return lambda it, pair, k0, kt: rows(w)[:, k0:k0 + kt, bass.ds(it * 2 * UCOLS + pair * UCOLS + first, UCOLS)]

    def stats(tokens, source, half=False):
        c = {"stat": 1} if source == "gemm" else {"stat": 1, "sq": 4, "sum": 2}
        return Stage("stats", c, tokens=tokens, source=source, half=half)

    def rider_cols(i, piece, tile=0):
        return in_turn(T["w_mod"][i], piece * 3 * D + tile * P)

    def coef_stage(i, piece, parts=(0, 24)):
        return Stage("coef", {"coef": 1}, layer=i, piece=piece, parts=parts)

    def block1():
        out = [Gemm("mod", 1, [], None, NTOK, riders=2, rider_src=rider_cols(0, 0), brings=(0, 0)),
               Stage("squares", {"sq": 4, "sum": 2}),
               Gemm("mod", 3, [], None, NTOK, riders=2, rider_src=rider_cols(0, 0, 4), brings=(0, 4)),
               stats(NTOK, "gemm"),
               coef_stage(0, 0, (0, 16))]
        for i in range(2):
            for piece in range(3):
                tokens = NTOK if i == 0 or piece < 2 else SEQ
                if (i, piece) != (0, 0):
                    out.append(stats(tokens, "gemm"))
                apply = Stage("apply", {"xr": DT, "uhi": DT, "ulo": DT}, tokens=tokens, mod=True, piece=piece)
                if (i, piece) != (0, 1):
                    out.append(apply)
                if piece != 1:
                    j = piece // 2
                    ahead = {(0, 0): [(0, 1), (0, 2)], (0, 2): [(1, 0)], (1, 0): [(1, 1), (1, 2)], (1, 2): []}[i, piece]
                    w, at = T["ffn_w_in"][i, j], 0
                    parts = [(6, rider_cols(*ahead[0]), coef_stage(*ahead[0]), (ahead[0][1], 0))] if ahead else []
                    if (i, piece) == (0, 0):
                        parts = [(2, rider_cols(0, 0, 16), coef_stage(0, 0, (16, 24)), (0, 16))] + parts
                    parts.append((FT // 2 - sum(p[0] for p in parts), None, None, None))
                    for n, src, after, brings in parts:
                        out.append(Gemm("up", n, [4, 4], two_halves(w, DFF, at), tokens, evac="swiglu",
                                        k_outer=at == 0, waits="ulo" if at == 0 else None, wide=True, first=at,
                                        riders=2 if src else 0, rider_src=src, brings=brings))
                        if after:
                            out.append(after)
                        at += n
                    more = dict(riders=6, rider_src=rider_cols(*ahead[1]), brings=(ahead[1][1], 0)) if len(ahead) == 2 else {}
                    out.append(Gemm("down", 2, [4, 4, 4, 4, 3, 3], in_turn(T["ffn_w_out"][i, j]), tokens, act="g",
                                    evac="resid", waits="g", wide=True, piece=piece, **more))
                    if len(ahead) == 2:
                        out.append(coef_stage(*ahead[1]))
                elif i == 0:
                    out.append(Stage("fourier", {"fl": 16, "xr": DT, "uhi": DT, "ulo": DT}, tokens=tokens, mod=True,
                                     piece=piece))
                    out.append(Gemm("fnet", 2, [4, 4], in_turn(T["fnet_w_out"][0]), tokens, evac="resid",
                                    waits="fl", piece=1))
                else:
                    w = T["ret_w_in"][0]
                    out.append(Gemm("q", 2, [4, 4], in_turn(w), SEQ, evac="to_q", k_outer=True, waits="ulo"))
                    out.append(Stage("decay_rates", {}))
                    out.append(Gemm("k", 2, [4, 4], in_turn(w, D), NTOK, evac="to_k"))
                    out.append(Gemm("v", 4, [4, 4], in_turn(w, 2 * D), NTOK, mode="tokens", evac="to_v"))
                    out.append(Gemm("gate", 4, [4, 4], in_turn(w, 4 * D), SEQ, evac="to_gate"))
                    out.append(Stage("retention", {"mix_lo": RET_HEADS}))
                    out.append(Gemm("ret_out", 2, [4, 4, 4, 4], in_turn(T["ret_w_out"][0]), SEQ, evac="resid",
                                    k_outer=True, waits="heads", view="ret", piece=1))
        out.append(stats(SEQ, "gemm"))
        out.append(Stage("final", {"post": DT}))
        return out

    def block2(l):
        w = lambda name: T[name][l]
        wi = w("w_in_2")
        fixed = lambda cols: (lambda it, pair, k0, kt: rows(wi)[:, k0:k0 + kt, cols[pair]:cols[pair] + UCOLS])

        def ffn(n, pre, post):
            gate, up = w(f"ff{n}_w_gate_2"), w(f"ff{n}_w_up_2")
            pick = lambda it, pair, k0, kt: rows((gate, up)[pair])[:, k0:k0 + kt, bass.ds(it * UCOLS, UCOLS)]
            return [Stage("gain", {"uhi": DT, "ulo": DT, "sq": 4, "sum": 2}, gain=pre),
                    Gemm("up", 11, [4, 4], pick, SEQ, evac="swiglu", k_outer=True, waits="ulo", norm_after=True,
                         wide=False),
                    Gemm("down", 2, [4, 4, 4, 4, 3, 3], in_turn(w(f"ff{n}_w_down_2")), SEQ, act="g", evac="store",
                         waits="g", wide=False),
                    stats(SEQ, "gemm", half=True), Stage("post", {"post": DT, "px": DT}, gain=post)]
        return ffn(1, "pre1", "post1") + [
            stats(SEQ, "post"), Stage("apply", {"xr": DT, "uhi": DT, "ulo": DT}, tokens=SEQ, gain="mix_pre"),
            Gemm("z", 1, [4, 4], in_turn(wi, 0), SEQ, evac="to_z", k_outer=True, waits="ulo"),
            Gemm("xbc", 2, [4, 4], in_turn(wi, 512), SEQ, evac="to_xbc"),
            Stage("conv", {}),
            Gemm("pool_v", 1, [4, 4], fixed((1544, 2312)), SEQ, mode="tokens", evac="to_pool_v"),
            Stage("steps", {}),
            Gemm("q_k", 1, [4, 4], fixed((1800, 2056)), SEQ, evac="to_q_k"),
            Stage("mixer", {"mix_lo": 3}),
            Gemm("mix_out", 2, [4, 4], in_turn(w("w_out_2")), SEQ, evac="store", waits="mix_lo", k_outer=True,
                 last_half_first=True),
            stats(SEQ, "gemm"), Stage("post", {"post": DT, "px": DT}, gain="mix_post")
        ] + ffn(2, "pre2", "post2")

    def follower(stages, j):
        return next((s for s in stages[j + 1:] if isinstance(s, Gemm)), None)

    ctx = ExitStack()
    with ctx:
        def overlay(specs):
            with ExitStack() as s:
                return [s.enter_context(nc.sbuf_tensor(n, shape, dt)) for n, shape, dt in specs]

        def sb(name, shape, dt=f32):
            return ctx.enter_context(nc.sbuf_tensor(name, shape, dt))

        def sem(name):
            return ctx.enter_context(nc.semaphore(name))

        h = sb("h", [P, DT, NTOK])
        f_out = h[:, :, SEQ:NTOK]
        u_hi, u_lo = sb("u_hi", [P, DT, NTOK], f32r), sb("u_lo", [P, DT, NTOK], f32r)
        raw = sb("raw", [P, RING, KT_MAX * UCOLS])
        w_hi = sb("w_hi", [P, RING, KT_MAX * UCOLS], f32r)
        w_lo = sb("w_lo", [P, RING, KT_MAX * UCOLS], f32r)
        ones = sb("ones", [P, P])
        acc = sb("acc", [P, 2, NTOK])
        rstd = sb("rstd", [P, NTOK])
        tmp1, tmp2 = sb("tmp1", [P, 2, NTOK]), sb("tmp2", [P, 2, NTOK])
        vec = sb("vec", [P, VEC_N])
        lvecs = sb("lvecs", [P, LAYERS2 * LAYER_N])
        lvec = sb("lvec", [P, LAYER_N])
        mod = sb("mod", [P, 3, 24, 2])
        coef = sb("coef", [P, 3, DT, 2])
        cond_cols = sb("cond_cols", [P, 5 * DT * 4], f32r)
        cond_hi = cond_cols[:, :].rearrange("p (g k s x) -> p g k s x", g=5, s=2, x=2)
        root_of_eps = sb("root_of_eps", [P, 1])
        turned = sb("turned", [P, 2, 2, 32])
        cond = sb("cond", [P, DT, 2])
        eps = sb("eps", [P, 2])

        g_hi, g_lo = overlay([("g_hi", [P, FT, NTOK], f32r), ("g_lo", [P, FT, NTOK], f32r)])
        dft, dft_hi, dft_lo, ab_hi, ab_lo = overlay([
            ("dft", [P, 5, SEQ], f32), ("dft_hi", [P, 5, SEQ], f32r), ("dft_lo", [P, 5, SEQ], f32r),
            ("ab_hi", [P, 2, NTOK], f32r), ("ab_lo", [P, 2, NTOK], f32r)])
        rq, rk, rv, rg, rtab, decay, weighted, lgam = overlay([
            ("rq", [P, DT, SEQ], f32), ("rk", [P, DT, NTOK], f32), ("rv", [P, 4, 2 * D], f32),
            ("rg", [P, 16, SEQ], f32), ("rtab", [P, 1664], f32), ("decay_w", [P, 4, SEQ], f32),
            ("weighted", [P, 4, SEQ], f32), ("lgam", [P, 64], f32)])
        ro = (tmp1[:, :, :].rearrange("p a (b n) -> p (a b) n", n=SEQ), f_out[:, 4:8, :])
        past_decay, rotated = f_out[:, 0:2, :], f_out[:, 2:4, :]
        rt = tmp2[:, :, :].rearrange("p a (b n) -> p (a b) n", n=SEQ)
        rcos = rtab[:, 0:512].rearrange("p (r n) -> p r n", r=2)
        rsin = rtab[:, 512:1024].rearrange("p (r n) -> p r n", r=2)
        rdelta = rtab[:, 1024:1536].rearrange("p (b n) -> p b n", b=2)
        rswap = rtab[:, 1536:1664]

        tab_spec = [("tables", [P, TWO_N], f32), ("poolw", [P, 2, P], f32), ("dtw", [P, 64], f32)]
        tables, poolw, dtw, g2_hi, g2_lo = overlay(tab_spec + [
            ("g2_hi", [P, FT, SEQ], f32r), ("g2_lo", [P, FT, SEQ], f32r)])
        (_, _, _, zs, xpad, cx, pool_u, att_v, qk, xtok, cb, seg, mixf, probs, probs_t, dtw_hi, dtw_lo,
         small) = overlay([(n + "_", s, d) for n, s, d in tab_spec] + [
             ("zs", [P, 4, SEQ], f32), ("xpad", [P, 8, SEQ + 3], f32), ("cx", [P, 8, SEQ], f32),
             ("pool_u", [P, 2, SEQ], f32), ("att_v", [P, 2, SEQ], f32), ("qk", [P, 4, SEQ], f32),
             ("xtok", [P, 2, SSD_INNER], f32), ("cb", [P, 4, SEQ], f32), ("seg", [P, 4, 2, SEQ], f32),
             ("mixf", [P, 8, SEQ], f32), ("probs", [P, 2, 2, SEQ], f32), ("probs_t", [P, 2, 2, SEQ], f32),
             ("dtw_hi", [P, 64], f32r), ("dtw_lo", [P, 64], f32r), ("small", [P, 320], f32)])
        tab = {n: tables[:, TWO_AT[n]:TWO_AT[n] + c] for n, c in TWO_FIELDS}
        tri = tab["tri"].rearrange("p (b n) -> p b n", b=2)
        band = tab["band"].rearrange("p (b g n) -> p b g n", b=2, g=POOL_GROUPS)
        mask = tab["mask"].rearrange("p (b n) -> p b n", b=2)
        small_fields, _ = offsets([(n, 16) for n in """dt_in neg_abs e_dt s_den s_dt s2 series log1p dt da neg_a
                                                       acs mx neg_mx sums inv""".split()])

        def sm(name):
            return small[:, small_fields[name]:small_fields[name] + 16].rearrange("p (b n) -> p b n", b=2)

        ps = ctx.enter_context(nc.psum_tensor("ps", [P, 8, 512], f32))
        STAT = 4

        def vecs(name, a=0, n=1):
            return vec[:, VEC_AT[name] + a:VEC_AT[name] + a + n]

        def lv(name, a=0, n=1):
            return lvec[:, LAYER_AT[name] + a:LAYER_AT[name] + a + n]

        hi_ready = sem("hi_ready")
        lo_ready = sem("lo_ready")
        unit_used = sem("unit_used")
        banks01_read = sem("banks01_read")
        banks23_read = sem("banks23_read")
        x_landed = sem("x_landed")
        vec_landed = sem("vec_landed")
        cond_landed = sem("cond_landed")
        dft_landed = sem("dft_landed")
        ret_landed = sem("ret_landed")
        tables_landed = sem("tables_landed")
        lvec_landed = sem("lvec_landed")
        lvec_copied = sem("lvec_copied")
        poolw_landed = sem("poolw_landed")
        dtw_landed = sem("dtw_landed")
        out_landed = sem("out_landed")
        setup_ready = sem("setup_ready")
        cond_silu_ready = sem("cond_silu_ready")
        cond_ready = sem("cond_ready")
        cond_lo_ready = sem("cond_lo_ready")
        squares_ready = sem("squares_ready")
        sums_ready = sem("sums_ready")
        stat_ready = sem("stat_ready")
        root_ready = sem("root_ready")
        rstd_ready = sem("rstd_ready")
        scaled_ready = sem("scaled_ready")
        u_hi_ready = sem("u_hi_ready")
        u_lo_ready = sem("u_lo_ready")
        g_hi_ready = sem("g_hi_ready")
        g_lo_ready = sem("g_lo_ready")
        a_normed = sem("a_normed")
        b_normed = sem("b_normed")
        rows_turned = sem("rows_turned")
        parts_added = sem("parts_added")
        coef_ready = sem("coef_ready")
        post_ready = sem("post_ready")
        post_scaled_ready = sem("post_scaled_ready")
        dft_hi_ready = sem("dft_hi_ready")
        dft_lo_ready = sem("dft_lo_ready")
        ab_ready = sem("ab_ready")
        ab_hi_ready = sem("ab_hi_ready")
        ab_lo_ready = sem("ab_lo_ready")
        f_ready = sem("f_ready")
        f_hi_ready = sem("f_hi_ready")
        f_lo_ready = sem("f_lo_ready")
        dve_order = sem("dve_order")
        mix_hi_ready = sem("mix_hi_ready")
        mix_lo_ready = sem("mix_lo_ready")
        swapped = sem("swapped")
        swap_taken = sem("swap_taken")
        scores_ready = sem("scores_ready")
        head_out_ready = sem("head_out_ready")
        head_stat_ready = sem("head_stat_ready")
        decay_exp_ready = sem("decay_exp_ready")
        decays_ready = sem("decays_ready")
        head_out_copied = sem("head_out_copied")
        head_squares_ready = sem("head_squares_ready")
        head_root_ready = sem("head_root_ready")
        decay_abs_ready = sem("decay_abs_ready")
        log_gamma_ready = sem("log_gamma_ready")
        roped = sem("roped")
        exponents_ready = sem("exponents_ready")
        weighted_ready = sem("weighted_ready")
        head_sums_ready = sem("head_sums_ready")
        centred_ready = sem("centred_ready")
        gated_ready = sem("gated_ready")
        dt_ready = sem("dt_ready")
        qk_swapped = sem("qk_swapped")
        pool_mean_ready = sem("pool_mean_ready")
        cb_ready = sem("cb_ready")
        pool_out_ready = sem("pool_out_ready")
        xtok_ready = sem("xtok_ready")
        acs_ready = sem("acs_ready")
        head_acs_ready = sem("head_acs_ready")
        head_y_ready = sem("head_y_ready")
        att_scores_ready = sem("att_scores_ready")
        probs_turned = sem("probs_turned")
        att_out_ready = sem("att_out_ready")
        ssd_stat_ready = sem("ssd_stat_ready")
        dtw_hi_ready = sem("dtw_hi_ready")
        conv_ready = sem("conv_ready")
        pool_mean_copied = sem("pool_mean_copied")
        dt_exp_ready = sem("dt_exp_ready")
        xtok_copied = sem("xtok_copied")
        segment_exp_ready = sem("segment_exp_ready")
        probs_exp_ready = sem("probs_exp_ready")
        probs_t_copied = sem("probs_t_copied")
        att_copied = sem("att_copied")
        ssd_squares_ready = sem("ssd_squares_ready")
        ssd_root_ready = sem("ssd_root_ready")
        dtw_lo_ready = sem("dtw_lo_ready")
        conv_sum_ready = sem("conv_sum_ready")
        dt_taken = sem("dt_taken")
        da_ready = sem("da_ready")
        qk_roped = sem("qk_roped")
        cb_taken = sem("cb_taken")
        pool_out_taken = sem("pool_out_taken")
        acs_taken = sem("acs_taken")
        segment_taken = sem("segment_taken")
        att_masked = sem("att_masked")
        max_ready = sem("max_ready")
        segment_ready = sem("segment_ready")
        probs_ready = sem("probs_ready")
        y_gated = sem("y_gated")
        y_normed = sem("y_normed")
        poolw_zeroed = sem("poolw_zeroed")
        raw_landed = [sem(f"raw_landed{i}") for i in range(RING)]
        read = (banks01_read, banks23_read)

        def begun(value):
            return not isinstance(value, int) or value > 0

        class Order:

            def __init__(self, eng, sem):
                self.eng, self.sem, self.n = eng, sem, 0

            def enter(self, layer, per):
                self.first, self.per, self.n = self.n, per, layer * per + self.n
                self.k = 0

            def leave(self, layers):
                assert self.k == self.per, ("instructions of a layer in order", self.k)
                self.n = self.first + layers * self.per

            def link(self, ins):
                self.n = self.n + 1
                self.k = self.k + 1 if hasattr(self, "k") else 0
                ins.then_inc(self.sem, 1)
                self.eng.wait_ge(self.sem, self.n)

        def operand(g, k):
            if g.more.get("view") == "ret":
                v = [t[:, :, :].rearrange("p a (b n) -> p (a b) n", n=SEQ) for t in (u_hi, u_lo)]
                return [x[:, k, 0:g.tokens] for x in v]
            pair = (u_hi, u_lo) if g.act == "u" else (g_hi, g_lo) if g.more["wide"] else (g2_hi, g2_lo)
            return [t[:, k, 0:g.tokens] for t in pair]

        def sp_gemm(sp, g, t):
            def turn(it):
                for u, (kind, pair, k0, kt) in enumerate(g.order(it)):
                    q, slot = it * g.units + u + t["unit"], u % RING
                    dst = raw[:, slot, 0:kt * UCOLS].rearrange("p (k n) -> p k n", k=kt)
                    src = (g.src(it, pair, k0, kt) if kind == "main" else
                           g.rider_src(it * (g.riders // 2) + pair // 2, pair % 2, k0, kt))
                    both = g.last_half_first and it_is_first(it)
                    if both and u == 1:
                        sp.wait_ge(lo_ready, q - (RING - 1) + 1)
                    elif begun(q - (RING - 1)) and not (both and u == 2):
                        sp.wait_ge(lo_ready, q - (RING - 1))
                    sp.dma_start(dst, src).then_inc(raw_landed[slot], 16)
            turn(0)
            loop(sp, 1, g.n, turn)

        def split_hi(act, g, t, it, u):
            q, slot = it * g.units + u + t["unit"], u % RING
            cols = g.order(it)[u][3] * UCOLS
            landed = (it * (g.units // RING) + u // RING) * 16 + (t["unit_div"]) * 16 + 16
            act.wait_ge(raw_landed[slot], landed)
            if begun(q - (RING - 1)):
                act.wait_ge(unit_used, q - (RING - 1))
            act.activation(w_hi[:, slot, 0:cols], raw[:, slot, 0:cols], ACT.Copy).then_inc(hi_ready, 1)

        def split_lo(dve, g, t, it, u):
            q, slot = it * g.units + u + t["unit"], u % RING
            cols = g.order(it)[u][3] * UCOLS
            dve.wait_ge(hi_ready, q + 1)
            dve.tensor_tensor(w_lo[:, slot, 0:cols], raw[:, slot, 0:cols], w_hi[:, slot, 0:cols].bitcast(f32),
                              ALU.subtract).then_inc(lo_ready, 1)

        def stream(eng, g, t, nxt, split, evacuate, turn_rows=None):
            t_next = {"unit": t["unit"] + g.n * g.units, "unit_div": t["unit_div"] + g.n * (g.units // RING)}

            def turn(it):
                last = isinstance(it, int) and it == g.n - 1
                for u in range(g.units):
                    v = u + RING
                    if v < g.units:
                        split(eng, g, t, it, v)
                    elif not last:
                        split(eng, g, t, it + 1, v - g.units)
                    elif nxt is not None:
                        split(eng, nxt, t_next, 0, v - g.units)
                    kind, pair = g.order(it)[u][:2]
                    if g.closes(it, kind, pair) == u + 1:
                        if kind == "main":
                            evacuate(eng, g, t, it, pair)
                        elif turn_rows:
                            turn_rows(eng, g, t, it, pair)
            turn(0)
            if g.n > 1:
                loop(eng, 1, g.n - 1, turn)
                turn(g.n - 1)

        def dve_turn_rows(dve, g, t, it, r):
            if begun(it * g.units + t["unit"] + g.closes(it, "rider", r)):
                dve.wait_ge(unit_used, it * g.units + t["unit"] + g.closes(it, "rider", r))
            if begun(it * g.riders + r + t["rider"] - 1):
                dve.wait_ge(parts_added, it * g.riders + r + t["rider"] - 1)
            for q in range(4):
                part = slice(32 * q, 32 * q + 32)
                rows4 = ps[part, 4 + r % 2, 0:UCOLS].rearrange("p (j n) -> p j n", j=2)
                ins = dve.transpose(turned[part, r % 2, :, :], rows4[:, :, 32 * q:32 * q + 32])
            ins.then_inc(rows_turned, 1)
            dve.wait_ge(rows_turned, it * g.riders + r + t["rider"] + 1)
            piece, j0 = g.more["brings"]
            four = turned[:, r % 2, :, 0:4].rearrange("p j (s x) -> p j s x", x=2)
            dve.tensor_tensor(mod[:, piece, bass.ds((it * g.riders + r) * 2 + j0, 2), :], four[:, :, :, 0],
                              four[:, :, :, 1], ALU.add).then_inc(parts_added, 1)

        def complete(eng, g, t, it, pair):
            if begun(it * g.units + t["unit"] + g.closes(it, "main", pair)):
                eng.wait_ge(unit_used, it * g.units + t["unit"] + g.closes(it, "main", pair))

        def blocks(g, pair):
            return ps[:, 2 * pair:2 * pair + 2, 0:g.tokens]

        def act_evacuate(act, g, t, it, pair):
            done = read[pair]
            tile2 = bass.ds(it * 4 + 2 * pair, 2)
            if g.evac == "swiglu":
                if pair == 0:
                    if g.norm_after:
                        act.wait_ge(a_normed, it + t["normed"] + 1)
                        act.activation(tmp1[:, :, 0:g.tokens], tmp1[:, :, 0:g.tokens], ACT.Silu).then_inc(done, 1)
                    else:
                        complete(act, g, t, it, 0)
                        if begun(it + t["pair"]):
                            act.wait_ge(banks23_read, it + t["pair"])
                        act.activation(tmp1[:, :, 0:g.tokens], blocks(g, 0), ACT.Silu).then_inc(done, 1)
                else:
                    act.wait_ge(banks23_read, it + t["pair"] + 1)
                    hi = g_hi if g.more["wide"] else g2_hi
                    act.activation(hi[:, bass.ds((it + g.first) * 2, 2), 0:g.tokens], tmp2[:, :, 0:g.tokens],
                                   ACT.Copy).then_inc(g_hi_ready, 1)
                return
            if g.squares:
                act.wait_ge(done, it + t["pair"] + 1)
                act_square(act, f_out if g.evac == "store" else h, g.tokens, 2 * it + pair, t)
                return
            complete(act, g, t, it, pair)
            func = ACT.Silu if g.evac in ("to_gate", "to_z") else ACT.Copy
            if g.evac == "to_v":
                src = ps[:, 2 * pair:2 * pair + 2, :].rearrange("p b (c n) -> p (b c) n", c=2)
                dst = rv[:, :, bass.ds(it * 2 * UCOLS + pair * UCOLS, UCOLS)]
            elif g.evac == "to_pool_v":
                src = ps[:, 2 * pair, :].rearrange("p (c n) -> p c n", c=2)
                dst = (pool_u, att_v)[pair][:, :, :]
            elif g.evac == "to_q_k":
                src, dst = blocks(g, pair), qk[:, 2 * pair:2 * pair + 2, :]
            elif g.evac == "to_xbc":
                src, dst = blocks(g, pair), xpad[:, tile2, 3:3 + SEQ]
            else:
                to = {"to_q": rq, "to_k": rk, "to_gate": rg, "to_z": zs}[g.evac]
                src, dst = blocks(g, pair), to[:, tile2, 0:g.tokens]
            act.activation(dst, src, func).then_inc(done, 1)

        def dve_evacuate(dve, g, t, it, pair):
            done = read[pair]
            if g.evac == "swiglu":
                per_token = rstd[:, 0:g.tokens].unsqueeze(1).to_broadcast([P, 2, g.tokens])
                if pair == 0 and g.norm_after:
                    complete(dve, g, t, it, 0)
                    if it_is_first(it):
                        dve.wait_ge(rstd_ready, t["stat"] + 1)
                    if begun(it + t["pair"]):
                        dve.wait_ge(banks23_read, it + t["pair"])
                    dve.tensor_tensor(tmp1[:, :, 0:g.tokens], blocks(g, 0), per_token, ALU.mult
                                      ).then_inc(a_normed, 1)
                if pair == 1:
                    complete(dve, g, t, it, 1)
                    if begun(it + t["g"]):
                        dve.wait_ge(g_lo_ready, it + t["g"])
                    b = blocks(g, 1)
                    if g.norm_after:
                        b = tmp2[:, :, 0:g.tokens]
                        dve.tensor_tensor(b, blocks(g, 1), per_token, ALU.mult).then_inc(b_normed, 1)
                        dve.wait_ge(b_normed, it + t["normed"] + 1)
                    dve.wait_ge(banks01_read, it + t["pair"] + 1)
                    dve.tensor_tensor(tmp2[:, :, 0:g.tokens], b, tmp1[:, :, 0:g.tokens], ALU.mult
                                      ).then_inc(done, 1)
                    dve.wait_ge(g_hi_ready, it + t["g"] + 1)
                    hi, lo = (g_hi, g_lo) if g.more["wide"] else (g2_hi, g2_lo)
                    two = bass.ds((it + g.first) * 2, 2)
                    dve.tensor_tensor(lo[:, two, 0:g.tokens], tmp2[:, :, 0:g.tokens],
                                      hi[:, two, 0:g.tokens].bitcast(f32), ALU.subtract
                                      ).then_inc(g_lo_ready, 1)
                return
            if g.squares and 2 * it + pair >= 2:
                dve_add_squares(dve, g.tokens, 2 * it + pair - 1, t)
            if g.evac == "store":
                complete(dve, g, t, it, pair)
                dve.tensor_copy(f_out[:, bass.ds(it * 4 + 2 * pair, 2), :], blocks(g, pair)).then_inc(done, 1)
            elif g.evac == "resid":
                complete(dve, g, t, it, pair)
                for b in range(2):
                    for s in range(g.tokens // SEQ):
                        tile, tok = it * 4 + 2 * pair + b, slice(s * SEQ, (s + 1) * SEQ)
                        ins = dve.scalar_tensor_tensor(h[:, tile, tok], ps[:, 2 * pair + b, tok],
                                                       mod[:, g.more["piece"], 16 + tile, s:s + 1], h[:, tile, tok],
                                                       ALU.mult, ALU.add)
                ins.then_inc(done, 1)

        def pe_gemm(pe, g, t):
            def turn(it):
                for u, (kind, pair, k0, kt) in enumerate(g.order(it)):
                    slot = u % RING
                    if kind == "main" and (k0 == 4 if g.last_half_first else k0 == 0):
                        if begun(it + t["pair"]):
                            pe.wait_ge(read[pair], it + t["pair"])
                    if kind == "rider" and k0 == 0:
                        if it_is_first(it) and pair == 0 and begun(t["stat"]):
                            pe.wait_ge(root_ready, t["stat"])
                        if begun(it * g.riders + pair + t["rider"] - 1):
                            pe.wait_ge(rows_turned, it * g.riders + pair + t["rider"] - 1)
                    pe.wait_ge(lo_ready, it * g.units + u + t["unit"] + 1)
                    begins = k0 + kt == sum(g.ks) if g.last_half_first else k0 == 0
                    final = k0 == 0 if g.last_half_first else k0 + kt == sum(g.ks)
                    if kind == "rider":
                        for k in range(kt):
                            for w in (w_hi, w_lo):
                                ins = pe.matmul(ps[:, 4 + pair % 2, 0:UCOLS], cond_cols[:, 4 * (k0 + k):4 * (k0 + k) + P],
                                                w[:, slot, k * UCOLS:(k + 1) * UCOLS],
                                                start=k0 + k == 0 and w is w_hi,
                                                stop=k0 + k == DT - 1 and w is w_lo)
                    elif g.mode == "tokens":
                        for tb in range(g.tokens // P):
                            out = ps[:, 2 * pair + tb // 2, (tb % 2) * UCOLS:(tb % 2 + 1) * UCOLS]
                            for k in range(kt):
                                if tb == 0 and it_is_first(it):
                                    arrived(pe, g, t, k0 + k)
                                hi, lo = [x[:, tb * P:(tb + 1) * P] for x in operand(g, k0 + k)]
                                cols = slice(k * UCOLS, (k + 1) * UCOLS)
                                for n, (a, w) in enumerate(((hi, w_hi), (hi, w_lo), (lo, w_hi))):
                                    ins = pe.matmul(out, a, w[:, slot, cols],
                                                    start=begins and k == 0 and n == 0 and tb % 2 == 0,
                                                    stop=final and k == kt - 1 and n == 2, skip_group_check=True)
                    else:
                        for b in range(2):
                            out = ps[:, 2 * pair + b, 0:g.tokens]
                            for k in range(kt):
                                if b == 0 and it_is_first(it):
                                    arrived(pe, g, t, k0 + k)
                                hi, lo = operand(g, k0 + k)
                                cols = slice(k * UCOLS + b * P, k * UCOLS + b * P + P)
                                for n, (w, a) in enumerate(((w_hi, hi), (w_hi, lo), (w_lo, hi))):
                                    ins = pe.matmul(out, w[:, slot, cols], a, start=begins and k == 0 and n == 0,
                                                    stop=final and k == kt - 1 and n == 2)
                    ins.then_inc(unit_used, 1)
                    if g.more.get("waits") == "heads" and it_is_first(it) and u in (0, 2):
                        head_stat(pe, RET_HEADS - 1, u // 2)
                    if g.norm_after and it_is_first(it) and u == 1:
                        pe_stats(pe, stats(g.tokens, "gemm"), t)
            turn(0)
            loop(pe, 1, g.n, turn)

        def it_is_first(it):
            return isinstance(it, int) and it == 0

        def arrived(pe, g, t, k):
            what = g.more.get("waits")
            if what == "ulo":
                if begun(t["ulo"] - DT + k + 1):
                    pe.wait_ge(u_lo_ready, t["ulo"] - DT + k + 1)
            elif what == "g" and k in (0, 19, 20):
                if begun(t["g"] - (FT // 2) + k // 2 + 1 if k else t["g"] - 2):
                    pe.wait_ge(g_lo_ready, t["g"] - (FT // 2) + k // 2 + 1 if k else t["g"] - 2)
            elif what == "fl" and k == 0:
                pe.wait_ge(f_lo_ready, 16)
            elif what == "heads" and k % 4 == 0:
                pe.wait_ge(mix_lo_ready, k // 4 + 1)
            elif what == "mix_lo" and k == 4 and g.last_half_first:
                pe.wait_ge(mix_lo_ready, t["mix_lo"] - 1)
            elif what == "mix_lo" and k == 0:
                if begun(t["mix_lo"]):
                    pe.wait_ge(mix_lo_ready, t["mix_lo"])

        def act_square(act, source, n, m, t):
            first_pair = isinstance(m, int) and m == 0
            if not first_pair and m >= 2:
                act.wait_ge(sums_ready, t["sum"] + m - 1)
            out = acc if first_pair else tmp1
            act.activation(out[:, :, 0:n], source[:, 2 * m:2 * m + 2, 0:n], ACT.Square
                           ).then_inc(squares_ready, 1)

        def dve_add_squares(dve, n, m, t):
            dve.wait_ge(squares_ready, t["sq"] + m + 1)
            if m == 2:
                dve.wait_ge(sums_ready, t["sum"] + 1)
            dve.tensor_tensor(acc[:, :, 0:n], acc[:, :, 0:n], tmp1[:, :, 0:n], ALU.add).then_inc(sums_ready, 1)

        def act_load_root(act):
            act.activation(root_of_eps[:, :], eps[:, 0:1], ACT.Sqrt)

        def act_stats(act, g, t):
            src, n = g.more["source"], g.more["tokens"]
            for m in range(4 if src == "post" else 0):
                act.wait_ge(post_ready, t["post"] - DT + 2 * m + 2)
                act_square(act, h, n, m, t)
            act.wait_ge(stat_ready, t["stat"] + 1)
            four = 4.0 if g.more.get("half") else 1.0
            act.activation(rstd[:, 0:n], ps[:, STAT, 0:n], ACT.Sqrt, scale=four / D,
                           bias=eps[:, 1:2] if four == 4.0 else eps[:, 0:1]).then_inc(root_ready, 1)

        def dve_stats(dve, g, t):
            n = g.more["tokens"]
            if g.more["source"] != "gemm":
                for m in (1, 2):
                    dve_add_squares(dve, n, m, t)
            dve.wait_ge(root_ready, t["stat"] + 1)
            dve.reciprocal(rstd[:, 0:n], rstd[:, 0:n]).then_inc(rstd_ready, 1)

        def pe_stats(pe, g, t):
            n, more = g.more["tokens"], g.more["source"] != "gemm"
            sums, squares = (t["sum"] + 2, t["sq"] + 4) if more else (t["sum"], t["sq"])
            if begun(t["rider"]):
                pe.wait_ge(rows_turned, t["rider"])
            pe.wait_ge(sums_ready, sums)
            for i in range(2):
                pe.matmul(ps[:, STAT, 0:n], ones[:, :], acc[:, i, 0:n], start=i == 0, stop=False)
            pe.wait_ge(squares_ready, squares)
            for i in range(2):
                ins = pe.matmul(ps[:, STAT, 0:n], ones[:, :], tmp1[:, i, 0:n], start=False, stop=i == 1)
            ins.then_inc(stat_ready, 1)

        def act_apply_tile(act, g, t, k):
            n = g.more["tokens"]
            if g.more.get("mod") and k == 0 and begun(t["coef"]):
                act.wait_ge(coef_ready, t["coef"])
            act.wait_ge(scaled_ready, t["xr"] + k + 1)
            if begun(t["ulo"] + k - 1):
                act.wait_ge(u_lo_ready, t["ulo"] + k - 1)
            for out in (tmp1[:, k % 2, :], u_hi[:, k, :]):
                if g.more.get("mod"):
                    for s in range(n // SEQ):
                        tok = slice(s * SEQ, (s + 1) * SEQ)
                        ins = act.activation(out[:, tok], tmp2[:, k % 2, tok], ACT.Identity,
                                             scale=coef[:, g.more["piece"], k, s:s + 1],
                                             bias=mod[:, g.more["piece"], k, s:s + 1])
                else:
                    ins = act.activation(out[:, 0:n], tmp2[:, k % 2, 0:n], ACT.Copy, scale=lv(g.more["gain"], k))
            ins.then_inc(u_hi_ready, 1)

        def act_apply(act, g, t):
            for k in range(DT):
                act_apply_tile(act, g, t, k)

        def act_gain(act, g, t):
            for k in range(DT):
                if begun(t["post"] - DT + k + 1):
                    act.wait_ge(post_ready, t["post"] - DT + k + 1)
                act.activation(u_hi[:, k, 0:SEQ], h[:, k, 0:SEQ], ACT.Copy, scale=lv(g.more["gain"], k)
                               ).then_inc(u_hi_ready, 1)
                if k % 2 == 1:
                    act_square(act, h, SEQ, k // 2, t)

        def dve_gain_tile(dve, g, t, k):
            dve.wait_ge(u_hi_ready, t["uhi"] + k + 1)
            dve.scalar_tensor_tensor(u_lo[:, k, 0:SEQ], h[:, k, 0:SEQ], lv(g.more["gain"], k),
                                     u_hi[:, k, 0:SEQ].bitcast(f32), ALU.mult, ALU.subtract
                                     ).then_inc(u_lo_ready, 1)
            if k in (3, 5):
                dve_add_squares(dve, SEQ, k // 2, t)

        def dve_gain(dve, g, t, units_after, gemm):
            for k in range(DT):
                dve_gain_tile(dve, g, t, k)
                for u in units_after.get(k, []):
                    split_lo(dve, gemm, t, 0, u)

        def dve_scaled(dve, g, t, k):
            n = g.more["tokens"]
            if k == 0 and begun(t["stat"]):
                dve.wait_ge(rstd_ready, t["stat"])
            if begun(t["uhi"] + k - 1):
                dve.wait_ge(u_hi_ready, t["uhi"] + k - 1)
            dve.tensor_tensor(tmp2[:, k % 2, 0:n], h[:, k, 0:n], rstd[:, 0:n], ALU.mult).then_inc(scaled_ready, 1)

        def dve_apply_tile(dve, g, t, k):
            n = g.more["tokens"]
            if k + 1 < DT:
                dve_scaled(dve, g, t, k + 1)
            dve.wait_ge(u_hi_ready, t["uhi"] + k + 1)
            dve.tensor_tensor(u_lo[:, k, 0:n], tmp1[:, k % 2, 0:n], u_hi[:, k, 0:n].bitcast(f32),
                              ALU.subtract).then_inc(u_lo_ready, 1)

        def dve_apply(dve, g, t):
            dve_scaled(dve, g, t, 0)
            for k in range(DT):
                dve_apply_tile(dve, g, t, k)

        def dve_post(dve, g, t, gain=None):
            if begun(t["stat"]):
                dve.wait_ge(rstd_ready, t["stat"])
            for k in range(DT + 3):
                if k < DT:
                    if begun(t["post"] + k - 1):
                        dve.wait_ge(post_ready, t["post"] + k - 1)
                    dve.tensor_tensor(tmp2[:, k % 2, 0:SEQ], f_out[:, k, :], rstd[:, 0:SEQ], ALU.mult
                                      ).then_inc(post_scaled_ready, 1)
                if 0 < k <= DT:
                    if begun(t["px"] + k):
                        dve.wait_ge(post_scaled_ready, t["px"] + k)
                    dve.scalar_tensor_tensor(h[:, k - 1, 0:SEQ], tmp2[:, (k - 1) % 2, 0:SEQ],
                                             lv(g.more["gain"], k - 1), h[:, k - 1, 0:SEQ], ALU.mult, ALU.add
                                             ).then_inc(post_ready, 1)
                if gain and k >= 3:
                    dve_gain_tile(dve, gain, t, k - 3)

        def dve_coef(dve, g, t, order):
            i, piece, (j0, j1) = g.more["layer"], g.more["piece"], g.more["parts"]
            m, c = mod[:, piece, :, :], coef[:, piece, :, :]
            if begun(t["rider"]):
                dve.wait_ge(parts_added, t["rider"])
            bias = vecs("b_mod", i * 72 + piece * 24 + j0, j1 - j0).unsqueeze(2).to_broadcast([P, j1 - j0, 2])
            order.link(dve.tensor_tensor(m[:, j0:j1, :], m[:, j0:j1, :], bias, ALU.add))
            if j1 == 24 and piece != 1:
                ins = dve.tensor_scalar(m[:, 16:24, :], m[:, 16:24, :], 0.5, None, ALU.mult)
            if j0 == 0:
                gain = vecs("norm_g", (i * 3 + piece) * 8, 8).unsqueeze(2).to_broadcast([P, DT, 2])
                ins = dve.scalar_tensor_tensor(c, m[:, 8:16, :], 1.0, gain, ALU.add, ALU.mult)
            ins.then_inc(coef_ready, 1)

        def log1p(dve, order, e, den, s, s2, r, out):
            order.link(dve.tensor_scalar(den, e, 2.0, None, ALU.add))
            order.link(dve.reciprocal(den, den))
            order.link(dve.tensor_tensor(s, e, den, ALU.mult))
            order.link(dve.tensor_tensor(s2, s, s, ALU.mult))
            order.link(dve.tensor_scalar(r, s2, LOG1P_TERMS[0], None, ALU.mult))
            for c in LOG1P_TERMS[1:]:
                order.link(dve.scalar_tensor_tensor(r, r, c, s2, ALU.add, ALU.mult))
            order.link(dve.scalar_tensor_tensor(out, r, 1.0, s, ALU.add, ALU.mult))
            order.link(dve.tensor_scalar(out, out, 2.0, None, ALU.mult))

        def pe_fourier(pe, t):
            def step1(j):
                g, s = j // 2, j % 2
                if s == 0:
                    pe.wait_ge(u_lo_ready, t["ulo"] + g + 1)
                pe.wait_ge(dft_lo_ready, 1)
                if begun(j - 1):
                    pe.wait_ge(ab_lo_ready, j - 1)
                for tb in range(2):
                    tok = slice(s * SEQ + tb * P, s * SEQ + (tb + 1) * P)
                    for n, (a, w) in enumerate(((u_hi, dft_hi), (u_hi, dft_lo), (u_lo, dft_hi))):
                        ins = pe.matmul(ps[:, 5 + j % 2, tb * SEQ:(tb + 1) * SEQ], a[:, g, tok], w[:, 0, :],
                                        start=n == 0, stop=n == 2)
                ins.then_inc(ab_ready, 1)

            def step2(j):
                pe.wait_ge(ab_lo_ready, j + 1)
                if begun(j - 1):
                    pe.wait_ge(f_lo_ready, j - 1)
                n = 0
                for tb in range(2):
                    for part in range(2):
                        cols = slice(tb * SEQ + part * P, tb * SEQ + (part + 1) * P)
                        for a, w in ((ab_hi, dft_hi), (ab_hi, dft_lo), (ab_lo, dft_hi)):
                            ins = pe.matmul(ps[:, j % 2, 0:SEQ], a[:, j % 2, cols], w[:, 1 + 2 * part + tb, :],
                                            start=n == 0, stop=n == 11)
                            n += 1
                ins.then_inc(f_ready, 1)
            step1(0)
            for j in range(16):
                if j + 1 < 16:
                    step1(j + 1)
                step2(j)

        def act_fourier(act, g, t):
            for k in (0, 1):
                act_apply_tile(act, g, t, k)
            act.wait_ge(dft_landed, 16)
            act.activation(dft_hi[:, :, :], dft[:, :, :], ACT.Copy).then_inc(dft_hi_ready, 1)

            def take_ab(j):
                act.wait_ge(ab_ready, j + 1)
                if begun(j - 1):
                    act.wait_ge(f_ready, j - 1)
                act.activation(ab_hi[:, j % 2, :], ps[:, 5 + j % 2, :], ACT.Copy).then_inc(ab_hi_ready, 1)
            act_apply_tile(act, g, t, 2)
            take_ab(0)
            for j in range(16):
                if j % 2 == 0 and j // 2 + 3 < DT:
                    act_apply_tile(act, g, t, j // 2 + 3)
                if j + 1 < 16:
                    take_ab(j + 1)
                tile, tok = j // 2, slice((j % 2) * SEQ, (j % 2 + 1) * SEQ)
                act.wait_ge(f_ready, j + 1)
                act.activation(u_hi[:, tile, tok], ps[:, j % 2, 0:SEQ], ACT.Copy).then_inc(f_hi_ready, 1)

        def dve_fourier(dve, g, t):
            dve_scaled(dve, g, t, 0)
            for k in (0, 1):
                dve_apply_tile(dve, g, t, k)
            dve.wait_ge(dft_hi_ready, 1)
            dve.tensor_tensor(dft_lo[:, :, :], dft[:, :, :], dft_hi[:, :, :].bitcast(f32), ALU.subtract
                              ).then_inc(dft_lo_ready, 1)

            def take_ab(j):
                dve.wait_ge(ab_hi_ready, j + 1)
                dve.tensor_tensor(ab_lo[:, j % 2, :], ps[:, 5 + j % 2, :], ab_hi[:, j % 2, :].bitcast(f32),
                                  ALU.subtract).then_inc(ab_lo_ready, 1)
            dve_apply_tile(dve, g, t, 2)
            take_ab(0)
            for j in range(16):
                if j % 2 == 0 and j // 2 + 3 < DT:
                    dve_apply_tile(dve, g, t, j // 2 + 3)
                if j + 1 < 16:
                    take_ab(j + 1)
                tile, tok = j // 2, slice((j % 2) * SEQ, (j % 2 + 1) * SEQ)
                dve.wait_ge(f_hi_ready, j + 1)
                dve.tensor_tensor(u_lo[:, tile, tok], ps[:, j % 2, 0:SEQ], u_hi[:, tile, tok].bitcast(f32),
                                  ALU.subtract).then_inc(f_lo_ready, 1)

        LG = {n: lgam[:, 8 * i:8 * i + 8] for i, n in
              enumerate("neg_abs e den s s2 r log1p lg".split())}

        def rope_pair(hd, i):
            return (rq, rk)[i][:, 2 * hd:2 * hd + 2, 0:SEQ]

        def ret_view(tensor):
            return tensor[:, :, :].rearrange("p a (b n) -> p (a b) n", n=SEQ)

        def head_banks(hd):
            return ps[:, 2 * (hd % 2):2 * (hd % 2) + 2, :]

        def head_stat(pe, hd, i):
            pe.wait_ge(head_sums_ready, 2 * hd + i + 1)
            pe.matmul(ps[:, STAT, 0:SEQ], ones[:, :], acc[:, 0, 0:SEQ], start=True, stop=True
                      ).then_inc(head_stat_ready, 1)

        def pe_retention(pe, t):
            if begun(t["pair"]):
                pe.wait_ge(banks01_read, t["pair"])
            if begun(t["pair"]):
                pe.wait_ge(banks23_read, t["pair"])
            pe.wait_ge(ret_landed, 16)

            def swap(hd, i):
                if hd >= RET_HEADS:
                    return
                if begun(2 * hd + i):
                    pe.wait_ge(swap_taken, 2 * hd + i)
                for half in range(2):
                    ins = pe.matmul(ps[:, 7, half * SEQ:(half + 1) * SEQ], rswap, rope_pair(hd, i)[:, half, :],
                                    start=True, stop=True)
                ins.then_inc(swapped, 1)

            def scores(hd):
                pe.wait_ge(roped, 2 * hd + 2)
                if begun(hd):
                    pe.wait_ge(weighted_ready, hd)
                for kb in range(4):
                    for i in range(2):
                        ins = pe.matmul(ps[:, 5 + kb // 2, (kb % 2) * SEQ:(kb % 2 + 1) * SEQ],
                                        rk[:, 2 * hd + i, kb * P:(kb + 1) * P], rq[:, 2 * hd + i, :],
                                        start=i == 0, stop=i == 1)
                ins.then_inc(scores_ready, 1)

            def head_out(hd):
                pe.wait_ge(weighted_ready, hd + 1)
                if begun(hd - 1):
                    pe.wait_ge(head_out_copied, hd - 1)
                for dv in range(4):
                    for kb in range(4):
                        at = hd * RET_DV + dv * P
                        ins = pe.matmul(head_banks(hd)[:, dv // 2, (dv % 2) * SEQ:(dv % 2 + 1) * SEQ],
                                        rv[:, kb, at:at + P], weighted[:, kb, :], start=kb == 0, stop=kb == 3)
                ins.then_inc(head_out_ready, 1)

            swap(0, 0)
            swap(0, 1)
            scores(0)
            swap(1, 0)
            for hd in range(RET_HEADS):
                if hd > 0:
                    head_stat(pe, hd - 1, 0)
                head_out(hd)
                swap(hd + 1, 1)
                if hd > 0:
                    head_stat(pe, hd - 1, 1)
                if hd + 1 < RET_HEADS:
                    scores(hd + 1)
                swap(hd + 2, 0)
            pe.wait_ge(head_out_copied, RET_HEADS)

        def act_decays(act, hd):
            act.wait_ge(exponents_ready, hd + 1)
            act.activation(decay[:, 0:2, :], decay[:, 0:2, :], ACT.Exp)
            act.activation(decay[:, 2:4, :], rdelta, ACT.Exp, scale=lgam[:, 56 + hd:57 + hd],
                           bias=lgam[:, 40 + hd:41 + hd])
            act.activation(past_decay, rdelta, ACT.Exp, scale=lgam[:, 36 + hd:37 + hd],
                           bias=lgam[:, 44 + hd:45 + hd]).then_inc(decays_ready, 1)

        def act_decay_rates(act):
            act.wait_ge(vec_landed, 16)
            act.wait_ge(decay_abs_ready, 1)
            act.activation(LG["e"], LG["neg_abs"], ACT.Exp).then_inc(decay_exp_ready, 1)
            act.wait_ge(log_gamma_ready, 1)
            act.wait_ge(ret_landed, 16)
            act_decays(act, 0)

        def act_retention(act, t):
            def copy_out(hd):
                act.wait_ge(head_out_ready, hd + 1)
                if begun(hd - 1):
                    act.wait_ge(mix_lo_ready, hd - 1)
                act.activation(ro[hd % 2], head_banks(hd).rearrange("p a (b n) -> p (a b) n", b=2), ACT.Copy
                               ).then_inc(head_out_copied, 1)

            def root(hd):
                act.wait_ge(centred_ready, hd + 1)
                act.activation(rt, ro[hd % 2], ACT.Square).then_inc(head_squares_ready, 1)
                act.wait_ge(head_stat_ready, 2 * hd + 2)
                act.activation(rstd[:, 0:SEQ], ps[:, STAT, 0:SEQ], ACT.Sqrt, scale=1.0 / RET_DV, bias=eps[:, 0:1]
                               ).then_inc(head_root_ready, 1)

            def normed(hd):
                act.wait_ge(gated_ready, hd + 1)
                act.activation(ret_view(u_hi)[:, 4 * hd:4 * hd + 4, :], ro[hd % 2], ACT.Copy
                               ).then_inc(mix_hi_ready, 1)

            act_decays(act, 1)
            copy_out(0)
            for hd in range(1, RET_HEADS):
                if hd + 1 < RET_HEADS:
                    act_decays(act, hd + 1)
                root(hd - 1)
                copy_out(hd)
                normed(hd - 1)
            root(RET_HEADS - 1)
            normed(RET_HEADS - 1)

        def dve_exponents(dve, hd, order):
            if begun(hd):
                dve.wait_ge(weighted_ready, hd)
            dve.tensor_scalar(decay[:, 0:2, :], rdelta, 0.0, lgam[:, 56 + hd:57 + hd], ALU.max, ALU.mult)
            order.link(dve.tensor_scalar(rotated, rdelta, 0.0, lgam[:, 36 + hd:37 + hd], ALU.min, ALU.mult))
            dve.tensor_tensor(decay[:, 0:2, :], decay[:, 0:2, :], rotated, ALU.add
                              ).then_inc(exponents_ready, 1)

        def dve_decay_rates(dve, order):
            x = vecs("decay", 0, 8)
            dve.scalar_tensor_tensor(LG["neg_abs"], x, -1.0, x, ALU.mult, ALU.min
                                     ).then_inc(decay_abs_ready, 1)
            dve.wait_ge(decay_exp_ready, 1)
            log1p(dve, order, LG["e"], LG["den"], LG["s"], LG["s2"], LG["r"], LG["log1p"])
            order.link(dve.scalar_tensor_tensor(LG["lg"], x, 0.0, LG["log1p"], ALU.min, ALU.subtract))
            order.link(dve.tensor_scalar(lgam[:, 32:40], LG["lg"], -1.0, None, ALU.mult))
            dve.tensor_scalar(lgam[:, 40:48], LG["lg"], float(SEQ), None, ALU.mult
                              ).then_inc(log_gamma_ready, 1)
            dve.wait_ge(log_gamma_ready, 1)
            dve.wait_ge(ret_landed, 16)
            dve_exponents(dve, 0, order)

        def dve_retention(dve, t, order):
            def rotate(hd, i):
                dve.wait_ge(swapped, 2 * hd + i + 1)
                if begun(2 * hd + i):
                    dve.wait_ge(roped, 2 * hd + i)
                dve.wait_ge(exponents_ready, hd + 1)
                dve.tensor_tensor(rotated, ps[:, 7, :].rearrange("p (b n) -> p b n", b=2), rsin, ALU.mult
                                  ).then_inc(swap_taken, 1)
                order.link(dve.tensor_tensor(rope_pair(hd, i), rope_pair(hd, i), rcos, ALU.mult))
                dve.tensor_tensor(rope_pair(hd, i), rope_pair(hd, i), rotated, ALU.add).then_inc(roped, 1)

            def weigh(hd):
                dve.wait_ge(decays_ready, hd + 1)
                order.link(dve.tensor_tensor(decay[:, 2:4, :], decay[:, 2:4, :], past_decay, ALU.add))
                dve.wait_ge(scores_ready, hd + 1)
                if begun(hd):
                    dve.wait_ge(head_out_ready, hd)
                dve.scalar_tensor_tensor(weighted[:, :, :], ps[:, 5:7, :].rearrange("p a (b n) -> p (a b) n", b=2),
                                         RET_DK ** -0.5, decay[:, :, :], ALU.mult, ALU.mult
                                         ).then_inc(weighted_ready, 1)

            def sum_features(hd):
                dve.wait_ge(head_out_copied, hd + 1)
                dve.tensor_reduce(acc[:, 0, 0:SEQ], ro[hd % 2].rearrange("p t n -> p n t"), AX, ALU.add
                                  ).then_inc(head_sums_ready, 1)

            def centre_and_gate(hd):
                o = ro[hd % 2]
                dve.wait_ge(head_stat_ready, 2 * hd + 1)
                mean = ps[:, STAT, 0:SEQ].unsqueeze(1).to_broadcast([P, 4, SEQ])
                dve.scalar_tensor_tensor(o, mean, -1.0 / RET_DV, o, ALU.mult, ALU.add
                                         ).then_inc(centred_ready, 1)
                dve.wait_ge(head_squares_ready, hd + 1)
                dve.tensor_reduce(acc[:, 0, 0:SEQ], rt.rearrange("p t n -> p n t"), AX, ALU.add
                                  ).then_inc(head_sums_ready, 1)
                order.link(dve.tensor_tensor(o, o, rg[:, 4 * hd:4 * hd + 4, :], ALU.mult))

            def norm(hd):
                o = ro[hd % 2]
                dve.wait_ge(head_root_ready, hd + 1)
                order.link(dve.reciprocal(rstd[:, 0:SEQ], rstd[:, 0:SEQ]))
                dve.tensor_tensor(o, o, rstd[:, 0:SEQ].unsqueeze(1).to_broadcast([P, 4, SEQ]), ALU.mult
                                  ).then_inc(gated_ready, 1)
                dve.wait_ge(mix_hi_ready, hd + 1)
                four = slice(4 * hd, 4 * hd + 4)
                dve.tensor_tensor(ret_view(u_lo)[:, four, :], o, ret_view(u_hi)[:, four, :].bitcast(f32),
                                  ALU.subtract).then_inc(mix_lo_ready, 1)

            rotate(0, 0)
            rotate(0, 1)
            weigh(0)
            dve_exponents(dve, 1, order)
            rotate(1, 0)
            rotate(1, 1)
            for hd in range(1, RET_HEADS):
                sum_features(hd - 1)
                weigh(hd)
                if hd + 1 < RET_HEADS:
                    dve_exponents(dve, hd + 1, order)
                    rotate(hd + 1, 0)
                centre_and_gate(hd - 1)
                if hd + 1 < RET_HEADS:
                    rotate(hd + 1, 1)
                norm(hd - 1)
            sum_features(RET_HEADS - 1)
            centre_and_gate(RET_HEADS - 1)
            norm(RET_HEADS - 1)

        HD2 = SSD_INNER // SSD_HEADS

        y_squares = tmp1[:, :, :].rearrange("p a (b n) -> p (a b) n", n=SEQ)

        def head_y(hd):
            return ps[(hd % 2) * HD2:(hd % 2 + 1) * HD2, (hd // 2) % 2, (hd // 4) * SEQ:(hd // 4 + 1) * SEQ]

        def pe_steps(pe, l):
            pe.wait_ge(dtw_lo_ready, l + 1)
            for tb in range(2):
                for k in range(DT):
                    tok = slice(tb * P, (tb + 1) * P)
                    for n, (a, w) in enumerate(((u_hi, dtw_hi), (u_hi, dtw_lo), (u_lo, dtw_hi))):
                        ins = pe.matmul(ps[:, 5, tb * 8:tb * 8 + 8], a[:, k, tok], w[:, k * 8:k * 8 + 8],
                                        start=k == 0 and n == 0, stop=k == DT - 1 and n == 2)
            ins.then_inc(dt_ready, 1)

        def pe_mixer(pe, t, l):
            if begun(t["pair"]):
                pe.wait_ge(banks01_read, t["pair"])
            if begun(t["pair"]):
                pe.wait_ge(banks23_read, t["pair"])
            pe.wait_ge(tables_landed, 16)
            for i in range(4):
                ins = pe.matmul(ps[:, 6 + i // 2, (i % 2) * SEQ:(i % 2 + 1) * SEQ], tab["swap"], qk[:, i, :],
                                start=True, stop=True)
            ins.then_inc(qk_swapped, 1)
            for g in range(POOL_GROUPS):
                out = ps[(g % 2) * 64:(g % 2 + 1) * 64, 0, (g // 2) * SEQ:(g // 2 + 1) * SEQ]
                for tb in range(2):
                    ins = pe.matmul(out, pool_u[:, tb, g * 64:(g + 1) * 64], band[:, tb, g, :], start=tb == 0,
                                    stop=tb == 1)
            ins.then_inc(pool_mean_ready, 1)
            pe.wait_ge(conv_ready, l + 1)
            for g in range(SSD_GROUPS):
                for sbk in range(2):
                    ins = pe.matmul(ps[:, 2 + g, sbk * SEQ:(sbk + 1) * SEQ], cx[:, 4 + g, sbk * P:(sbk + 1) * P],
                                    cx[:, 6 + g, :], start=True, stop=True)
            ins.then_inc(cb_ready, 1)
            pe.wait_ge(pool_mean_copied, l + 1)
            pe.wait_ge(poolw_landed, 64 * (l + 1))
            for j in range(2):
                ins = pe.matmul(ps[:, 1, j * SEQ:(j + 1) * SEQ], poolw[:, j, :], mixf[:, 6 + j, :], start=True,
                                stop=True)
            ins.then_inc(pool_out_ready, 1)
            pe.wait_ge(dt_taken, l + 1)
            for tb in range(2):
                for j in range(4):
                    ins = pe.matmul(ps[:, 4 + tb, j * P:(j + 1) * P], cx[:, j, tb * P:(tb + 1) * P], tab["ident"],
                                    start=True, stop=True)
            ins.then_inc(xtok_ready, 1)
            pe.wait_ge(da_ready, l + 1)
            pe.wait_ge(qk_roped, l + 1)
            for tb in range(2):
                for sbk in range(tb + 1):
                    ins = pe.matmul(ps[:, 6, tb * 8:tb * 8 + 8], tri[:, sbk, tb * P:(tb + 1) * P],
                                    sm("da")[:, sbk, :], start=sbk == 0, stop=sbk == tb)
            ins.then_inc(acs_ready, 1)

            def sums(x):
                for hd in (2 * x, 2 * x + 1):
                    if hd == 0:
                        pe.wait_ge(acs_taken, l + 1)
                    if hd >= 2:
                        pe.wait_ge(segment_taken, l * SSD_HEADS + hd - 1)
                    for sbk in range(2):
                        ins = pe.matmul(ps[:, 6 + hd % 2, 0:SEQ], sm("da")[:, sbk, hd:hd + 1].to_broadcast([P, P]),
                                        tri[:, sbk, :], start=sbk == 0, stop=sbk == 1)
                    ins.then_inc(head_acs_ready, 1)

            def scan_out(x):
                if x == 0:
                    pe.wait_ge(xtok_copied, l + 1)
                    pe.wait_ge(pool_out_taken, l + 1)
                if x >= 2:
                    pe.wait_ge(y_gated, l * 4 + x - 1)
                for hd in (2 * x, 2 * x + 1):
                    pe.wait_ge(segment_ready, l * SSD_HEADS + hd + 1)
                    for sbk in range(2):
                        ins = pe.matmul(head_y(hd), xtok[:, sbk, hd * HD2:(hd + 1) * HD2], seg[:, hd % 4, sbk, :],
                                        start=sbk == 0, stop=sbk == 1)
                    ins.then_inc(head_y_ready, 1)

            def att_scores(a):
                r = slice((a % 2) * ATTN_DH, (a % 2 + 1) * ATTN_DH)
                if a == 0:
                    pe.wait_ge(cb_taken, l + 1)
                if a >= 2:
                    pe.wait_ge(att_masked, l * ATTN_HEADS + a - 1)
                for nb in range(2):
                    ins = pe.matmul(ps[:, 2 + a % 2, nb * SEQ:(nb + 1) * SEQ], qk[r, a // 2, nb * P:(nb + 1) * P],
                                    qk[r, 2 + a // 2, :], start=True, stop=True)
                ins.then_inc(att_scores_ready, 1)

            def turn_probs(a):
                pe.wait_ge(probs_ready, l * ATTN_HEADS + a + 1)
                if a == 0:
                    pe.wait_ge(xtok_copied, l + 1)
                else:
                    pe.wait_ge(probs_t_copied, l * ATTN_HEADS + a)
                for nb in range(2):
                    for mb in range(2):
                        at = mb * SEQ + nb * P
                        ins = pe.matmul(ps[:, 4, at:at + P], probs[:, a % 2, nb, mb * P:(mb + 1) * P], tab["ident"],
                                        start=True, stop=True)
                ins.then_inc(probs_turned, 1)

            def att_out(a):
                pe.wait_ge(probs_t_copied, l * ATTN_HEADS + a + 1)
                for mb in range(2):
                    out = ps[(a % 2) * 64:(a % 2 + 1) * 64, 5, (a // 2) * SEQ:(a // 2 + 1) * SEQ]
                    ins = pe.matmul(out, att_v[:, mb, a * 64:(a + 1) * 64], probs_t[:, a % 2, mb, :], start=mb == 0,
                                    stop=mb == 1)
                ins.then_inc(att_out_ready, 1)

            sums(0)
            att_scores(0)
            for x in range(4):
                if x + 1 < 4:
                    sums(x + 1)
                    att_scores(x + 1)
                if x > 0:
                    att_out(x - 1)
                scan_out(x)
                turn_probs(x)
            att_out(3)
            pe.wait_ge(segment_taken, (l + 1) * SSD_HEADS)
            for j in range(4):
                pe.wait_ge(ssd_squares_ready, l * 4 + j + 1)
                ins = pe.matmul(ps[:, 6, 0:SEQ], ones[:, :], y_squares[:, j, :], start=j == 0, stop=j == 3)
            ins.then_inc(ssd_stat_ready, 1)

        def act_conv(act, l):
            act.wait_ge(dtw_landed, 16 * (l + 1))
            act.activation(dtw_hi[:, :], dtw[:, :], ACT.Copy).then_inc(dtw_hi_ready, 1)
            for j in range(8):
                act.wait_ge(conv_sum_ready, 8 * l + j + 1)
                ins = act.activation(cx[:, j, :], cx[:, j, :], ACT.Silu, bias=lv("conv_b", j))
            ins.then_inc(conv_ready, 1)

        def act_steps(act, l):
            act.wait_ge(dt_taken, l + 1)
            act.activation(sm("e_dt"), sm("neg_abs"), ACT.Exp)
            act.activation(sm("neg_a")[:, 0, :], lv("a_log", 0, 8), ACT.Exp).then_inc(dt_exp_ready, 1)

        def act_mixer(act, l):
            act.wait_ge(pool_mean_ready, l + 1)
            act.activation(mixf[:, 6:8, :], ps[:, 0, :].rearrange("p (b n) -> p b n", b=2), ACT.Copy
                           ).then_inc(pool_mean_copied, 1)
            act.wait_ge(xtok_ready, l + 1)
            act.activation(xtok[:, :, :], ps[:, 4:6, :], ACT.Copy).then_inc(xtok_copied, 1)
            act.wait_ge(pool_out_taken, l + 1)
            act.activation(u_hi[:, 4:6, 0:SEQ], mixf[:, 4:6, :], ACT.Copy).then_inc(mix_hi_ready, 1)

            def exps(x):
                for hd in (2 * x, 2 * x + 1):
                    act.wait_ge(segment_taken, l * SSD_HEADS + hd + 1)
                    act.activation(seg[:, hd % 4, :, :], seg[:, hd % 4, :, :], ACT.Exp
                                   ).then_inc(segment_exp_ready, 1)
                act.wait_ge(max_ready, l * ATTN_HEADS + x + 1)
                for nb in range(2):
                    ins = act.activation(probs[:, x % 2, nb, :], probs[:, x % 2, nb, :], ACT.Exp,
                                         bias=sm("neg_mx")[:, x % 2, nb:nb + 1],
                                         accum_out=sm("sums")[:, x % 2, nb:nb + 1])
                ins.then_inc(probs_exp_ready, 1)

            def squares(x):
                act.wait_ge(y_gated, l * 4 + x + 1)
                act.activation(y_squares[:, x, :], mixf[:, x, :], ACT.Square).then_inc(ssd_squares_ready, 1)

            exps(0)
            for x in range(4):
                if x + 1 < 4:
                    exps(x + 1)
                if x > 0:
                    squares(x - 1)
                act.wait_ge(probs_turned, l * ATTN_HEADS + x + 1)
                if x >= 2:
                    act.wait_ge(att_out_ready, l * ATTN_HEADS + x - 1)
                act.activation(probs_t[:, x % 2, :, :], ps[:, 4, :].rearrange("p (b n) -> p b n", b=2), ACT.Copy
                               ).then_inc(probs_t_copied, 1)
            squares(3)
            act.wait_ge(att_out_ready, (l + 1) * ATTN_HEADS)
            act.activation(mixf[:, 6:8, :], ps[:, 5, :].rearrange("p (b n) -> p b n", b=2), ACT.Copy
                           ).then_inc(att_copied, 1)
            act.activation(u_hi[:, 6:8, 0:SEQ], ps[:, 5, :].rearrange("p (b n) -> p b n", b=2), ACT.Copy
                           ).then_inc(mix_hi_ready, 1)
            act.wait_ge(ssd_stat_ready, l + 1)
            act.activation(rstd[:, 0:SEQ], ps[:, 6, 0:SEQ], ACT.Sqrt, scale=1.0 / SSD_INNER, bias=eps[:, 0:1]
                           ).then_inc(ssd_root_ready, 1)
            act.wait_ge(y_normed, l + 1)
            act.activation(u_hi[:, 0:4, 0:SEQ], mixf[:, 0:4, :], ACT.Copy).then_inc(mix_hi_ready, 1)

        def dve_conv(dve, t, l, order):
            dve.wait_ge(dtw_hi_ready, l + 1)
            dve.tensor_tensor(dtw_lo[:, :], dtw[:, :], dtw_hi[:, :].bitcast(f32), ALU.subtract
                              ).then_inc(dtw_lo_ready, 1)
            if begun(t["pair"]):
                dve.wait_ge(banks01_read, t["pair"])
            if begun(t["pair"]):
                dve.wait_ge(banks23_read, t["pair"])
            order.link(dve.memset(xpad[:, :, 0:3], 0.0))
            for i in range(4):
                for j in range(8):
                    w = lv("conv_w", 4 * j + i)
                    if i == 0:
                        ins = dve.tensor_scalar(cx[:, j, :], xpad[:, j, 0:SEQ], w, None, ALU.mult)
                    else:
                        ins = dve.scalar_tensor_tensor(cx[:, j, :], xpad[:, j, i:i + SEQ], w, cx[:, j, :], ALU.mult,
                                                       ALU.add)
                    if i == 3:
                        ins.then_inc(conv_sum_ready, 1)
                    elif j == 7:
                        order.link(ins)

        def dve_steps(dve, l, order):
            dve.wait_ge(dt_ready, l + 1)
            heads = lambda name: lv(name, 0, 8).unsqueeze(1).to_broadcast([P, 2, 8])
            order.link(dve.tensor_tensor(sm("dt_in"), ps[:, 5, 0:16].rearrange("p (b n) -> p b n", b=2),
                                         heads("dt_bias"), ALU.add))
            dve.scalar_tensor_tensor(sm("neg_abs"), sm("dt_in"), -1.0, sm("dt_in"), ALU.mult, ALU.min
                                     ).then_inc(dt_taken, 1)
            dve.wait_ge(dt_exp_ready, l + 1)
            log1p(dve, order, sm("e_dt"), sm("s_den"), sm("s_dt"), sm("s2"), sm("series"), sm("log1p"))
            order.link(dve.scalar_tensor_tensor(sm("dt"), sm("dt_in"), 0.0, sm("log1p"), ALU.max, ALU.add))
            dve.scalar_tensor_tensor(sm("da"), sm("dt"), -1.0, sm("neg_a")[:, 0:1, :].to_broadcast([P, 2, 8]),
                                     ALU.mult, ALU.mult).then_inc(da_ready, 1)

        def dve_mixer(dve, l, order):
            dve.wait_ge(tables_landed, 16)
            dve.wait_ge(qk_swapped, l + 1)
            both = lambda name: tab[name].unsqueeze(1).to_broadcast([P, 2, SEQ])
            for i in range(2):
                part = tmp2[:, i, :].rearrange("p (b n) -> p b n", b=2)
                dve.tensor_tensor(part, ps[:, 6 + i, :].rearrange("p (b n) -> p b n", b=2), both("sin"), ALU.mult)
                order.link(dve.tensor_tensor(qk[:, 2 * i:2 * i + 2, :], qk[:, 2 * i:2 * i + 2, :], both("cos"),
                                             ALU.mult))
                ins = dve.tensor_tensor(qk[:, 2 * i:2 * i + 2, :], qk[:, 2 * i:2 * i + 2, :], part, ALU.add)
            ins.then_inc(qk_roped, 1)
            dve.wait_ge(cb_ready, l + 1)
            for g in range(SSD_GROUPS):
                ins = dve.tensor_tensor(cb[:, 2 * g:2 * g + 2, :], ps[:, 2 + g, :].rearrange("p (b n) -> p b n", b=2),
                                        tri, ALU.mult)
            ins.then_inc(cb_taken, 1)
            dve.wait_ge(pool_out_ready, l + 1)
            for j in range(2):
                ins = dve.tensor_scalar(mixf[:, 4 + j, :], ps[:, 1, j * SEQ:(j + 1) * SEQ], lv("pool_scale", j), None,
                                        ALU.mult)
            ins.then_inc(pool_out_taken, 1)

            def split(a, b, n):
                dve.wait_ge(mix_hi_ready, RET_HEADS + 3 * l + n)
                dve.tensor_tensor(u_lo[:, a:b, 0:SEQ], mixf[:, a:b, :], u_hi[:, a:b, 0:SEQ].bitcast(f32),
                                  ALU.subtract).then_inc(mix_lo_ready, 1)
            split(4, 6, 1)
            dve.wait_ge(acs_ready, l + 1)
            dve.tensor_copy(sm("acs"), ps[:, 6, 0:16].rearrange("p (b n) -> p b n", b=2)
                            ).then_inc(acs_taken, 1)
            dve.wait_ge(acs_taken, l + 1)

            def take(x):
                for hd in (2 * x, 2 * x + 1):
                    dve.wait_ge(head_acs_ready, l * SSD_HEADS + hd + 1)
                    if hd >= 4:
                        dve.wait_ge(head_y_ready, l * SSD_HEADS + hd - 3)
                    for sbk in range(2):
                        ins = dve.tensor_scalar(seg[:, hd % 4, sbk, :], ps[:, 6 + hd % 2, 0:SEQ],
                                                sm("acs")[:, sbk, hd:hd + 1], 0.0, ALU.subtract, ALU.min)
                    ins.then_inc(segment_taken, 1)
                dve.wait_ge(att_scores_ready, l * ATTN_HEADS + x + 1)
                if x >= 2:
                    dve.wait_ge(probs_turned, l * ATTN_HEADS + x - 1)
                dve.scalar_tensor_tensor(probs[:, x % 2, :, :], ps[:, 2 + x % 2, :].rearrange("p (b n) -> p b n", b=2),
                                         ATTN_DH ** -0.5, mask, ALU.mult, ALU.add
                                         ).then_inc(att_masked, 1)
                dve.wait_ge(att_masked, l * ATTN_HEADS + x + 1)
                dve.tensor_reduce(sm("neg_mx")[:, x % 2, 0:2], probs[:, x % 2, :, :], AX, ALU.max, negate=True
                                  ).then_inc(max_ready, 1)

            def weigh(x):
                for hd in (2 * x, 2 * x + 1):
                    dve.wait_ge(segment_exp_ready, l * SSD_HEADS + hd + 1)
                    for sbk in range(2):
                        ins = dve.scalar_tensor_tensor(seg[:, hd % 4, sbk, :], seg[:, hd % 4, sbk, :],
                                                       sm("dt")[:, sbk, hd:hd + 1], cb[:, 2 * (hd // 4) + sbk, :],
                                                       ALU.mult, ALU.mult)
                    ins.then_inc(segment_ready, 1)
                dve.wait_ge(probs_exp_ready, l * ATTN_HEADS + x + 1)
                order.link(dve.reciprocal(sm("inv")[:, x % 2, 0:2], sm("sums")[:, x % 2, 0:2]))
                for nb in range(2):
                    ins = dve.tensor_scalar(probs[:, x % 2, nb, :], probs[:, x % 2, nb, :],
                                            sm("inv")[:, x % 2, nb:nb + 1], None, ALU.mult)
                ins.then_inc(probs_ready, 1)

            def gate(x):
                dve.wait_ge(head_y_ready, l * SSD_HEADS + 2 * x + 2)
                order.link(dve.scalar_tensor_tensor(mixf[:, x, :], cx[:, x, :], lv("d_skip", x),
                                                    ps[:, x % 2, (x // 2) * SEQ:(x // 2 + 1) * SEQ],
                                                    ALU.mult, ALU.add))
                dve.tensor_tensor(mixf[:, x, :], mixf[:, x, :], zs[:, x, :], ALU.mult).then_inc(y_gated, 1)

            take(0)
            for x in range(4):
                if x + 1 < 4:
                    take(x + 1)
                weigh(x)
                if x > 0:
                    gate(x - 1)
            gate(3)
            dve.wait_ge(att_copied, l + 1)
            split(6, 8, 2)
            dve.wait_ge(ssd_root_ready, l + 1)
            order.link(dve.reciprocal(rstd[:, 0:SEQ], rstd[:, 0:SEQ]))
            for j in range(4):
                ins = dve.scalar_tensor_tensor(mixf[:, j, :], mixf[:, j, :], lv("ssd_norm", j), rstd[:, 0:SEQ],
                                               ALU.mult, ALU.mult)
            ins.then_inc(y_normed, 1)
            split(0, 4, 3)

        first, ORDER_DVE = block1(), 33
        block = ctx.enter_context(nc.Block())

        @block.sync
        def _(sp):
            t = Tally()
            sp.dma_start(h[:, :, :], rows(T["xT"])).then_inc(x_landed, 16)
            for g in first:
                if isinstance(g, Gemm):
                    sp_gemm(sp, g, t)
                t.add(g)
            with sp.Fori(0, LAYERS2) as l:
                stages = block2(l)
                t.enter(l, stages)
                for g in stages:
                    if isinstance(g, Gemm):
                        sp_gemm(sp, g, t)
                    t.add(g)
            t.leave(LAYERS2)
            if begun(t["post"]):
                sp.wait_ge(post_ready, t["post"])
            sp.dma_start(rows(T["outT"]), h[:, :, 0:SEQ]).then_inc(out_landed, 16)
            sp.wait_ge(out_landed, 16)

        @block.gpsimd
        def _(pool):
            pool.memset(ones[:, :], 1.0)
            pool.memset(eps[:, 0:1], EPS)
            pool.memset(eps[:, 1:2], 4.0 * EPS).then_inc(setup_ready, 1)

        @block.scalar
        def _(act):
            act.dma_start(cond[:, :, :], T["cond"]).then_inc(cond_landed, 16)
            act.dma_start(vec[:, :], T["vec"]).then_inc(vec_landed, 16)
            act.dma_start(lvecs[:, :], T["layer_vecs"]).then_inc(lvec_landed, 16)
            act.wait_ge(cond_landed, 16)
            act.wait_ge(setup_ready, 1)
            act.activation(cond[:, :, :], cond[:, :, :], ACT.Silu).then_inc(cond_silu_ready, 1)
            act.wait_ge(cond_silu_ready, 1)
            for i in range(5):
                ins = act.activation(cond_hi[:, i, :, :, 0], cond[:, :, :], ACT.Copy)
            ins.then_inc(cond_ready, 1)
            t = Tally()
            gemm0 = follower(first, -1)
            for u in range(RING):
                split_hi(act, gemm0, {"unit": 0, "unit_div": 0}, 0, u)
            for j, g in enumerate(first):
                if isinstance(g, Gemm):
                    if g.squares:
                        act_load_root(act)
                    stream(act, g, t, follower(first, j), split_hi, act_evacuate)
                elif g.kind == "squares":
                    act.wait_ge(x_landed, 16)
                    for m in range(4):
                        act_square(act, h, NTOK, m, t)
                    act_load_root(act)
                elif g.kind == "stats":
                    act_stats(act, g, t)
                elif g.kind == "apply":
                    if g.more["piece"] == 1:
                        act.wait_ge(stat_ready, t["stat"])
                        act.dma_start(rtab[:, :], T["ret_tables"]).then_inc(ret_landed, 16)
                    act_apply(act, g, t)
                elif g.kind == "fourier":
                    act.wait_ge(stat_ready, t["stat"])
                    act.dma_start(dft[:, :, :], T["dft"]).then_inc(dft_landed, 16)
                    act_fourier(act, g, t)
                elif g.kind == "decay_rates":
                    act_decay_rates(act)
                elif g.kind == "retention":
                    act_retention(act, t)
                elif g.kind == "final":
                    act.dma_start(tables[:, :], T["tables2"]).then_inc(tables_landed, 16)
                t.add(g)
            with act.Fori(0, LAYERS2) as l:
                stages = block2(l)
                t.enter(l, stages)
                for u in range(RING):
                    split_hi(act, follower(stages, -1), t, 0, u)
                act.wait_ge(lvec_landed, 16)
                act.wait_ge(poolw_zeroed, 1)
                act.wait_ge(post_ready, t["post"])
                for g in range(POOL_GROUPS):
                    r = slice((g % 2) * 64, (g % 2 + 1) * 64)
                    act.dma_start(poolw[r, g // 2, r], T["pool_w_2"][l, g]).then_inc(poolw_landed, 16)
                act.dma_start(dtw[:, :].rearrange("p (k n) -> p k n", n=8),
                              rows(T["w_in_2"][l])[:, :, 1536:1544]).then_inc(dtw_landed, 16)
                act.activation(lvec[:, :], lvecs[:, bass.ds(l * LAYER_N, LAYER_N)], ACT.Copy
                               ).then_inc(lvec_copied, 1)
                act.wait_ge(lvec_copied, l + 1)
                for j, g in enumerate(stages):
                    if isinstance(g, Gemm):
                        if g.squares:
                            act_load_root(act)
                        if g.norm_after:
                            act_stats(act, stats(g.tokens, "gemm"), t)
                        stream(act, g, t, follower(stages, j), split_hi, act_evacuate)
                    elif g.kind == "stats":
                        act_stats(act, g, t)
                    elif g.kind == "apply":
                        act_apply(act, g, t)
                    elif g.kind == "gain":
                        act_gain(act, g, t)
                    elif g.kind == "conv":
                        act_conv(act, l)
                    elif g.kind == "steps":
                        act_steps(act, l)
                    elif g.kind == "mixer":
                        act_mixer(act, l)
                    t.add(g)

        @block.vector
        def _(dve):
            order = Order(dve, dve_order)
            t = Tally()
            dve.wait_ge(vec_landed, 16)
            dve.wait_ge(cond_ready, 1)
            for i in range(5):
                ins = dve.tensor_tensor(cond_hi[:, i, :, :, 1], cond[:, :, :], cond_hi[:, i, :, :, 0].bitcast(f32),
                                        ALU.subtract)
            ins.then_inc(cond_lo_ready, 1)
            for u in range(RING):
                split_lo(dve, follower(first, -1), {"unit": 0, "unit_div": 0}, 0, u)
            for j, g in enumerate(first):
                if isinstance(g, Gemm):
                    stream(dve, g, t, follower(first, j), split_lo, dve_evacuate, dve_turn_rows)
                elif g.kind == "squares":
                    for m in (1, 2):
                        dve_add_squares(dve, NTOK, m, t)
                elif g.kind == "stats":
                    dve_stats(dve, g, t)
                elif g.kind == "coef":
                    dve_coef(dve, g, t, order)
                elif g.kind == "apply":
                    dve_apply(dve, g, t)
                elif g.kind == "fourier":
                    dve_fourier(dve, g, t)
                elif g.kind == "decay_rates":
                    dve_decay_rates(dve, order)
                elif g.kind == "retention":
                    dve_retention(dve, t, order)
                elif g.kind == "final":
                    if begun(t["stat"]):
                        dve.wait_ge(rstd_ready, t["stat"])
                    for k in range(DT):
                        if begun(k - 1):
                            dve.wait_ge(post_ready, k - 1)
                        order.link(dve.tensor_tensor(tmp2[:, k % 2, 0:SEQ], h[:, k, 0:SEQ], rstd[:, 0:SEQ], ALU.mult))
                        dve.tensor_scalar(h[:, k, 0:SEQ], tmp2[:, k % 2, 0:SEQ], vecs("final_g", k), None, ALU.mult
                                          ).then_inc(post_ready, 1)
                    dve.memset(poolw[:, :, :], 0.0).then_inc(poolw_zeroed, 1)
                t.add(g)
            with dve.Fori(0, LAYERS2) as l:
                stages = block2(l)
                t.enter(l, stages)
                order.enter(l, ORDER_DVE)
                up = follower(stages, -1)
                split_lo(dve, up, t, 0, 0)
                dve.wait_ge(lvec_copied, l + 1)
                for j, g in enumerate(stages):
                    if isinstance(g, Gemm):
                        if g.norm_after:
                            dve_stats(dve, stats(g.tokens, "gemm"), t)
                        stream(dve, g, t, follower(stages, j), split_lo, dve_evacuate, dve_turn_rows)
                    elif g.kind == "stats":
                        dve_stats(dve, g, t)
                    elif g.kind == "apply":
                        dve_apply(dve, g, t)
                    elif g.kind == "gain":
                        if j == 0:
                            dve_gain(dve, g, t, {3: [1], 7: [2, 3]}, up)
                    elif g.kind == "post":
                        behind = stages[j + 1] if j + 1 < len(stages) and stages[j + 1].kind == "gain" else None
                        dve_post(dve, g, t, behind)
                    elif g.kind == "conv":
                        dve_conv(dve, t, l, order)
                    elif g.kind == "steps":
                        dve_steps(dve, l, order)
                    elif g.kind == "mixer":
                        dve_mixer(dve, l, order)
                    t.add(g)
                order.leave(LAYERS2)

        @block.tensor
        def _(pe):
            t = Tally()
            pe.wait_ge(setup_ready, 1)
            for g in first:
                if g is follower(first, -1):
                    pe.wait_ge(cond_lo_ready, 1)
                if isinstance(g, Gemm):
                    pe_gemm(pe, g, t)
                elif g.kind == "stats":
                    pe_stats(pe, g, t)
                elif g.kind == "fourier":
                    pe_fourier(pe, t)
                elif g.kind == "retention":
                    pe_retention(pe, t)
                t.add(g)
            with pe.Fori(0, LAYERS2) as l:
                stages = block2(l)
                t.enter(l, stages)
                for g in stages:
                    if isinstance(g, Gemm):
                        pe_gemm(pe, g, t)
                    elif g.kind == "stats":
                        pe_stats(pe, g, t)
                    elif g.kind == "steps":
                        pe_steps(pe, l)
                    elif g.kind == "mixer":
                        pe_mixer(pe, t, l)
                    t.add(g)


def kernel(**inputs):
    import numpy as _np
    import concourse.bacc as _bacc
    from concourse import mybir as _mybir
    from concourse.bass_utils import run_bass_kernel_spmd as _run

    a = {k: _np.asarray(v) for k, v in inputs.items()}

    def tiles(v):
        return v.reshape(-1, P).T

    vec = [tiles(a["b_mod"]), tiles(a["norm_g"]), tiles(a["final_norm_g"]),
           _np.broadcast_to(a["ret_decay_logit"].reshape(1, 8), (P, 8))]
    layers = []
    for l in range(LAYERS2):
        conv = a["conv_w_2"][l].reshape(4, 8, P).transpose(2, 1, 0).reshape(P, 32)
        layers.append(_np.concatenate(
            [tiles(a[n][l]) for n in ("ff1_norm_pre_2", "ff1_norm_post_2", "mix_norm_pre_2", "mix_norm_post_2",
                                      "ff2_norm_pre_2", "ff2_norm_post_2")]
            + [conv, tiles(a["conv_b_2"][l]), tiles(a["ssd_norm_2"][l]), tiles(a["pool_scale_2"][l]),
               tiles(_np.repeat(a["d_skip_2"][l], SSD_INNER // SSD_HEADS)),
               _np.broadcast_to(a["dt_bias_2"][l][None], (P, 8)),
               _np.broadcast_to(a["a_log_2"][l][None], (P, 8))], axis=1))
    dft, ret_tables, tables2 = host_tables()
    arrays = {
        "xT": _np.concatenate([a["x"][0].T, a["ctx"][0].T], axis=1),
        "cond": _np.stack([a["c"][0].reshape(DT, P).T, a["c_ctx"].reshape(DT, P).T], axis=2),
        "vec": _np.concatenate(vec, axis=1), "layer_vecs": _np.concatenate(layers, axis=1),
        "dft": dft.reshape(P, 5, SEQ), "ret_tables": ret_tables, "tables2": tables2,
    }
    for name in ("w_mod", "ffn_w_in", "ffn_w_out", "fnet_w_out", "ret_w_in", "ret_w_out", "ff1_w_gate_2",
                 "ff1_w_up_2", "ff1_w_down_2", "ff2_w_gate_2", "ff2_w_up_2", "ff2_w_down_2", "w_in_2", "pool_w_2",
                 "w_out_2"):
        arrays[name] = a[name]
    arrays = {k: _np.ascontiguousarray(v) for k, v in arrays.items()}
    nc = _bacc.Bacc("TRN2", target_bir_lowering=False, num_devices=1)
    f = _mybir.dt.float32
    T = {k: nc.dram_tensor("in_" + k, v.shape, f, kind="ExternalInput").ap() for k, v in arrays.items()}
    T["outT"] = nc.dram_tensor("outT", (D, SEQ), f, kind="ExternalOutput").ap()
    build(nc, T)
    r = _run(nc, [{"in_" + k: v for k, v in arrays.items()}], core_ids=[0])
    return _np.ascontiguousarray(r.results[0]["outT"].T).reshape(1, SEQ, D)
```
